# Optimizing a Trainium2 kernel written in Bass

```python
import jax, jax.numpy as jnp
from jax import lax
import numpy as np

D_MODEL = 1024
BATCH = 1
SEQ = 256
DEPTH = 1

FOX_HEADS = 8
FOX_HEAD_DIM = 64
FOX_WIDTH = FOX_HEADS * FOX_HEAD_DIM
RET_HEADS = 4
RET_HEAD_DIM = 128
RET_WIDTH = RET_HEADS * RET_HEAD_DIM
MIX_WIDTH = FOX_WIDTH + RET_WIDTH
D_FF = 4 * D_MODEL
Q_BLOCK = 128
RET_CHUNK = 128
ROPE_BASE = 10000.0
EPS = 1e-6
N_MOD = 6
IN_COLS = 4 * FOX_WIDTH + FOX_HEADS + 4 * RET_WIDTH


def _rms(x):
    x32 = x.astype(jnp.float32)
    return x32 * lax.rsqrt(jnp.mean(x32 * x32, axis=-1, keepdims=True) + EPS)

def _rope(x):
    s, d = x.shape[1], x.shape[-1]
    pos = jnp.arange(s, dtype=jnp.float32)
    inv_freq = ROPE_BASE ** (-jnp.arange(0, d, 2, dtype=jnp.float32) / d)
    ang = pos[:, None] * inv_freq[None, :]
    cos = jnp.cos(ang)[None, :, None, :]
    sin = jnp.sin(ang)[None, :, None, :]
    x32 = x.astype(jnp.float32)
    x1, x2 = x32[..., : d // 2], x32[..., d // 2:]
    return jnp.concatenate([x1 * cos - x2 * sin, x1 * sin + x2 * cos], axis=-1).astype(x.dtype)

def _forgetting_attention(q, k, v, log_f):
    b, s, h, d = q.shape
    scale = 1.0 / np.sqrt(d)
    cum = jnp.cumsum(log_f, axis=1).transpose(0, 2, 1)
    qh = q.transpose(0, 2, 1, 3)
    kh = k.transpose(0, 2, 1, 3)
    vh = v.transpose(0, 2, 1, 3)
    outs = []
    for blk in range(s // Q_BLOCK):
        s0, s1 = blk * Q_BLOCK, (blk + 1) * Q_BLOCK
        logits = jnp.einsum('bhqd,bhkd->bhqk', qh[:, :, s0:s1], kh[:, :, :s1]).astype(jnp.float32) * scale
        logits = logits + cum[:, :, s0:s1, None] - cum[:, :, None, :s1]
        q_pos = jnp.arange(s0, s1)[:, None]
        k_pos = jnp.arange(s1)[None, :]
        logits = jnp.where(q_pos >= k_pos, logits, -jnp.inf)
        p = jax.nn.softmax(logits, axis=-1).astype(v.dtype)
        outs.append(jnp.einsum('bhqk,bhkd->bhqd', p, vh[:, :, :s1]))
    out = jnp.concatenate(outs, axis=2)
    return out.transpose(0, 2, 1, 3)

def _retention(q, k, v):
    b, s, h, dk = q.shape
    dv = v.shape[-1]
    n_chunks = s // RET_CHUNK
    log_g = jnp.log(1.0 - 2.0 ** (-5.0 - jnp.arange(h, dtype=jnp.float32)))
    n = jnp.arange(RET_CHUNK, dtype=jnp.float32)
    diff = n[:, None] - n[None, :]
    decay_mask = jnp.where(diff[None] >= 0,
                           jnp.exp(jnp.maximum(diff, 0.0)[None] * log_g[:, None, None]), 0.0)
    xi = jnp.exp((n[None, :] + 1.0) * log_g[:, None])
    zeta = jnp.exp((RET_CHUNK - 1.0 - n[None, :]) * log_g[:, None])
    g_chunk = jnp.exp(RET_CHUNK * log_g)

    def to_chunks(t):
        return t.astype(jnp.float32).reshape(b, n_chunks, RET_CHUNK, h, t.shape[-1]).transpose(1, 0, 3, 2, 4)

    qc, kc, vc = to_chunks(q), to_chunks(k * (dk ** -0.5)), to_chunks(v)

    def step(state, inp):
        qi, ki, vi = inp
        inner = jnp.einsum('bhnd,bhmd->bhnm', qi, ki) * decay_mask[None]
        inner_out = jnp.einsum('bhnm,bhmv->bhnv', inner, vi)
        cross_out = jnp.einsum('bhnd,bhdv->bhnv', qi, state) * xi[None, :, :, None]
        new_state = state * g_chunk[None, :, None, None] + \
            jnp.einsum('bhmd,bhmv->bhdv', ki * zeta[None, :, :, None], vi)
        return new_state, inner_out + cross_out

    state0 = jnp.zeros((b, h, dk, dv), jnp.float32)
    _, out = lax.scan(step, state0, (qc, kc, vc))
    return out.transpose(1, 0, 3, 2, 4).reshape(b, s, h, dv)

def first_inputs(seed: int = 0) -> dict:
    key = jax.random.key(seed)
    ks = jax.random.split(key, 16)
    nrm = jax.random.normal
    f32 = jnp.float32
    return {
        "x": nrm(ks[0], (BATCH, SEQ, D_MODEL), f32),
        "c": nrm(ks[1], (BATCH, D_MODEL), f32),
        "w_ada": nrm(ks[2], (DEPTH, D_MODEL, N_MOD * D_MODEL), f32) * (0.5 * D_MODEL ** -0.5),
        "b_ada": nrm(ks[3], (DEPTH, N_MOD * D_MODEL), f32) * 0.02,
        "w_in": nrm(ks[4], (DEPTH, D_MODEL, IN_COLS), f32) * D_MODEL ** -0.5,
        "b_forget": 2.0 + 0.5 * nrm(ks[5], (DEPTH, FOX_HEADS), f32),
        "q_norm_gain": 1.0 + 0.05 * nrm(ks[6], (DEPTH, FOX_HEAD_DIM), f32),
        "k_norm_gain": 1.0 + 0.05 * nrm(ks[7], (DEPTH, FOX_HEAD_DIM), f32),
        "fox_out_gain": 1.0 + 0.05 * nrm(ks[8], (DEPTH, FOX_HEADS, FOX_HEAD_DIM), f32),
        "ret_out_gain": 1.0 + 0.05 * nrm(ks[9], (DEPTH, RET_HEADS, RET_HEAD_DIM), f32),
        "w_out": nrm(ks[10], (DEPTH, MIX_WIDTH, D_MODEL), f32) * MIX_WIDTH ** -0.5,
        "w_mlp_in": nrm(ks[11], (DEPTH, D_MODEL, D_FF), f32) * D_MODEL ** -0.5,
        "w_mlp_out": nrm(ks[12], (DEPTH, D_FF, D_MODEL), f32) * D_FF ** -0.5,
    }

def first_block(x, c, w_ada, b_ada, w_in, b_forget, q_norm_gain, k_norm_gain,
              fox_out_gain, ret_out_gain, w_out, w_mlp_in, w_mlp_out):
    b, s, _ = x.shape
    dt = x.dtype
    c_act = jax.nn.silu(c)
    o_fq, o_fk, o_fv, o_fog = 0, FOX_WIDTH, 2 * FOX_WIDTH, 3 * FOX_WIDTH
    o_ff = 4 * FOX_WIDTH
    o_rq = o_ff + FOX_HEADS
    o_rk, o_rv, o_rg = o_rq + RET_WIDTH, o_rq + 2 * RET_WIDTH, o_rq + 3 * RET_WIDTH
    for l in range(DEPTH):
        mod = jnp.einsum('bd,de->be', c_act, w_ada[l]) + b_ada[l]
        shift_m, scale_m, gate_m, shift_f, scale_f, gate_f = [m[:, None, :] for m in jnp.split(mod, N_MOD, axis=-1)]

        h = (_rms(x) * (1.0 + scale_m) + shift_m).astype(dt)
        proj = jnp.einsum('bsd,de->bse', h, w_in[l])

        fq = proj[..., o_fq:o_fk].reshape(b, s, FOX_HEADS, FOX_HEAD_DIM)
        fk = proj[..., o_fk:o_fv].reshape(b, s, FOX_HEADS, FOX_HEAD_DIM)
        fv = proj[..., o_fv:o_fog].reshape(b, s, FOX_HEADS, FOX_HEAD_DIM)
        f_og = proj[..., o_fog:o_ff]
        f_logit = proj[..., o_ff:o_rq]
        fq = (_rms(fq) * q_norm_gain[l]).astype(dt)
        fk = (_rms(fk) * k_norm_gain[l]).astype(dt)
        log_f = jax.nn.log_sigmoid(f_logit.astype(jnp.float32) + b_forget[l])
        fox = _forgetting_attention(fq, fk, fv, log_f)
        fox = (_rms(fox) * fox_out_gain[l]).reshape(b, s, FOX_WIDTH) * jax.nn.sigmoid(f_og.astype(jnp.float32))

        rq = _rope(proj[..., o_rq:o_rk].reshape(b, s, RET_HEADS, RET_HEAD_DIM))
        rk = _rope(proj[..., o_rk:o_rv].reshape(b, s, RET_HEADS, RET_HEAD_DIM))
        rv = proj[..., o_rv:o_rg].reshape(b, s, RET_HEADS, RET_HEAD_DIM)
        r_gate = proj[..., o_rg:]
        ret = _retention(rq, rk, rv)
        ret = (_rms(ret) * ret_out_gain[l]).reshape(b, s, RET_WIDTH) * jax.nn.silu(r_gate.astype(jnp.float32))

        mixed = jnp.concatenate([fox, ret], axis=-1).astype(dt)
        x = x + gate_m * jnp.einsum('bse,ed->bsd', mixed, w_out[l])

        h = (_rms(x) * (1.0 + scale_f) + shift_f).astype(dt)
        u = jnp.square(jax.nn.relu(jnp.einsum('bsd,df->bsf', h, w_mlp_in[l])))
        x = x + gate_f * jnp.einsum('bsf,fd->bsd', u, w_mlp_out[l])
    return x


DEPTH_2 = 2

NSA_HEADS = 8
NSA_KV_GROUPS = 2
NSA_HPG = NSA_HEADS // NSA_KV_GROUPS
NSA_HEAD_DIM = 64
NSA_WIDTH = NSA_HEADS * NSA_HEAD_DIM
NSA_KV_WIDTH = NSA_KV_GROUPS * NSA_HEAD_DIM
NSA_N_KV = 6
CMP_BLOCK = 32
CMP_STRIDE = 16
SEL_BLOCK = 64
SEL_TOP_N = 16
WINDOW = 512
NSA_QBLOCK = 64
POOL_WINDOWS = (2, 4, 8, 16)
POOL_GROUPS = len(POOL_WINDOWS)
POOL_WIDTH = D_MODEL - NSA_WIDTH
POOL_GROUP_DIM = POOL_WIDTH // POOL_GROUPS
A_IN = NSA_WIDTH + NSA_N_KV * NSA_KV_WIDTH + 3 * NSA_HEADS + POOL_WIDTH
GLA_HEADS = 4
GLA_KEY_WIDTH = D_MODEL // 2
GLA_VAL_WIDTH = D_MODEL
GLA_DK = GLA_KEY_WIDTH // GLA_HEADS
GLA_DV = GLA_VAL_WIDTH // GLA_HEADS
GLA_GATE_RANK = 16
GLA_TAU = 16.0
GLA_CHUNK = 64
C_IN = 2 * GLA_KEY_WIDTH + 2 * GLA_VAL_WIDTH + GLA_GATE_RANK
D_FF_2 = 4 * D_MODEL
N_EVEN = (DEPTH_2 + 1) // 2
N_ODD = DEPTH_2 // 2
ALPHA = (2 * DEPTH_2) ** 0.25
BETA = (8 * DEPTH_2) ** -0.25
LN_EPS = 1e-5
MASK_VALUE = -1e30
FORCE_SCORE = 1e4


def layer_norm(x, g, b):
    xf = x.astype(jnp.float32)
    mu = jnp.mean(xf, axis=-1, keepdims=True)
    var = jnp.mean(jnp.square(xf - mu), axis=-1, keepdims=True)
    return ((xf - mu) * lax.rsqrt(var + LN_EPS) * g + b).astype(x.dtype)

def masked_softmax(s, mask):
    s = jnp.where(mask, s.astype(jnp.float32), MASK_VALUE)
    m = jnp.max(s, axis=-1, keepdims=True)
    e = jnp.where(mask, jnp.exp(s - m), 0.0)
    return e / jnp.maximum(jnp.sum(e, axis=-1, keepdims=True), 1e-30)

def compress_blocks(k, pos, w1, b1, w2):
    S = k.shape[2]
    n_cmp = (S - CMP_BLOCK) // CMP_STRIDE + 1
    idx = np.arange(n_cmp)[:, None] * CMP_STRIDE + np.arange(CMP_BLOCK)[None, :]
    blocks = k[:, :, idx, :] + pos
    flat = blocks.reshape(blocks.shape[:3] + (CMP_BLOCK * NSA_HEAD_DIM,))
    return jax.nn.gelu(flat @ w1 + b1) @ w2

def selection_map(n_cmp, n_sel):
    sub = np.arange(n_cmp)[:, None] + np.arange(CMP_BLOCK // CMP_STRIDE)[None, :]
    owner = sub // (SEL_BLOCK // CMP_STRIDE)
    return (owner[:, :, None] == np.arange(n_sel)[None, None, :]).sum(1).astype(np.float32)

def pool_mixer(u, pool_w, pool_scale):
    B, S, _ = u.shape
    uf = u.astype(jnp.float32).reshape(B, S, POOL_GROUPS, POOL_GROUP_DIM)
    cs = jnp.pad(jnp.cumsum(uf, axis=1), ((0, 0), (1, 0), (0, 0), (0, 0)))
    count_base = jnp.arange(1, S + 1, dtype=jnp.float32)
    outs = []
    for g, w in enumerate(POOL_WINDOWS):
        c = cs[:, :, g]
        lower = jnp.pad(c[:, :S + 1 - w], ((0, 0), (w - 1, 0), (0, 0)))
        mean = (c[:, 1:] - lower) / jnp.minimum(count_base, float(w))[None, :, None]
        outs.append(mean - uf[:, :, g])
    r = jnp.stack(outs, axis=2)
    y = jnp.einsum('bsgc,gcd->bsgd', r, pool_w.astype(jnp.float32))
    return (y.reshape(B, S, POOL_WIDTH) * pool_scale).astype(u.dtype)

def nsa_pool_mixer(x, w_in, cmp_pos, cmp_w1, cmp_b1, cmp_w2, pool_w, pool_scale, w_out):
    B, S, _ = x.shape
    G, HPG, DH = NSA_KV_GROUPS, NSA_HPG, NSA_HEAD_DIM
    h = x @ w_in
    o1 = NSA_WIDTH
    o2 = o1 + NSA_N_KV * NSA_KV_WIDTH
    o3 = o2 + 3 * NSA_HEADS
    q = h[..., :o1].reshape(B, S, G, HPG, DH).transpose(0, 2, 3, 1, 4)
    kv = h[..., o1:o2].reshape(B, S, NSA_N_KV, G, DH).transpose(2, 0, 3, 1, 4)
    gates = jax.nn.sigmoid(h[..., o2:o3].astype(jnp.float32))
    gates = gates.reshape(B, S, G, HPG, 3).transpose(0, 2, 3, 1, 4)
    u = h[..., o3:]
    k_cmp, v_cmp, k_slc, v_slc, k_win, v_win = kv[0], kv[1], kv[2], kv[3], kv[4], kv[5]

    kc = compress_blocks(k_cmp, cmp_pos[0], cmp_w1[0], cmp_b1[0], cmp_w2[0])
    vc = compress_blocks(v_cmp, cmp_pos[1], cmp_w1[1], cmp_b1[1], cmp_w2[1])
    n_cmp = kc.shape[2]
    n_sel = S // SEL_BLOCK
    top_n = min(SEL_TOP_N, n_sel)
    sel_map = jnp.asarray(selection_map(n_cmp, n_sel))
    cmp_end = jnp.arange(n_cmp) * CMP_STRIDE + CMP_BLOCK - 1
    ks_b = k_slc.reshape(B, G, n_sel, SEL_BLOCK, DH)
    vs_b = v_slc.reshape(B, G, n_sel, SEL_BLOCK, DH)
    kw = jnp.pad(k_win, ((0, 0), (0, 0), (WINDOW, 0), (0, 0)))
    vw = jnp.pad(v_win, ((0, 0), (0, 0), (WINDOW, 0), (0, 0)))
    bi = jnp.arange(B)[:, None, None, None]
    gi = jnp.arange(G)[None, :, None, None]
    scale = DH ** -0.5

    def query_block(i):
        t0 = i * NSA_QBLOCK
        t = t0 + jnp.arange(NSA_QBLOCK)
        qb = lax.dynamic_slice_in_dim(q, t0, NSA_QBLOCK, axis=3) * scale
        gb = lax.dynamic_slice_in_dim(gates, t0, NSA_QBLOCK, axis=3)
        s_c = jnp.einsum('bghqd,bgcd->bghqc', qb, kc)
        p_c = masked_softmax(s_c, cmp_end[None, :] <= t[:, None])
        o_c = jnp.einsum('bghqc,bgcd->bghqd', p_c.astype(vc.dtype), vc)
        imp = jnp.einsum('bghqc,cj->bgqj', p_c, sel_map)
        blk = jnp.arange(n_sel)[None, :]
        cur = (t // SEL_BLOCK)[:, None]
        forced = (blk == 0) | (blk == cur) | (blk == cur - 1)
        imp = jnp.where(forced, FORCE_SCORE, jnp.where(blk > cur, -FORCE_SCORE, imp))
        _, sel = lax.top_k(imp, top_n)
        k_sel = ks_b[bi, gi, sel].reshape(B, G, NSA_QBLOCK, top_n * SEL_BLOCK, DH)
        v_sel = vs_b[bi, gi, sel].reshape(B, G, NSA_QBLOCK, top_n * SEL_BLOCK, DH)
        kpos = (sel[..., None] * SEL_BLOCK + jnp.arange(SEL_BLOCK)).reshape(
            B, G, NSA_QBLOCK, top_n * SEL_BLOCK)
        s_s = jnp.einsum('bghqd,bgqnd->bghqn', qb, k_sel)
        p_s = masked_softmax(s_s, (kpos <= t[:, None])[:, :, None])
        o_s = jnp.einsum('bghqn,bgqnd->bghqd', p_s.astype(v_sel.dtype), v_sel)
        k_w = lax.dynamic_slice_in_dim(kw, t0, WINDOW + NSA_QBLOCK, axis=2)
        v_w = lax.dynamic_slice_in_dim(vw, t0, WINDOW + NSA_QBLOCK, axis=2)
        wpos = t0 - WINDOW + jnp.arange(WINDOW + NSA_QBLOCK)
        wmask = ((wpos[None, :] <= t[:, None]) & (wpos[None, :] > t[:, None] - WINDOW)
                 & (wpos[None, :] >= 0))
        s_w = jnp.einsum('bghqd,bgkd->bghqk', qb, k_w)
        p_w = masked_softmax(s_w, wmask)
        o_w = jnp.einsum('bghqk,bgkd->bghqd', p_w.astype(v_w.dtype), v_w)
        o = gb[..., 0:1] * o_c + gb[..., 1:2] * o_s + gb[..., 2:3] * o_w
        return o.astype(x.dtype)

    ob = lax.map(query_block, jnp.arange(S // NSA_QBLOCK))
    o_nsa = ob.transpose(1, 0, 4, 2, 3, 5).reshape(B, S, NSA_WIDTH)
    o_pool = pool_mixer(u, pool_w, pool_scale)
    return jnp.concatenate([o_nsa, o_pool], axis=-1) @ w_out

def gla_mixer(x, w_in, gate_w2, gate_b, norm_g, w_out):
    B, S, _ = x.shape
    N, C, H = S // GLA_CHUNK, GLA_CHUNK, GLA_HEADS
    h = x @ w_in
    o1 = GLA_KEY_WIDTH
    o2 = o1 + GLA_KEY_WIDTH
    o3 = o2 + GLA_VAL_WIDTH
    o4 = o3 + GLA_VAL_WIDTH
    q_, k_, v_, r, a = h[..., :o1], h[..., o1:o2], h[..., o2:o3], h[..., o3:o4], h[..., o4:]
    loga = jax.nn.log_sigmoid((a @ gate_w2 + gate_b).astype(jnp.float32)) / GLA_TAU

    def heads(t, d):
        return t.reshape(B, N, C, H, d).transpose(0, 3, 1, 2, 4).astype(jnp.float32)

    q = heads(q_, GLA_DK) * GLA_DK ** -0.5
    k = heads(k_, GLA_DK)
    v = heads(v_, GLA_DV)
    b = jnp.cumsum(heads(loga, GLA_DK), axis=3)
    q_t = q * jnp.exp(b)
    k_t = k * jnp.exp(-b)
    causal = jnp.tril(jnp.ones((C, C), dtype=bool))
    att = jnp.where(causal, jnp.einsum('bhncd,bhnjd->bhncj', q_t, k_t), 0.0)
    o_intra = jnp.einsum('bhncj,bhnje->bhnce', att, v)
    b_last = b[:, :, :, -1:, :]
    upd = jnp.einsum('bhncd,bhnce->bhnde', k * jnp.exp(b_last - b), v)
    decay = jnp.exp(b_last[:, :, :, 0])

    def step(state, inp):
        d, u = inp
        return d[..., None] * state + u, state

    s0 = jnp.zeros((B, H, GLA_DK, GLA_DV), jnp.float32)
    _, s_prev = lax.scan(step, s0, (jnp.moveaxis(decay, 2, 0), jnp.moveaxis(upd, 2, 0)))
    s_prev = jnp.moveaxis(s_prev, 0, 2)
    o = o_intra + jnp.einsum('bhncd,bhnde->bhnce', q_t, s_prev)
    o = o * lax.rsqrt(jnp.mean(jnp.square(o), axis=-1, keepdims=True) + LN_EPS) * norm_g
    o = o.transpose(0, 2, 3, 1, 4).reshape(B, S, GLA_VAL_WIDTH).astype(x.dtype)
    return (o * jax.nn.silu(r)) @ w_out

def sqrelu_mlp(x, w1, w2):
    return jnp.square(jax.nn.relu(x @ w1)) @ w2

def second_inputs(seed: int = 0) -> dict:
    key = jax.random.key(seed)
    ks = jax.random.split(key, 24)

    def nrm(k, shape, scale):
        return jax.random.normal(k, shape, jnp.float32) * scale

    DH = NSA_HEAD_DIM
    return {
        "x": nrm(ks[0], (BATCH, SEQ, D_MODEL), 1.0),
        "a_w_in": nrm(ks[1], (N_EVEN, D_MODEL, A_IN), D_MODEL ** -0.5),
        "a_cmp_pos": nrm(ks[2], (N_EVEN, 2, CMP_BLOCK, DH), 0.1),
        "a_cmp_w1": nrm(ks[3], (N_EVEN, 2, CMP_BLOCK * DH, DH), (CMP_BLOCK * DH) ** -0.5),
        "a_cmp_b1": nrm(ks[4], (N_EVEN, 2, DH), 0.02),
        "a_cmp_w2": nrm(ks[5], (N_EVEN, 2, DH, DH), DH ** -0.5),
        "a_pool_w": nrm(ks[6], (N_EVEN, POOL_GROUPS, POOL_GROUP_DIM, POOL_GROUP_DIM), POOL_GROUP_DIM ** -0.5),
        "a_pool_scale": 1.0 + nrm(ks[7], (N_EVEN, POOL_WIDTH), 0.1),
        "a_w_out": nrm(ks[8], (N_EVEN, D_MODEL, D_MODEL), BETA * D_MODEL ** -0.5),
        "c_w_in": nrm(ks[9], (N_ODD, D_MODEL, C_IN), D_MODEL ** -0.5),
        "c_gate_w2": nrm(ks[10], (N_ODD, GLA_GATE_RANK, GLA_KEY_WIDTH), GLA_GATE_RANK ** -0.5),
        "c_gate_b": nrm(ks[11], (N_ODD, GLA_KEY_WIDTH), 0.1),
        "c_norm_g": 1.0 + nrm(ks[12], (N_ODD, GLA_DV), 0.1),
        "c_w_out": nrm(ks[13], (N_ODD, D_MODEL, D_MODEL), BETA * D_MODEL ** -0.5),
        "ln1_g": 1.0 + nrm(ks[14], (DEPTH_2, D_MODEL), 0.05),
        "ln1_b": nrm(ks[15], (DEPTH_2, D_MODEL), 0.02),
        "ln2_g": 1.0 + nrm(ks[16], (DEPTH_2, D_MODEL), 0.05),
        "ln2_b": nrm(ks[17], (DEPTH_2, D_MODEL), 0.02),
        "mlp_w1": nrm(ks[18], (DEPTH_2, D_MODEL, D_FF_2), D_MODEL ** -0.5),
        "mlp_w2": nrm(ks[19], (DEPTH_2, D_FF_2, D_MODEL), BETA * D_FF_2 ** -0.5),
    }

def second_block(x, a_w_in, a_cmp_pos, a_cmp_w1, a_cmp_b1, a_cmp_w2, a_pool_w, a_pool_scale,
              a_w_out, c_w_in, c_gate_w2, c_gate_b, c_norm_g, c_w_out,
              ln1_g, ln1_b, ln2_g, ln2_b, mlp_w1, mlp_w2):
    for i in range(DEPTH_2):
        j = i // 2
        if i % 2 == 0:
            mix = nsa_pool_mixer(x, a_w_in[j], a_cmp_pos[j], a_cmp_w1[j], a_cmp_b1[j],
                                 a_cmp_w2[j], a_pool_w[j], a_pool_scale[j], a_w_out[j])
        else:
            mix = gla_mixer(x, c_w_in[j], c_gate_w2[j], c_gate_b[j], c_norm_g[j], c_w_out[j])
        x = layer_norm(ALPHA * x + mix, ln1_g[i], ln1_b[i])
        x = layer_norm(ALPHA * x + sqrelu_mlp(x, mlp_w1[i], mlp_w2[i]), ln2_g[i], ln2_b[i])
    return x


def setup_inputs(seed=0):
    out = dict(first_inputs(seed))
    for name, value in second_inputs(seed + 1).items():
        if name != "x":
            out[name + "_2"] = value
    return out


def reference(
    x, c, w_ada, b_ada, w_in, b_forget, q_norm_gain, k_norm_gain, fox_out_gain, ret_out_gain,
    w_out, w_mlp_in, w_mlp_out, a_w_in_2, a_cmp_pos_2, a_cmp_w1_2, a_cmp_b1_2, a_cmp_w2_2,
    a_pool_w_2, a_pool_scale_2, a_w_out_2, c_w_in_2, c_gate_w2_2, c_gate_b_2, c_norm_g_2,
    c_w_out_2, ln1_g_2, ln1_b_2, ln2_g_2, ln2_b_2, mlp_w1_2, mlp_w2_2,
):
    x = first_block(
        x, c, w_ada, b_ada, w_in, b_forget, q_norm_gain, k_norm_gain, fox_out_gain,
        ret_out_gain, w_out, w_mlp_in, w_mlp_out,
    )
    return second_block(
        x, a_w_in_2, a_cmp_pos_2, a_cmp_w1_2, a_cmp_b1_2, a_cmp_w2_2, a_pool_w_2,
        a_pool_scale_2, a_w_out_2, c_w_in_2, c_gate_w2_2, c_gate_b_2, c_norm_g_2, c_w_out_2,
        ln1_g_2, ln1_b_2, ln2_g_2, ln2_b_2, mlp_w1_2, mlp_w2_2,
    )


_drawn_inputs = setup_inputs


def setup_inputs(seed=0):
    import zlib

    import numpy as np

    out = dict(_drawn_inputs(seed))
    spreads = {}
    factors = {'q_norm_gain': 8.0,
     'k_norm_gain': 8.0,
     'fox_out_gain': 8.0,
     'ret_out_gain': 7.239,
     'a_cmp_pos_2': 7.672,
     'a_cmp_b1_2': 54.69,
     'c_gate_b_2': 5.543}
    for name, (base, spread) in spreads.items():
        noise = np.random.default_rng([zlib.crc32(name.encode()), seed]).standard_normal(out[name].shape)
        drawn = base * np.exp(spread * noise) if base else spread * noise
        out[name] = __import__('jax').numpy.asarray(drawn.astype(out[name].dtype))
    for name, factor in factors.items():
        out[name] = (out[name] * factor).astype(out[name].dtype)
    return out
```

```python
from contextlib import ExitStack

import concourse.bass as bass
from concourse import mybir

F32 = mybir.dt.float32
F32R = mybir.dt.float32r
BF16 = mybir.dt.bfloat16
ACT = mybir.ActivationFunctionType
ALU = mybir.AluOpType
AX = mybir.AxisListType.X

P = 128
D = 1024
S = 256
NT = S // P
KC = D // P
FF = 4 * D
EPS = 1e-6
LN_EPS = 1e-5
ALPHA = 4.0 ** 0.25
GELU_C = 1.5957691216057308

TW = 1024
RAW = 8
SPL = 4
BLK = 4
KPT = 2
FFB = 256
MLP_STEPS = FF // FFB
MLP_TILES = 4 * MLP_STEPS
W_IN = [0, 512, 1024, 2056, 2568, 3080, 1536, 3592]
FF_COL = 2048
A_IN = [(512, 512), (0, 512), (1024, 280), (1304, 512)]
C_IN = [0, 512, 1024, 1536, 2048, 2560]
A16_COL = 3072
T_IN = 0
T_OUT = T_IN + BLK * len(W_IN)
T_MLP0 = T_OUT + 2 * BLK
T_AIN = T_MLP0 + MLP_TILES
T_AOUT = T_AIN + BLK * len(A_IN)
T_MLP1 = T_AOUT + 2 * BLK
T_CIN = T_MLP1 + MLP_TILES
T_COUT = T_CIN + BLK * len(C_IN)
T_MLP2 = T_COUT + 2 * BLK
ADA_ORDER = [1, 0, 2, 4, 3, 5]
ADA_FIRST = 2 * KC
ADA_ALL = 6 * KC


def raw_of(s):
    return ADA_FIRST + s + min(s, ADA_ALL - ADA_FIRST)


def raw_items(s0, s1):
    for s in range(s0, s1 + 1):
        yield "w", s
        if s < ADA_ALL - ADA_FIRST:
            yield "ada", ADA_FIRST + s


C_ID, C_TRI, C_TRC, C_SUF, C_IND, C_CAU, C_NEG = 0, 128, 384, 512, 640, 642, 770
C_COS, C_SIN, C_M01, C_MNG, C_HM = 898, 1154, 1410, 1440, 1470
C_ALL = 1478
NCMP = 15
HC = 8 * NCMP


def constants():
    import numpy as np
    c = np.zeros((P, C_ALL), np.float32)
    i = np.arange(P)
    s, t = i[:, None], i[None, :]
    same = (s // 64) == (t // 64)
    c[:, C_ID:C_ID + P] = np.eye(P)
    c[:, C_TRI:C_TRI + P] = s <= t
    c[:, C_TRI + P:C_TRI + 2 * P] = 1.0
    c[:, C_TRC:C_TRC + P] = (same & (s <= t)) / 16.0
    c[:, C_SUF:C_SUF + P] = (same & (s > t)) / 16.0
    c[:, C_IND:C_IND + 2] = (i[:, None] // 64 == np.arange(2)) / 16.0
    c[:, C_CAU:C_CAU + P] = same & (s <= t)
    c[:, C_NEG:C_NEG + P] = np.where(s >= t, 0.0, -1e30)
    freq = 10000.0 ** (-np.arange(0, P, 2, dtype=np.float32) / np.float32(P))
    for tile in range(NT):
        ang = (np.arange(P, dtype=np.float32) + P * tile)[:, None] * freq[None].astype(np.float32)
        c[:, C_COS + P * tile:C_COS + P * (tile + 1)] = np.tile(np.cos(ang), 2)
        c[:, C_SIN + P * tile:C_SIN + P * (tile + 1)] = np.concatenate([-np.sin(ang), np.sin(ang)], 1)
        seen = (np.arange(NCMP) * 16 + 31)[None, :] <= (i + P * tile)[:, None]
        c[:, C_M01 + NCMP * tile:C_M01 + NCMP * (tile + 1)] = seen
        c[:, C_MNG + NCMP * tile:C_MNG + NCMP * (tile + 1)] = np.where(seen, 0.0, -1e30)
    c[:, C_HM:C_HM + 8] = i[:, None] // NCMP == np.arange(8)
    decay = np.zeros((P, 4, 384), np.float64)
    q = np.arange(S)
    for h in range(4):
        lg = np.log(1.0 - 2.0 ** (-5.0 - h))
        d0, d1 = q[None, :] - s, t - s
        decay[:, h, 0:S] = np.where(d0 >= 0, np.exp(np.maximum(d0, 0) * lg), 0) * P ** -0.5
        decay[:, h, S:] = np.where(d1 >= 0, np.exp(np.maximum(d1, 0) * lg), 0) * P ** -0.5
    bands = np.zeros((P, 4, 384), np.float64)
    for g, w in enumerate((2, 4, 8, 16)):
        full = np.zeros((S, S))
        for a in range(S):
            full[max(0, a - w + 1):a + 1, a] = 1.0 / min(a + 1, w)
        full -= np.eye(S)
        bands[:, g, 0:S] = full[0:P]
        bands[:, g, S:] = full[P:, P:]
    sel = np.zeros((8, 8, S), np.float32)
    sel[np.arange(8), np.arange(8)] = 1.0
    return {"const_c": c, "decay_c": decay.reshape(P, -1).astype(np.float32),
            "bands_c": bands.reshape(P, -1).astype(np.float32), "sel_c": sel.reshape(8, -1)}


def block_program(nc, dram, out):
    with ExitStack() as ctx:
        def sb(name, shape, dt=F32):
            return ctx.enter_context(nc.sbuf_tensor(name, shape, dt))

        def sem(name):
            return ctx.enter_context(nc.semaphore(name))

        raw = sb("raw", [P, RAW, TW])
        whi = sb("whi", [P, SPL, TW], F32R)
        wlo = sb("wlo", [P, SPL, TW], F32R)
        x = sb("x", [P, NT, D])
        hT_hi = sb("hT_hi", [P, KC, S], F32R)
        hT_lo = sb("hT_lo", [P, KC, S], F32R)
        acc = sb("acc", [P, 6 * D])
        rows = sb("rows", [P, 2, D])
        proj = sb("proj", [P, NT, 3072])
        qT = sb("qT", [P, 2 * D])
        kT = sb("kT", [P, 2 * D])
        uhi = sb("uhi", [P, 2, 512], F32R)
        ulo = sb("ulo", [P, 2, 512], F32R)
        sc = sb("sc", [P, 2, 512])
        pr = sb("pr", [P, 2, 512])
        prT = sb("prT", [P, 2, 512])
        cst = sb("cst", [P, C_ALL])
        tab = sb("tab", [P, 1536])
        identb = sb("identb", [P, P], BF16)
        negb = sb("negb", [P, P], BF16)
        wsm = sb("wsm", [P, KC, 16])
        wsm_hi = sb("wsm_hi", [P, KC, 16], F32R)
        wsm_lo = sb("wsm_lo", [P, KC, 16], F32R)
        cvec = sb("cvec", [P, 4, KC])
        fgain = sb("fgain", [P, 512])
        rgain = sb("rgain", [P, 512])
        qkgain = sb("qkgain", [64, 3])
        bfor = sb("bfor", [P, 8])
        lf = sb("lf", [P, 6, 16])
        stat = sb("stat", [P, 160])
        rstd = sb("rstd", [P, 160])
        bn = sb("bn", [P, NT, 16])
        nhalf = sb("nhalf", [P, 8])
        nmax = sb("nmax", [P, 2, 4])
        rsum = sb("rsum", [P, NT, 16])
        rinv = sb("rinv", [P, NT, 16])
        nsm = sb("nsm", [64, 200])
        gel = sb("gel", [64, 6, 60])
        cred = sb("cred", [P, 4, 16])
        aT = sb("aT", [16, S])
        dec = sb("dec", [P, 4, 4])

        PJ = ctx.enter_context(nc.psum_tensor("PJ", [P, 4, 512], F32))
        AT = ctx.enter_context(nc.psum_tensor("AT", [P, 4, 512], F32))

        ident = cst[:, C_ID:C_ID + P]

        raw_full = [sem(f"raw_full{i}") for i in range(RAW)]
        hi_done = sem("hi_done")
        raw_done = sem("raw_done")
        w_used = sem("w_used")
        bank_free = [sem("bank_free0"), sem("bank_free1")]
        ld_c, ld_x, ld_cst, ld_row, ld_tab, ld_sel, ld_sm = [sem(n) for n in (
            "ld_c", "ld_x", "ld_cst", "ld_row", "ld_tab", "ld_sel", "ld_sm")]
        acc_zero, ld_bada = sem("acc_zero"), sem("ld_bada")
        exp_c, c_done = sem("exp_c"), sem("c_done")
        cast_done = sem("cast_done")
        ones_row = sem("ones_row")
        mod_mm, mod_row = sem("mod_mm"), sem("mod_row")
        var_ready, rstd_ready = sem("var_ready"), sem("rstd_ready")
        sq_done = sem("sq_done")
        sc_free = sem("sc_free")
        src_ready = sem("src_ready")
        tr_done, hThi_done, hTlo_done = sem("tr_done"), sem("hThi_done"), sem("hTlo_done")
        wsm_hi_done, wsm_done = sem("wsm_hi_done"), sem("wsm_done")
        dseq, aseq = sem("dseq"), sem("aseq")
        ff_mm, ff_abs, ff_ln, ff_done, cum_mm, cum_done = [sem(n) for n in (
            "ff_mm", "ff_abs", "ff_ln", "ff_done", "cum_mm", "cum_done")]
        qk_norm, hd_tr, hd_done = sem("qk_norm"), sem("hd_tr"), sem("hd_done")
        sel_done = sem("sel_done")
        at_mm, at_max, at_exp, at_tr, at_trd, at_pv, at_out = [sem(n) for n in (
            "at_mm", "at_max", "at_exp", "at_tr", "at_trd", "at_pv", "at_out")]
        rope_done, rt_tr, rt_done, rs_mm, rp_done, rv_mm = [sem(n) for n in (
            "rope_done", "rt_tr", "rt_done", "rs_mm", "rp_done", "rv_mm")]
        gate_exp = sem("gate_exp")
        x_upd = sem("x_upd")
        relu_done, uhi_done, ulo_done, usq = [sem(n) for n in (
            "relu_done", "uhi_done", "ulo_done", "usq")]
        n_ev = sem("n_ev")
        nt_tr, nt_done, kb_done, c_mm, c_z, c_e, c_gel, c2_mm, c2_done, cs_mm, cs_sub, cs_exp, cs_p = [sem(n) for n in (
            "nt_tr", "nt_done", "kb_done", "c_mm", "c_z", "c_e", "c_gel", "c2_mm", "c2_done", "cs_mm", "cs_sub",
            "cs_exp", "cs_p")]
        ct_tr, ct_done, cv_mm, cv_done, gates_done, pm_mm, pm_done, py_mm = [sem(n) for n in (
            "ct_tr", "ct_done", "cv_mm", "cv_done", "gates_done", "pm_mm", "pm_done", "py_mm")]
        ld_nsa, ld_gla = sem("ld_nsa"), sem("ld_gla")
        a_mm, a_ev, aT_tr, aT_done, z_mm, z_abs, z_ln, loga_done, b_mm, eb_done, kz_done = [sem(n) for n in (
            "a_mm", "a_ev", "aT_tr", "aT_done", "z_mm", "z_abs", "z_ln", "loga_done", "b_mm", "eb_done",
            "kz_done")]
        g_tr, g_trd, ga_mm, ga_done, up_st, st_done, go_mm, gv_done, gr_exp = [sem(n) for n in (
            "g_tr", "g_trd", "ga_mm", "ga_done", "up_st", "st_done", "go_mm", "gv_done", "gr_exp")]
        stored = sem("stored")

        def bank(pb, t):
            return PJ[:, 2 * (pb % 2) + t, :]

        B_IN, B_OUT = 0, 8
        B_MLP0, B_AIN = 10, 12
        B_AOUT, B_MLP1, B_CIN = 16, 18, 20
        B_COUT, B_MLP2 = 26, 28
        FQ, FK, FV, OG, RV, RG = 0, 512, 1024, 1536, 2048, 2560
        RQ, RK = RG, OG
        VCB, PCT, CSB = 1816, 2328, 2584
        RT_, GVR = 1816, 2840
        N_U = 1304
        N_GT = 1280
        KB, POOLW, POOLS = 4096, 5056, 5568
        LOGA, ST, GB, NG, GW2 = 0, 1024, 4096, 4608, 4864
        S_N1, S_FQ, S_FK, S_FO, S_RO, S_N2, S_LN, S_GO = 0, 2, 18, 34, 50, 58, 60, 68
        FOX = [(0, [0, 1, 2, 3]), (0, [4, 5, 6, 7]), (1, [0, 1]), (1, [2, 3]), (1, [4, 5]), (1, [6, 7])]
        NSA = [(0, [2 * g, 2 * g + 1]) for g in range(4)] + [(1, [g]) for g in range(8)]
        NF, NN = len(FOX), len(NSA)

        def rows_of(t):
            return slice(t * P, (t + 1) * P)

        raw_slot = lambda r: raw[:, r % RAW, :]
        block = ctx.enter_context(nc.Block())

        @block.sync
        def _(sp):
            def fetch(r, src, view=None):
                if r >= RAW:
                    sp.wait_ge(raw_done, r - RAW + 1)
                dst = raw_slot(r)
                sp.dma_start(dst if view is None else view(dst), src).then_inc(raw_full[r % RAW], 16)

            def fetch_ada(n):
                r = n if n < ADA_FIRST else raw_of(n - ADA_FIRST) + 1
                col = ADA_ORDER[n // KC] * D
                k = n % KC
                fetch(r, dram["w_ada"][0, k * P:(k + 1) * P, col:col + D])

            def fetch_block(w, s0, col, n=512):
                for i in range(BLK):
                    src = w[i * KPT * P:(i + 1) * KPT * P, col:col + n].rearrange("(k p) n -> p k n", p=P)
                    fetch(raw_of(s0 + i), src,
                          lambda d: d.rearrange("p (k n) -> p k n", k=KPT)[:, :, 0:n])
                    if s0 + i < ADA_ALL - ADA_FIRST:
                        fetch_ada(ADA_FIRST + s0 + i)

            w1_view = lambda d: d.rearrange("p (k n) -> p k n", k=4)

            def fetch_mlp(w1, w2, s0):
                def up(r, half, col):
                    src = w1[half * 512:(half + 1) * 512, bass.ds(col, FFB)] if not isinstance(col, int) else \
                        w1[half * 512:(half + 1) * 512, col:col + FFB]
                    return r, src.rearrange("(k p) n -> p k n", p=P), w1_view

                def down(r, row):
                    return r, (w2[bass.ds(row, P), :] if not isinstance(row, int) else w2[row:row + P, :]), None

                def pair(r, p):
                    return [up(r, 0, (p + 1) * FFB), up(r + 1, 1, (p + 1) * FFB),
                            down(r + 2, p * FFB), down(r + 3, p * FFB + P)]

                r0 = raw_of(s0)
                for f in [up(r0, 0, 0), up(r0 + 1, 1, 0)] + pair(r0 + 2, 0):
                    fetch(*f)
                with sp.Fori(0, (MLP_STEPS - 2) // 2) as i:
                    for q in range(2):
                        for r, src, view in pair(r0 + 6 + 4 * q, i * 2 + (q + 1)):
                            sp.wait_ge(raw_done, i * 8 + (r - RAW + 1))
                            dst = raw_slot(r)
                            sp.dma_start(dst if view is None else view(dst), src).then_inc(raw_full[r % RAW], 16)
                last = (MLP_STEPS - 1) * FFB
                for f in [down(r0 + MLP_TILES - 2, last), down(r0 + MLP_TILES - 1, last + P)]:
                    fetch(*f)

            for n in range(ADA_FIRST):
                fetch_ada(n)
            for b, col in enumerate(W_IN):
                fetch_block(dram["w_in"][0], T_IN + BLK * b, col)
            for h in range(2):
                fetch_block(dram["w_out"][0], T_OUT + BLK * h, 512 * h)
            fetch_mlp(dram["w_mlp_in"][0], dram["w_mlp_out"][0], T_MLP0)
            for b, (col, n) in enumerate(A_IN):
                fetch_block(dram["a_w_in_2"][0], T_AIN + BLK * b, col, n)
            for h in range(2):
                fetch_block(dram["a_w_out_2"][0], T_AOUT + BLK * h, 512 * h)
            fetch_mlp(dram["mlp_w1_2"][0], dram["mlp_w2_2"][0], T_MLP1)
            for b, col in enumerate(C_IN):
                fetch_block(dram["c_w_in_2"][0], T_CIN + BLK * b, col)
            for h in range(2):
                fetch_block(dram["c_w_out_2"][0], T_COUT + BLK * h, 512 * h)
            fetch_mlp(dram["mlp_w1_2"][1], dram["mlp_w2_2"][1], T_MLP2)
            for t in range(NT):
                sp.wait_ge(src_ready, 18 + t + 1)
                sp.dma_start(out[0, rows_of(t), :], x[:, t, :]).then_inc(stored, 16)
            sp.wait_ge(stored, 16 * NT)

        @block.gpsimd
        def _(pool):
            asked = [0]

            def rsqrt(col, n):
                asked[0] += 1
                pool.wait_ge(var_ready, asked[0])
                nc.gpsimd.tensor_tensor(rstd[:, col:col + n], stat[:, col:col + n], nhalf[:, 0:n],
                                        ALU.pow).then_inc(rstd_ready, 1)

            def bcast(dst, src):
                return pool.dma_start(dst, src.unsqueeze(0).broadcast_to([P, src.shape[0]]))

            nc.gpsimd.memset(acc[:, :], 0.0).then_inc(acc_zero, 1)
            nc.gpsimd.memset(nhalf[:, :], -0.5).then_inc(acc_zero, 1)
            pool.wait_ge(acc_zero, 2)
            pool.dma_start(acc[0:1, :], dram["b_ada"]).then_inc(ld_bada, 16)
            rsqrt(S_N1, 1)
            rsqrt(S_N1 + 1, 1)
            pool.wait_ge(rstd_ready, 2)
            nc.gpsimd.memset(kT[64:P, :], 0.0).then_inc(acc_zero, 1)
            pool.wait_ge(tr_done, 4)
            pool.wait_ge(acc_zero, 3)
            nc.gpsimd.memset(qT[64:P, :], 0.0).then_inc(acc_zero, 1)
            pool.wait_ge(acc_zero, 4)
            pool.dma_start(qT[64:72, :], dram["sel_c"]).then_inc(ld_sel, 16)
            pool.dma_start(kT[96:104, :], dram["sel_c"]).then_inc(ld_sel, 16)
            for c in (S_FQ, S_FK):
                rsqrt(c, 8)
                rsqrt(c + 8, 8)
            for t in range(NT):
                rsqrt(S_FO + 8 * t, 8)
            for t in range(NT):
                rsqrt(S_RO + 4 * t, 4)
            pool.wait_ge(rp_done, 4)
            pool.dma_start(tab[:, :], dram["bands_c"]).then_inc(ld_tab, 16)

            def load_ln(n):
                g, b = (("ln1_g_2", "ln1_b_2"), ("ln2_g_2", "ln2_b_2"))[n % 2]
                bcast(rows[:, 0, :], dram[g][n // 2]).then_inc(ld_row, 16)
                bcast(rows[:, 1, :], dram[b][n // 2]).then_inc(ld_row, 16)

            load_ln(0)
            rsqrt(S_N2, 1)
            rsqrt(S_N2 + 1, 1)
            pool.wait_ge(src_ready, 8)
            pool.dma_start(acc[0:64, 0:4096].rearrange("d (i j e) -> d i j e", i=2, j=32),
                           dram["a_cmp_w1_2"][0].rearrange("i (j d) e -> d i j e", d=64)).then_inc(ld_nsa, 16)
            pool.dma_start(acc[:, POOLW:POOLW + 512].rearrange("c (g d) -> c g d", g=4),
                           dram["a_pool_w_2"][0].rearrange("g c d -> c g d")).then_inc(ld_nsa, 16)
            bcast(acc[:, POOLS:POOLS + 512], dram["a_pool_scale_2"][0]).then_inc(ld_nsa, 16)
            for t in range(NT):
                rsqrt(S_LN + t, 1)
            pool.wait_ge(src_ready, 10)
            bcast(acc[:, GB:GB + 512], dram["c_gate_b_2"][0]).then_inc(ld_gla, 16)
            bcast(acc[:, NG:NG + 256], dram["c_norm_g_2"][0]).then_inc(ld_gla, 16)
            pool.dma_start(acc[0:16, GW2:GW2 + 512], dram["c_gate_w2_2"][0]).then_inc(ld_gla, 16)
            pool.wait_ge(wsm_done, 1)
            pool.wait_ge(ff_mm, 1)
            pool.dma_start(wsm[:, :, :], dram["c_w_in_2"][0][:, A16_COL:A16_COL + 16].rearrange(
                "(k p) n -> p k n", p=P)).then_inc(ld_gla, 16)
            pool.wait_ge(src_ready, 12)
            load_ln(1)
            for t in range(NT):
                rsqrt(S_LN + 2 + t, 1)
            pool.wait_ge(src_ready, 14)
            load_ln(2)
            for t in range(NT):
                rsqrt(S_GO + 4 * t, 4)
            for t in range(NT):
                rsqrt(S_LN + 4 + t, 1)
            pool.wait_ge(src_ready, 18)
            load_ln(3)
            for t in range(NT):
                rsqrt(S_LN + 6 + t, 1)

        @block.scalar
        def _(act):
            order = [0]

            def link(ins):
                order[0] += 1
                ins.then_inc(aseq, 1)
                act.wait_ge(aseq, order[0])

            nxt = [0]

            def hi_to(s1):
                while nxt[0] <= s1:
                    s = nxt[0]
                    r = raw_of(s)
                    act.wait_ge(raw_full[r % RAW], 16 * (r // RAW + 1))
                    if s >= SPL:
                        act.wait_ge(w_used, s - SPL + 1)
                    nc.scalar.activation(whi[:, s % SPL, :], raw_slot(r), ACT.Copy).then_inc(hi_done, 1)
                    nxt[0] += 1

            def hT_hi_stage(n):
                for t in range(NT):
                    for j in range(2):
                        act.wait_ge(tr_done, 4 * n + 2 * t + j + 1)
                        nc.scalar.activation(hT_hi[:, 4 * j:4 * j + 4, rows_of(t)],
                                             AT[:, 2 * t + j, :].rearrange("p (c s) -> p c s", c=4),
                                             ACT.Copy).then_inc(hThi_done, 1)

            def sq_sum(t, col):
                nc.scalar.activation(qT[:, t * D:(t + 1) * D], x[:, t, :], ACT.Square,
                                     accum_out=stat[:, col:col + 1]).then_inc(sq_done, 1)

            def mlp(m, s0):
                r0, j0 = raw_of(s0), m * MLP_STEPS

                def hi(k, i=None):
                    s, r = s0 + k, r0 + k
                    act.wait_ge(raw_full[r % RAW], 16 * (r // RAW + 1) if i is None else i * 16 + 16 * (r // RAW + 1))
                    act.wait_ge(w_used, s - SPL + 1 if i is None else i * 8 + (s - SPL + 1))
                    nc.scalar.activation(whi[:, s % SPL, :], raw_slot(r), ACT.Copy).then_inc(hi_done, 1)

                def relu(j, i=None):
                    n = j0 + j
                    at = (lambda v: v if i is None else i * 2 + v)
                    used = s0 + (2 + 2 * j if j < 2 else 4 * j)
                    act.wait_ge(w_used, used if i is None else i * 8 + used)
                    if n >= 1:
                        act.wait_ge(usq, at(n))
                        act.wait_ge(uhi_done, at(n))
                    nc.scalar.activation(pr[:, 0, :], AT[:, j % 2, :], ACT.Relu).then_inc(relu_done, 1)
                    act.wait_ge(relu_done, at(n + 1))
                    nc.scalar.activation(uhi[:, j % 2, :], pr[:, 0, :], ACT.Square).then_inc(uhi_done, 1)

                hi(0)
                hi(1)
                for k in range(2, 4):
                    hi(k)
                relu(0)
                for k in range(4, 6):
                    hi(k)
                relu(1)
                with act.Fori(0, (MLP_STEPS - 2) // 2) as i:
                    for q in range(2):
                        for k in range(4):
                            hi(6 + 4 * q + k, i)
                        relu(2 + q, i)
                for k in range(MLP_TILES - 2, MLP_TILES):
                    hi(k)
                nxt[0] = s0 + MLP_TILES

            act.dma_start(cvec[:, 0, :], dram["c"].rearrange("a (k p) -> p (a k)", p=P),
                          allow_slow_non_contiguous=True).then_inc(ld_c, 16)
            for t in range(NT):
                act.dma_start(x[:, t, :], dram["x"][0, rows_of(t), :]).then_inc(ld_x, 16)
            act.dma_start(cst[:, :], dram["const_c"]).then_inc(ld_cst, 16)
            act.dma_start(wsm[:, :, 0:8], dram["w_in"][0][:, FF_COL:FF_COL + 8].rearrange(
                "(k p) n -> p k n", p=P)).then_inc(ld_sm, 16)
            act.dma_start(bfor[:, :], dram["b_forget"].broadcast_to([P, 8])).then_inc(ld_sm, 16)
            act.dma_start(qkgain[:, 0:1], dram["q_norm_gain"].rearrange("a d -> d a"),
                          allow_slow_non_contiguous=True).then_inc(ld_sm, 16)
            act.dma_start(qkgain[:, 1:2], dram["k_norm_gain"].rearrange("a d -> d a"),
                          allow_slow_non_contiguous=True).then_inc(ld_sm, 16)
            act.dma_start(fgain[:, :], dram["fox_out_gain"].rearrange("a h d -> a (h d)").broadcast_to(
                [P, 512])).then_inc(ld_sm, 16)
            act.dma_start(rgain[:, :], dram["ret_out_gain"].rearrange("a h d -> a (h d)").broadcast_to(
                [P, 512])).then_inc(ld_sm, 16)
            act.dma_start(tab[:, :], dram["decay_c"]).then_inc(ld_sm, 16)
            act.dma_start(nsm[:, 0:64].rearrange("d (i j) -> d i j", i=2),
                          dram["a_cmp_pos_2"][0].rearrange("i j d -> d i j"), allow_slow_non_contiguous=True).then_inc(ld_sm, 16)
            act.dma_start(nsm[:, 64:66], dram["a_cmp_b1_2"][0].rearrange("i e -> e i"),
                          allow_slow_non_contiguous=True).then_inc(ld_sm, 16)
            act.dma_start(nsm[:, 66:194].rearrange("e (i d) -> e i d", i=2),
                          dram["a_cmp_w2_2"][0].rearrange("i e d -> e i d")).then_inc(ld_sm, 16)
            act.wait_ge(ld_c, 16)
            nc.scalar.activation(cvec[:, 1, :], cvec[:, 0, :], ACT.Exp, scale=-1.0).then_inc(exp_c, 1)
            act.wait_ge(ld_x, 16 * NT)
            sq_sum(0, S_N1)
            sq_sum(1, S_N1 + 1)
            act.wait_ge(ld_cst, 16)
            nc.scalar.activation(identb[:, :], ident, ACT.Copy).then_inc(cast_done, 1)
            nc.scalar.activation(negb[:, :], cst[:, C_NEG:C_NEG + P], ACT.Copy).then_inc(cast_done, 1)
            act.wait_ge(ld_sm, 160)
            nc.scalar.activation(qkgain[:, 2:3], qkgain[:, 0:1], ACT.Copy, scale=0.125).then_inc(cast_done, 1)
            nc.scalar.activation(wsm_hi[:, :, 0:8], wsm[:, :, 0:8], ACT.Copy).then_inc(wsm_hi_done, 1)
            hi_to(3)
            hT_hi_stage(0)
            act.wait_ge(ff_abs, 1)
            link(nc.scalar.activation(lf[:, 2, :], lf[:, 1, :], ACT.Exp, scale=-1.0))
            nc.scalar.activation(lf[:, 3, :], lf[:, 2, :], ACT.Ln, bias=1.0).then_inc(ff_ln, 1)
            hi_to(5)

            def head_squares(b):
                act.wait_ge(w_used, T_IN + BLK * (b + 1))
                for t in range(NT):
                    if b > 0:
                        act.wait_ge(sc_free, 2 * (b - 1) + t + 1)
                    nc.scalar.activation(sc[:, t, :], bank(b, t), ACT.Square).then_inc(sq_done, 1)

            head_squares(0)
            hi_to(8)
            act.wait_ge(cum_mm, 1)
            act.wait_ge(acc_zero, 3)
            nc.scalar.activation(kT[64:72, :].rearrange("r (h s) -> r h s", h=8),
                                 AT[64:72, 1, 0:S].unsqueeze(1).broadcast_to([8, 8, S]), ACT.Copy,
                                 scale=-1.0).then_inc(cum_done, 1)
            hi_to(9)
            head_squares(1)
            hi_to(10)

            def heads_out(f):
                t, j = (f // 2) % 2, f % 2
                act.wait_ge(hd_tr, f + 1)
                dst = (qT if f < 4 else kT)[0:64, :].rearrange("d (h s) -> d h s", h=8)
                gain = qkgain[:, 2:3] if f < 4 else qkgain[:, 1:2]
                nc.scalar.activation(dst[:, 4 * j:4 * j + 4, rows_of(t)],
                                     AT[0:64, 2 + f % 2, :].rearrange("d (h s) -> d h s", h=4), ACT.Copy,
                                     scale=gain).then_inc(hd_done, 1)

            act.wait_ge(cast_done, 3)
            for f in range(4):
                heads_out(f)
            hi_to(13)
            act.wait_ge(w_used, T_IN + BLK * 3)
            for t in range(NT):
                nc.scalar.activation(proj[:, t, FV:FV + 512], bank(2, t), ACT.Copy).then_inc(bank_free[0], 1)
            for f in range(4, 8):
                heads_out(f)
            hi_to(16)

            def exps(g, groups, base):
                t, heads = groups[g]
                n = base + g
                act.wait_ge(at_max, n + 1)
                act.wait_ge(at_tr, n - 1) if n >= 2 else None
                fox = groups is FOX
                units = len(heads) if fox else 2 * len(heads)
                w = 512 // units
                for u in range(units):
                    col = heads[u] if fox else 8 * (u % 2) + heads[u // 2]
                    ins = nc.scalar.activation(pr[:, n % 2, u * w:(u + 1) * w], AT[:, g % 2, u * w:(u + 1) * w],
                                               ACT.Exp, bias=nmax[:, n % 2, u:u + 1],
                                               accum_out=rsum[:, t, col:col + 1])
                ins.then_inc(at_exp, 1)

            for g in range(NF):
                exps(g, FOX, 0)
                hi_to([16, 18, 19, 20, 22, 24][g])
            for t in range(NT):
                act.wait_ge(at_out, t + 1)
                act.wait_ge(sc_free, 5 + t)
                nc.scalar.activation(sc[:, 0, :], proj[:, t, FQ:FQ + 512], ACT.Square).then_inc(sq_done, 1)
            hi_to(25)
            act.wait_ge(w_used, T_IN + BLK * 6)
            for t in range(NT):
                nc.scalar.activation(proj[:, t, RV:RV + 512], bank(5, t), ACT.Copy).then_inc(bank_free[1], 1)

            def turned_out(f):
                t = f % 2
                act.wait_ge(rt_tr, f + 1)
                nc.scalar.activation(rows[:, f // 2, :].rearrange("d (h s) -> d h s", h=4)[:, :, rows_of(t)],
                                     AT[:, f % 2, :].rearrange("d (h s) -> d h s", h=4),
                                     ACT.Copy).then_inc(rt_done, 1)

            for f in range(4):
                turned_out(f)
            hi_to(29)
            act.wait_ge(w_used, T_IN + BLK * 7)
            for t in range(NT):
                nc.scalar.activation(proj[:, t, OG:OG + 512], bank(6, t), ACT.Exp, scale=-1.0).then_inc(gate_exp, 1)
            hi_to(31)
            act.wait_ge(w_used, T_IN + BLK * 8)
            for t in range(NT):
                nc.scalar.activation(proj[:, t, RG:RG + 512], bank(7, t), ACT.Exp, scale=-1.0).then_inc(gate_exp, 1)
            hi_to(34)
            for t in range(NT):
                act.wait_ge(rv_mm, 4)
                act.wait_ge(sc_free, 7 + t)
                nc.scalar.activation(sc[:, 0, :], AT[:, 2 + t, :], ACT.Square).then_inc(sq_done, 1)
            hi_to(35)
            hT_hi_stage(1)
            hi_to(T_MLP0 - 1)
            for t in range(NT):
                act.wait_ge(x_upd, 3 + t)
                sq_sum(t, S_N2 + t)
            hT_hi_stage(2)
            mlp(0, T_MLP0)
            hi_to(T_AIN + 3)
            hT_hi_stage(3)
            hi_to(T_AIN + 7)

            def nt_out(f, dst):
                act.wait_ge(nt_tr, f + 1)
                nc.scalar.activation(dst, AT[0:64, 2 + f % 2, :] if dst.shape[1] == 512 else
                                     AT[0:64, 2 + f % 2, :].rearrange("d (h s) -> d h s", h=4),
                                     ACT.Copy).then_inc(nt_done, 1)

            for f in range(3):
                nt_out(f, kT[0:64, f * 512:(f + 1) * 512])
            hi_to(T_AIN + 9)
            act.wait_ge(w_used, T_AIN + 8)
            for t in range(NT):
                nc.scalar.activation(proj[:, t, 0:512], bank(B_AIN + 1, t), ACT.Copy, scale=0.125)\
                    .then_inc(bank_free[1], 1)
            act.wait_ge(c_mm, 1)
            for i in range(2):
                ins = nc.scalar.activation(gel[:, 0, 30 * i:30 * i + 30], AT[0:64, 0, 32 * i:32 * i + 30], ACT.Identity,
                                           bias=nsm[:, 64 + i:65 + i])
            ins.then_inc(c_z, 1)
            hi_to(T_AIN + 11)
            act.wait_ge(c_e, 1)
            nc.scalar.activation(gel[:, 3, :], gel[:, 2, :], ACT.Exp, scale=-GELU_C).then_inc(c_gel, 1)
            qT8 = qT[0:64, :].rearrange("d (h s) -> d h s", h=8)
            for f in range(3, 7):
                t, j = (f - 3) // 2, (f - 3) % 2
                nt_out(f, qT8[:, 4 * j:4 * j + 4, rows_of(t)])
            hi_to(T_AIN + 14)
            act.wait_ge(w_used, T_AIN + 12)
            for t in range(NT):
                nc.scalar.activation(proj[:, t, 1024:1304], bank(B_AIN + 2, t)[:, 0:280], ACT.Copy)\
                    .then_inc(bank_free[0], 1)
            act.wait_ge(bank_free[0], 2 * ((B_AIN + 2) // 2) + 2)
            nc.scalar.activation(proj[:, :, N_GT:N_GT + 24], proj[:, :, N_GT:N_GT + 24], ACT.Exp,
                                 scale=-1.0).then_inc(gate_exp, 1)
            nt_out(7, kT[0:64, 1536:2048])
            hi_to(T_AIN + 16)
            act.wait_ge(cs_sub, 1)
            nc.scalar.activation(proj[:, 0, CSB:CSB + 240], proj[:, 0, CSB:CSB + 240], ACT.Exp).then_inc(cs_exp, 1)
            exps(0, NSA, NF)
            exps(1, NSA, NF)
            hi_to(T_AIN + 19)
            act.wait_ge(ct_tr, 1)
            nc.scalar.activation(proj[0:HC, 0, PCT:PCT + S], AT[0:HC, 2, 0:S], ACT.Copy).then_inc(ct_done, 1)
            for g in range(2, NN):
                if g == 4:
                    for k in range(2):
                        act.wait_ge(pm_mm, k + 1)
                        nc.scalar.activation(proj[:, 1, RT_ + 512 * k:RT_ + 512 * (k + 1)], PJ[:, k, :],
                                             ACT.Copy).then_inc(pm_done, 1)
                exps(g, NSA, NF)
            hT_hi_stage(4)
            hi_to(T_MLP1 - 1)
            hT_hi_stage(5)
            mlp(1, T_MLP1)
            act.wait_ge(ld_gla, 64)
            act.wait_ge(ff_mm, 1)
            nc.scalar.activation(wsm_hi[:, :, :], wsm[:, :, :], ACT.Copy).then_inc(wsm_hi_done, 1)
            hi_to(T_CIN + 3)
            hT_hi_stage(6)
            hi_to(T_CIN + 5)
            act.wait_ge(aT_tr, 1)
            nc.scalar.activation(aT[:, :], AT[0:16, 1, 0:S], ACT.Copy).then_inc(aT_done, 1)
            act.wait_ge(w_used, T_CIN + 4)
            for t in range(NT):
                nc.scalar.activation(proj[:, t, 0:512], bank(B_CIN, t), ACT.Copy, scale=P ** -0.5)\
                    .then_inc(bank_free[0], 1)
            hi_to(T_CIN + 10)
            act.wait_ge(w_used, T_CIN + 8)
            for t in range(NT):
                nc.scalar.activation(proj[:, t, 512:1024], bank(B_CIN + 1, t), ACT.Copy).then_inc(bank_free[1], 1)
            for t in range(NT):
                act.wait_ge(z_abs, t + 1)
                link(nc.scalar.activation(pr[:, t, :], prT[:, t, :], ACT.Exp, scale=-1.0))
                nc.scalar.activation(prT[:, t, :], pr[:, t, :], ACT.Ln, bias=1.0).then_inc(z_ln, 1)
            hi_to(T_CIN + 14)
            for t in range(NT):
                act.wait_ge(b_mm, t + 1)
                if t:
                    act.wait_ge(kz_done, 1)
                nc.scalar.activation(sc[:, 0, :], AT[:, 2 * t, :], ACT.Exp).then_inc(eb_done, 1)
                nc.scalar.activation(sc[:, 1, :], AT[:, 2 * t, :], ACT.Exp, scale=-1.0).then_inc(eb_done, 1)
                nc.scalar.activation(pr[:, 0, :], AT[:, 2 * t + 1, :], ACT.Exp).then_inc(eb_done, 1)
            act.wait_ge(b_mm, 3)
            nc.scalar.activation(dec[:, :, :].rearrange("p a b -> p (a b)"), AT[:, 0, 0:16], ACT.Exp)\
                .then_inc(eb_done, 1)
            hi_to(T_CIN + 16)
            act.wait_ge(w_used, T_CIN + 12)
            for t in range(NT):
                nc.scalar.activation(proj[:, t, 1024:1536], bank(B_CIN + 2, t), ACT.Copy).then_inc(bank_free[0], 1)
            hi_to(T_CIN + 18)
            act.wait_ge(w_used, T_CIN + 16)
            for t in range(NT):
                nc.scalar.activation(proj[:, t, 1536:2048], bank(B_CIN + 3, t), ACT.Copy).then_inc(bank_free[1], 1)
            for f in range(4):
                act.wait_ge(g_tr, f + 1)
                nc.scalar.activation((qT, kT)[f % 2][:, 0:D].rearrange("d (h s) -> d h s", h=4)[:, :, rows_of(f // 2)],
                                     AT[:, (1, 2, 3, 1)[f], :].rearrange("d (h s) -> d h s", h=4),
                                     ACT.Copy).then_inc(g_trd, 1)
            hi_to(T_CIN + 22)
            act.wait_ge(w_used, T_CIN + 20)
            for t in range(NT):
                nc.scalar.activation(proj[:, t, 2048:2560], bank(B_CIN + 4, t), ACT.Exp, scale=-1.0).then_inc(gr_exp, 1)
            hi_to(T_CIN + 24)
            act.wait_ge(w_used, T_CIN + 24)
            for t in range(NT):
                nc.scalar.activation(proj[:, t, 2560:3072], bank(B_CIN + 5, t), ACT.Exp, scale=-1.0).then_inc(gr_exp, 1)
            hi_to(T_CIN + 27)
            for t in range(NT):
                act.wait_ge(go_mm, t + 1)
                if t:
                    act.wait_ge(gv_done, 1)
                for j in range(2):
                    nc.scalar.activation(sc[:, j, :], AT[:, 2 * t + j, :], ACT.Square).then_inc(sq_done, 1)
            hT_hi_stage(7)
            hi_to(T_MLP2 - 1)
            hT_hi_stage(8)
            mlp(2, T_MLP2)

        @block.vector
        def _(dve):
            order = [0]

            def link(ins):
                order[0] += 1
                ins.then_inc(dseq, 1)
                dve.wait_ge(dseq, order[0])

            tt, ts, stt = nc.vector.tensor_tensor, nc.vector.tensor_scalar, nc.vector.scalar_tensor_tensor
            ada_at = lambda n: acc[:, ADA_ORDER[n // KC] * D:(ADA_ORDER[n // KC] + 1) * D]

            def add_ada(n, r):
                dve.wait_ge(raw_full[r % RAW], 16 * (r // RAW + 1))
                if n >= 1:
                    dve.wait_ge(raw_done, r)
                stt(ada_at(n), raw_slot(r), cvec[:, 3, n % KC:n % KC + 1], ada_at(n), ALU.mult, ALU.add)\
                    .then_inc(raw_done, 1)

            nxt = [0]

            def lo_to(s1):
                for kind, n in raw_items(nxt[0], s1):
                    if kind == "w":
                        dve.wait_ge(hi_done, n + 1)
                        tt(wlo[:, n % SPL, :], raw_slot(raw_of(n)), whi[:, n % SPL, :].bitcast(F32),
                           ALU.subtract).then_inc(raw_done, 1)
                    else:
                        add_ada(n, raw_of(n - ADA_FIRST) + 1)
                nxt[0] = max(nxt[0], s1 + 1)

            def hT_lo_stage(n):
                for t in range(NT):
                    for j in range(2):
                        dve.wait_ge(hThi_done, 4 * n + 2 * t + j + 1)
                        hi = hT_hi[:, 4 * j:4 * j + 4, rows_of(t)].bitcast(F32)
                        tt(hT_lo[:, 4 * j:4 * j + 4, rows_of(t)],
                           AT[:, 2 * t + j, :].rearrange("p (c s) -> p c s", c=4), hi,
                           ALU.subtract).then_inc(hTlo_done, 1)

            asked = [0]

            def rsqrt_of(col, n, ins=None):
                asked[0] += 1
                dve.wait_ge(rstd_ready, asked[0])

            def variance(col, n, width, eps=EPS):
                ts(stat[:, col:col + n], stat[:, col:col + n], 1.0 / width, eps, ALU.mult, ALU.add).then_inc(var_ready, 1)

            def modulated_norm(sq0, col, scale, shift, stage):
                for t in range(NT):
                    dve.wait_ge(sq_done, sq0 + t + 1)
                    variance(col + t, 1, D)
                for t in range(NT):
                    rsqrt_of(col + t, 1)
                    h = qT[:, t * D:(t + 1) * D]
                    link(stt(h, x[:, t, :], rstd[:, col + t:col + t + 1], scale, ALU.mult, ALU.mult))
                    tt(h, h, shift, ALU.add).then_inc(src_ready, 1)

            mod = lambda i: acc[:, i * D:(i + 1) * D]

            def mod_row_out(n, i, one):
                for j in range(2):
                    dve.wait_ge(mod_mm, 2 * n + 2)
                    a = AT[:, (0, 2, 0, 0, 2, 0)[n] + j, :]
                    ts(acc[:, i * D + 512 * j:i * D + 512 * (j + 1)], a, 1.0 if one else 0.0, None, ALU.add)\
                        .then_inc(mod_row, 1)

            def add_gated(pb, s_last, gate, n):
                for h in range(2):
                    for t in range(NT):
                        dve.wait_ge(w_used, s_last[h] + 1)
                        tmp = sc[:, t, :]
                        xs = x[:, t, 512 * h:512 * (h + 1)]
                        ins = tt(tmp, bank(pb + h, t), gate[:, 512 * h:512 * (h + 1)], ALU.mult)
                        ins.then_inc(bank_free[(pb + h) % 2], 1)
                        dve.wait_ge(bank_free[(pb + h) % 2], 2 * ((pb + h) // 2) + t + 1)
                        yield h, t, tt(xs, xs, tmp, ALU.add)

            def layer_norm(n, pb, s_last, stage):
                c = S_LN + 2 * n
                for t in range(NT):
                    for h in range(2):
                        dve.wait_ge(w_used, s_last[h] + 1)
                        xs = x[:, t, 512 * h:512 * (h + 1)]
                        stt(xs, xs, ALPHA, bank(pb + h, t), ALU.mult, ALU.add).then_inc(bank_free[(pb + h) % 2], 1)
                        dve.wait_ge(bank_free[(pb + h) % 2], 2 * ((pb + h) // 2) + t + 1)
                        link(nc.vector.bn_stats(bn[:, t, 6 * h:6 * h + 6], xs))
                    link(nc.vector.bn_aggr(bn[:, t, 12:14], bn[:, t, 0:12].rearrange("p (a b) -> p a b", a=2)))
                    ts(stat[:, c + t:c + t + 1], bn[:, t, 13:14], LN_EPS, None, ALU.add).then_inc(var_ready, 1)
                dve.wait_ge(ld_row, 32 * (n + 1))
                for t in range(NT):
                    rsqrt_of(c + t, 1)
                    xs = x[:, t, :]
                    link(ts(xs, xs, bn[:, t, 12:13], rstd[:, c + t:c + t + 1], ALU.subtract, ALU.mult))
                    link(tt(xs, xs, rows[:, 0, :], ALU.mult))
                    tt(xs, xs, rows[:, 1, :], ALU.add).then_inc(src_ready, 1)

            def mlp(m, s0):
                r0, j0 = raw_of(s0), m * MLP_STEPS

                def lo(k, i=None):
                    s, r = s0 + k, r0 + k
                    dve.wait_ge(hi_done, s + 1 if i is None else i * 8 + (s + 1))
                    tt(wlo[:, s % SPL, :], raw_slot(r), whi[:, s % SPL, :].bitcast(F32), ALU.subtract)\
                        .then_inc(raw_done, 1)

                def square(j, i=None):
                    n = j0 + j
                    at = (lambda v: v if i is None else i * 2 + v)
                    dve.wait_ge(relu_done, at(n + 1))
                    if n >= 1:
                        dve.wait_ge(ulo_done, at(n))
                    tt(pr[:, 1, :], pr[:, 0, :], pr[:, 0, :], ALU.mult).then_inc(usq, 1)
                    dve.wait_ge(usq, at(n + 1))
                    dve.wait_ge(uhi_done, at(n + 1))
                    tt(ulo[:, j % 2, :], pr[:, 1, :], uhi[:, j % 2, :].bitcast(F32), ALU.subtract).then_inc(ulo_done, 1)

                for k in range(4):
                    lo(k)
                square(0)
                lo(4)
                lo(5)
                square(1)
                with dve.Fori(0, (MLP_STEPS - 2) // 2) as i:
                    for q in range(2):
                        for k in range(4):
                            lo(6 + 4 * q + k, i)
                        square(2 + q, i)
                lo(MLP_TILES - 2)
                lo(MLP_TILES - 1)
                nxt[0] = s0 + MLP_TILES

            dve.wait_ge(exp_c, 1)
            link(ts(cvec[:, 1, :], cvec[:, 1, :], 1.0, None, ALU.add))
            link(nc.vector.reciprocal(cvec[:, 2, :], cvec[:, 1, :]))
            link(tt(cvec[:, 3, :], cvec[:, 2, :], cvec[:, 0, :], ALU.mult))
            dve.wait_ge(ld_bada, 16)
            for n in range(ADA_FIRST):
                add_ada(n, n)
            mod_row_out(0, 1, True)
            mod_row_out(1, 0, False)
            dve.wait_ge(mod_row, 4)
            modulated_norm(0, S_N1, mod(1), mod(0), 0)
            dve.wait_ge(wsm_hi_done, 1)
            tt(wsm_lo[:, :, 0:8], wsm[:, :, 0:8], wsm_hi[:, :, 0:8].bitcast(F32), ALU.subtract).then_inc(wsm_done, 1)
            lo_to(1)
            hT_lo_stage(0)
            lo_to(2)
            dve.wait_ge(ff_mm, 1)
            lf2 = lambda k: lf[:, k, :].rearrange("p (t h) -> p t h", t=NT)
            link(tt(lf2(0), AT[:, 0, 0:16].rearrange("p (t h) -> p t h", t=NT),
                    bfor[:, :].unsqueeze(1).broadcast_to([P, NT, 8]), ALU.add))
            stt(lf[:, 1, :], lf[:, 0, :], -1.0, lf[:, 0, :], ALU.mult, ALU.max).then_inc(ff_abs, 1)
            lo_to(4)
            dve.wait_ge(ff_ln, 1)
            stt(lf[:, 4, :], lf[:, 0, :], 0.0, lf[:, 3, :], ALU.min, ALU.subtract).then_inc(ff_done, 1)
            lo_to(5)

            def head_norm(b, col, sq0):
                for t in range(NT):
                    c = col + 8 * t
                    dve.wait_ge(sq_done, sq0 + t + 1)
                    ins = nc.vector.tensor_reduce(stat[:, c:c + 8], sc[:, t, :].rearrange("p (h d) -> p h d", h=8),
                                                  AX, ALU.add)
                    ins.then_inc(sc_free, 1)
                    dve.wait_ge(sc_free, 2 * b + t + 1)
                    variance(c, 8, 64)
                for t in range(NT):
                    c = col + 8 * t
                    rsqrt_of(c, 8)
                    tt(proj[:, t, FQ + 512 * b:FQ + 512 * (b + 1)].rearrange("p (h d) -> p h d", h=8),
                       bank(b, t).rearrange("p (h d) -> p h d", h=8),
                       rstd[:, c:c + 8].unsqueeze(2).broadcast_to([P, 8, 64]), ALU.mult).then_inc(qk_norm, 1)
                    dve.wait_ge(qk_norm, 2 * b + t + 1)
                    dve.nop().then_inc(bank_free[b % 2], 1)

            head_norm(0, S_FQ, 2)
            lo_to(7)
            dve.wait_ge(cum_done, 1)
            dve.wait_ge(ld_sel, 32)
            nc.vector.tensor_copy(qT[96:104, :].rearrange("r (h s) -> r h s", h=8),
                                  AT[96:104, 1, S:2 * S].unsqueeze(1).broadcast_to([8, 8, S])).then_inc(cum_done, 1)
            lo_to(9)
            head_norm(1, S_FK, 4)
            lo_to(14)

            def maxima(g, groups, base):
                t, heads = groups[g]
                n = base + g
                units = len(heads) if groups is FOX else 2 * len(heads)
                dve.wait_ge(at_mm, n + 1)
                if n >= 2:
                    dve.wait_ge(at_exp, n - 1)
                nc.vector.tensor_reduce(nmax[:, n % 2, 0:units], AT[:, g % 2, :].rearrange("p (u k) -> p u k", u=units),
                                        AX, ALU.max, negate=True).then_inc(at_max, 1)

            def probs_out(g, base):
                n = base + g
                dve.wait_ge(at_tr, n + 1)
                if n >= 2:
                    dve.wait_ge(at_pv, n - 1)
                nc.vector.tensor_copy(prT[:, n % 2, :], AT[:, 2, :]).then_inc(at_trd, 1)

            heads8 = lambda a: a.rearrange("p (h d) -> p h d", h=8)
            wide = lambda a, d: a.unsqueeze(2).broadcast_to([P, a.shape[1], d])

            def fox_out(t):
                dve.wait_ge(at_pv, (2, 6)[t])
                link(nc.vector.reciprocal(rinv[:, t, 0:8], rsum[:, t, 0:8]))
                dve.wait_ge(hd_tr, 4)
                tt(heads8(proj[:, t, FQ:FQ + 512]), heads8(AT[:, 3, :]), wide(rinv[:, t, 0:8], 64), ALU.mult)\
                    .then_inc(at_out, 1)

            def rotate(b, dst, n):
                dve.wait_ge(w_used, T_IN + BLK * (b + 1))
                for t in range(NT):
                    xh = bank(b, t).rearrange("p (h d) -> p h d", h=4)
                    cos = cst[:, C_COS + P * t:C_COS + P * (t + 1)].unsqueeze(1).broadcast_to([P, 4, P])
                    sin = cst[:, C_SIN + P * t:C_SIN + P * (t + 1)].unsqueeze(1).broadcast_to([P, 4, P])
                    a = sc[:, 0, :].rearrange("p (h d) -> p h d", h=4)
                    c = sc[:, 1, :].rearrange("p (h d) -> p h d", h=4)
                    tt(a, xh, cos, ALU.mult)
                    tt(c[:, :, 0:64], xh[:, :, 64:P], sin[:, :, 0:64], ALU.mult)
                    ins = tt(c[:, :, 64:P], xh[:, :, 0:64], sin[:, :, 64:P], ALU.mult)
                    ins.then_inc(bank_free[b % 2], 1)
                    dve.wait_ge(bank_free[b % 2], 2 * (b // 2) + t + 1)
                    link(tt(proj[:, t, dst:dst + 512], sc[:, 0, :], sc[:, 1, :], ALU.add))
                dve.nop().then_inc(rope_done, 1)

            maxima(0, FOX, 0)
            maxima(1, FOX, 0)
            lo_to(16)
            rotate(3, RQ, 0)
            probs_out(0, 0)
            lo_to(17)
            maxima(2, FOX, 0)
            probs_out(1, 0)
            lo_to(18)
            maxima(3, FOX, 0)
            fox_out(0)
            lo_to(20)
            probs_out(2, 0)
            maxima(4, FOX, 0)
            lo_to(21)
            rotate(4, RK, 1)
            dve.nop().then_inc(sc_free, 1)
            probs_out(3, 0)
            maxima(5, FOX, 0)
            lo_to(23)
            probs_out(4, 0)
            probs_out(5, 0)
            lo_to(24)
            fox_out(1)

            def squares_summed(sq, col, n, width, k):
                dve.wait_ge(sq_done, sq)
                ins = nc.vector.tensor_reduce(stat[:, col:col + n], sc[:, 0, :].rearrange("p (h d) -> p h d", h=n),
                                              AX, ALU.add)
                ins.then_inc(sc_free, 1)
                dve.wait_ge(sc_free, k)
                variance(col, n, width)

            for t in range(NT):
                squares_summed(7 + t, S_FO + 8 * t, 8, 64, 5 + t + 1)
            lo_to(26)
            for t in range(NT):
                rsqrt_of(S_FO + 8 * t, 8)
                o = heads8(proj[:, t, FQ:FQ + 512])
                tt(o, o, wide(rstd[:, S_FO + 8 * t:S_FO + 8 * t + 8], 64), ALU.mult)

            def decayed(h):
                dve.wait_ge(rs_mm, h + 1)
                if h >= 2:
                    dve.wait_ge(rv_mm, h - 1)
                tt(pr[:, h % 2, 0:384], AT[:, h % 2, 0:384], tab[:, 384 * h:384 * (h + 1)], ALU.mult).then_inc(rp_done, 1)

            decayed(0)
            decayed(1)
            lo_to(28)
            decayed(2)
            decayed(3)
            for t in range(NT):
                dve.wait_ge(gate_exp, t + 1)
                dve.nop().then_inc(bank_free[0], 1)
                g = proj[:, t, OG:OG + 512]
                link(ts(g, g, 1.0, None, ALU.add))
                link(nc.vector.reciprocal(g, g))
                link(tt(g, g, fgain[:, :], ALU.mult))
                link(tt(proj[:, t, FQ:FQ + 512], proj[:, t, FQ:FQ + 512], g, ALU.mult))
            lo_to(31)
            mod_row_out(2, 2, False)
            for t in range(NT):
                squares_summed(9 + t, S_RO + 4 * t, 4, P, 7 + t + 1)
            for t in range(NT):
                dve.wait_ge(gate_exp, 2 + t + 1)
                g = proj[:, t, RG:RG + 512]
                link(ts(g, g, 1.0, None, ALU.add))
                link(nc.vector.reciprocal(g, g))
                link(tt(g, g, bank(7, t), ALU.mult))
                dve.nop().then_inc(bank_free[1], 1)
                link(tt(g, g, rgain[:, :], ALU.mult))
            lo_to(33)
            for t in range(NT):
                rsqrt_of(S_RO + 4 * t, 4)
                o = proj[:, t, FK:FK + 512].rearrange("p (h d) -> p h d", h=4)
                dve.wait_ge(hd_tr, 8)
                link(tt(o, AT[:, 2 + t, :].rearrange("p (h d) -> p h d", h=4), wide(
                    rstd[:, S_RO + 4 * t:S_RO + 4 * t + 4], P), ALU.mult))
                tt(proj[:, t, FK:FK + 512], proj[:, t, FK:FK + 512], proj[:, t, RG:RG + 512], ALU.mult)\
                    .then_inc(src_ready, 1)
            hT_lo_stage(1)
            lo_to(36)
            mod_row_out(3, 4, True)
            mod_row_out(4, 3, False)
            lo_to(38)
            mod_row_out(5, 5, False)
            lo_to(T_MLP0 - 1)
            upd = [0]
            for h, t, ins in add_gated(B_OUT, (T_OUT + 3, T_OUT + 7), mod(2), 0):
                ins.then_inc(x_upd, 1)
            dve.wait_ge(mod_row, 12)
            modulated_norm(10, S_N2, mod(4), mod(3), 2)
            hT_lo_stage(2)
            mlp(0, T_MLP0)
            for h, t, ins in add_gated(B_MLP0, (T_AIN - 1, T_AIN - 1), mod(5), 1):
                (ins.then_inc(src_ready, 1) if h == 1 else link(ins))
            lo_to(T_AIN + 1)
            hT_lo_stage(3)
            lo_to(T_AIN + 5)
            dve.wait_ge(w_used, T_AIN + 4)
            for t in range(NT):
                nc.vector.tensor_copy(proj[:, t, 512:1024], bank(B_AIN, t)).then_inc(bank_free[0], 1)
            lo_to(T_AIN + 7)
            dve.wait_ge(ld_nsa, 48)
            for i in range(2):
                dve.wait_ge(nt_done, i + 1)
                src = kT[0:64, i * 512:(i + 1) * 512].rearrange("d (g c j) -> d j g c", g=2, j=16)
                dst = (acc if i == 0 else qT)[0:64, (KB if i == 0 else 0):(KB if i == 0 else 0) + 960]
                dst = dst.rearrange("d (b j g c) -> d b j g c", b=2, j=16, g=2)
                for half in range(2):
                    pos = nsm[:, 32 * i + 16 * half:32 * i + 16 * half + 16]
                    ins = tt(dst[:, half], src[:, :, :, half:half + NCMP],
                             pos.unsqueeze(2).unsqueeze(3).broadcast_to([64, 16, 2, NCMP]), ALU.add)
                ins.then_inc(kb_done, 1)
            lo_to(T_AIN + 10)
            dve.wait_ge(c_z, 1)
            link(tt(gel[:, 1, :], gel[:, 0, :], gel[:, 0, :], ALU.mult))
            link(ts(gel[:, 1, :], gel[:, 1, :], 0.044715, 1.0, ALU.mult, ALU.add))
            tt(gel[:, 2, :], gel[:, 1, :], gel[:, 0, :], ALU.mult).then_inc(c_e, 1)
            lo_to(T_AIN + 11)
            dve.wait_ge(c_gel, 1)
            link(ts(gel[:, 3, :], gel[:, 3, :], 1.0, None, ALU.add))
            link(nc.vector.reciprocal(gel[:, 4, :], gel[:, 3, :]))
            link(tt(gel[:, 5, :], gel[:, 4, :], gel[:, 0, :], ALU.mult))
            nc.vector.tensor_copy(proj[0:64, 1, GVR:GVR + HC].rearrange("e (g a c) -> e g a c", g=2, a=4),
                                  gel[:, 5, 30:60].rearrange("e (g c) -> e g c", g=2).unsqueeze(2).broadcast_to(
                                      [64, 2, 4, NCMP])).then_inc(c_gel, 1)
            lo_to(T_AIN + 13)
            dve.wait_ge(c2_mm, 1)
            nc.vector.tensor_copy(gel[:, 0, 0:30], AT[0:64, 1, 0:30]).then_inc(c2_done, 1)
            tt(proj[0:HC, 0, VCB:VCB + 512].rearrange("r (h d) -> r h d", h=8),
               AT[0:HC, 1, 64:128].unsqueeze(1).broadcast_to([HC, 8, 64]),
               cst[0:HC, C_HM:C_HM + 8].unsqueeze(2).broadcast_to([HC, 8, 64]), ALU.mult).then_inc(c2_done, 1)
            dve.wait_ge(gate_exp, 5)
            gt = proj[:, :, N_GT:N_GT + 24]
            link(ts(gt, gt, 1.0, None, ALU.add))
            link(nc.vector.reciprocal(gt, gt))
            lo_to(T_AIN + 15)
            dve.wait_ge(cs_mm, 1)
            csf = proj[:, 0, CSB:CSB + 240]
            cs = csf.rearrange("p (t h c) -> p t h c", t=NT, h=8)
            csr = csf.rearrange("p (r c) -> p r c", c=NCMP)
            m01 = cst[:, C_M01:C_M01 + 30].rearrange("p (t c) -> p t c", t=NT).unsqueeze(2).broadcast_to([P, NT, 8, NCMP])
            mng = cst[:, C_MNG:C_MNG + 30].rearrange("p (t c) -> p t c", t=NT).unsqueeze(2).broadcast_to([P, NT, 8, NCMP])
            link(tt(cs, AT[:, 0, 0:240].rearrange("p (t h c) -> p t h c", t=NT, h=8), m01, ALU.mult))
            dve.nop().then_inc(cs_p, 1)
            link(tt(cs, cs, mng, ALU.add))
            link(nc.vector.tensor_reduce(cred[:, 0, :], csr, AX, ALU.max))
            tt(csr, csr, wide(cred[:, 0, :], NCMP), ALU.subtract).then_inc(cs_sub, 1)
            maxima(0, NSA, NF)
            maxima(1, NSA, NF)
            dve.wait_ge(cs_exp, 1)
            link(tt(cs, cs, m01, ALU.mult))
            link(nc.vector.tensor_reduce(cred[:, 1, :], csr, AX, ALU.add))
            link(ts(cred[:, 1, :], cred[:, 1, :], 1e-30, None, ALU.max))
            link(nc.vector.reciprocal(cred[:, 2, :], cred[:, 1, :]))
            tt(csr, csr, wide(cred[:, 2, :], NCMP), ALU.mult).then_inc(cs_p, 1)
            gate = lambda t, br: proj[:, t, N_GT:N_GT + 24].rearrange("p (h b) -> p h b", b=3)[:, :, br]
            lo_to(T_AIN + 16)
            dve.wait_ge(w_used, T_AIN + 16)
            for t in range(NT):
                nc.vector.tensor_copy(proj[:, t, N_U:N_U + 512], bank(B_AIN + 3, t)).then_inc(n_ev, 1)
            for t in range(NT):
                dve.wait_ge(cv_mm, t + 1)
                tt(heads8(proj[:, t, 0:512]), heads8(AT[:, 3, :]), wide(gate(t, 0), 64), ALU.mult).then_inc(cv_done, 1)
            lo_to(T_AIN + 19)
            dve.wait_ge(n_ev, 2)
            dve.nop().then_inc(bank_free[1], 2)

            def branch_out(k):
                t, grp = k // 2, k % 2
                h0 = 4 * grp
                dve.wait_ge(at_pv, NF + (2, 4, 8, 12)[k])
                for br in range(2):
                    r = rsum[:, t, 8 * br + h0:8 * br + h0 + 4]
                    v = rinv[:, t, 8 * br + h0:8 * br + h0 + 4]
                    link(ts(v, r, 1e-30, None, ALU.max))
                    link(nc.vector.reciprocal(v, v))
                    link(tt(v, v, gate(t, 1 + br)[:, h0:h0 + 4], ALU.mult))
                w = rinv[:, t, :].rearrange("p (b h) -> p b h", b=2)[:, :, h0:h0 + 4]
                link(tt(sc[:, 0, :].rearrange("p (b h d) -> p b h d", b=2, h=4),
                        AT[:, 3, :].rearrange("p (b h d) -> p b h d", b=2, h=4),
                        w.unsqueeze(3).broadcast_to([P, 2, 4, 64]), ALU.mult))
                dve.nop().then_inc(at_out, 1)
                o = proj[:, t, 64 * h0:64 * h0 + 256]
                link(tt(o, o, sc[:, 0, 0:256], ALU.add))
                ins = tt(o, o, sc[:, 0, 256:512], ALU.add)
                link(ins)

            def pooled_out(t):
                dve.wait_ge(py_mm, t + 1)
                link(tt(proj[:, t, N_U:N_U + 512], PJ[:, 2 + t, :], acc[:, POOLS:POOLS + 512], ALU.mult))

            for g in range(NN):
                probs_out(g, NF)
                if g + 2 < NN:
                    maxima(g + 2, NSA, NF)
                if g == 2:
                    branch_out(0)
                if g == 4:
                    branch_out(1)
                if g == 6:
                    pooled_out(0)
                    pooled_out(1)
                if g == 8:
                    branch_out(2)
            branch_out(3)
            dve.nop().then_inc(src_ready, 2)
            hT_lo_stage(4)
            lo_to(T_MLP1 - 1)
            layer_norm(0, B_AOUT, (T_AOUT + 3, T_AOUT + 7), 5)
            hT_lo_stage(5)
            mlp(1, T_MLP1)
            layer_norm(1, B_MLP1, (T_CIN - 1, T_CIN - 1), 6)
            dve.wait_ge(wsm_hi_done, 2)
            tt(wsm_lo[:, :, :], wsm[:, :, :], wsm_hi[:, :, :].bitcast(F32), ALU.subtract).then_inc(wsm_done, 1)
            lo_to(T_CIN + 1)
            hT_lo_stage(6)
            lo_to(T_CIN + 3)
            dve.wait_ge(a_mm, 1)
            nc.vector.tensor_copy(lf[:, 0:2, :], AT[:, 0, 0:32].rearrange("p (t a) -> p t a", t=NT)).then_inc(a_ev, 1)
            lo_to(T_CIN + 8)
            for t in range(NT):
                la = acc[:, LOGA + 512 * t:LOGA + 512 * (t + 1)]
                dve.wait_ge(z_mm, t + 1)
                link(tt(la, AT[:, 2 + t, :], acc[:, GB:GB + 512], ALU.add))
                stt(prT[:, t, :], la, -1.0, la, ALU.mult, ALU.max).then_inc(z_abs, 1)
            lo_to(T_CIN + 9)
            for t in range(NT):
                la = acc[:, LOGA + 512 * t:LOGA + 512 * (t + 1)]
                dve.wait_ge(z_ln, t + 1)
                stt(la, la, 0.0, prT[:, t, :], ALU.min, ALU.subtract).then_inc(loga_done, 1)
            lo_to(T_CIN + 11)
            for t in range(NT):
                q, k = proj[:, t, 0:512], proj[:, t, 512:1024]
                dve.wait_ge(eb_done, 3 * t + 3)
                tt(q, q, sc[:, 0, :], ALU.mult)
                link(tt(kT[:, D + 512 * t:D + 512 * (t + 1)], k, pr[:, 0, :], ALU.mult))
                tt(k, k, sc[:, 1, :], ALU.mult).then_inc(kz_done, 1)
            lo_to(T_CIN + 17)
            for t in range(NT):
                dve.wait_ge(ga_mm, t + 1)
                tt(prT[:, t, :].rearrange("p (h s) -> p h s", h=4),
                   AT[:, (2, 3)[t], :].rearrange("p (h s) -> p h s", h=4),
                   cst[:, C_CAU:C_CAU + P].unsqueeze(1).broadcast_to([P, 4, P]), ALU.mult).then_inc(ga_done, 1)
            lo_to(T_CIN + 18)
            dve.wait_ge(eb_done, 7)
            st = lambda n, h: acc[:, ST + D * n + 256 * h:ST + D * n + 256 * (h + 1)]
            for n in range(3):
                for j in range(2):
                    dve.wait_ge(up_st, 2 * n + j + 1)
                    for h in (2 * j, 2 * j + 1):
                        ups = AT[:, j, 256 * (h % 2):256 * (h % 2 + 1)]
                        if n == 0:
                            ins = nc.vector.tensor_copy(st(0, h), ups)
                        else:
                            ins = stt(st(n, h), st(n - 1, h), dec[:, h, n:n + 1], ups, ALU.mult, ALU.add)
                    ins.then_inc(st_done, 1)
                    dve.wait_ge(st_done, 2 * n + j + 1)
                lo_to(T_CIN + (20, 21, 22)[n])
            for j in range(2):
                for t in range(NT):
                    dve.wait_ge(gr_exp, 2 * j + t + 1)
                    g = proj[:, t, 2048 + 512 * j:2048 + 512 * (j + 1)]
                    link(ts(g, g, 1.0, None, ALU.add))
                    link(nc.vector.reciprocal(g, g))
                    link(tt(g, g, bank(B_CIN + 4 + j, t), ALU.mult))
                    dve.nop().then_inc(bank_free[j], 1)
                    link(tt(g.rearrange("p (h d) -> p h d", h=2), g.rearrange("p (h d) -> p h d", h=2),
                            acc[:, NG:NG + 256].unsqueeze(1).broadcast_to([P, 2, 256]), ALU.mult))
                lo_to(T_CIN + (24, 26)[j])
            for t in range(NT):
                c = S_GO + 4 * t
                dve.wait_ge(sq_done, 12 + 2 * t + 2)
                ins = nc.vector.tensor_reduce(stat[:, c:c + 4], sc[:, :, :].rearrange("p j (h d) -> p (j h) d", h=2),
                                              AX, ALU.add)
                ins.then_inc(gv_done, 1)
                dve.wait_ge(gv_done, t + 1)
                variance(c, 4, 256, LN_EPS)
                rsqrt_of(c, 4)
                for j in range(2):
                    link(tt(proj[:, t, 512 * j:512 * (j + 1)].rearrange("p (h d) -> p h d", h=2),
                            AT[:, 2 * t + j, :].rearrange("p (h d) -> p h d", h=2),
                            wide(rstd[:, c + 2 * j:c + 2 * j + 2], 256), ALU.mult))
                tt(proj[:, t, 0:D], proj[:, t, 0:D], proj[:, t, 2048:3072], ALU.mult).then_inc(src_ready, 1)
            hT_lo_stage(7)
            lo_to(T_MLP2 - 1)
            layer_norm(2, B_COUT, (T_COUT + 3, T_COUT + 7), 8)
            hT_lo_stage(8)
            mlp(2, T_MLP2)
            layer_norm(3, B_MLP2, (T_MLP2 + MLP_TILES - 1, T_MLP2 + MLP_TILES - 1), 9)

        @block.tensor
        def _(pe):
            mm = nc.tensor.matmul

            def transposes(n, src, first_wait=()):
                for t in range(NT):
                    pe.wait_ge(src_ready, 2 * n + t + 1)
                    for s, v in (first_wait[t] if first_wait else ()):
                        pe.wait_ge(s, v)
                    for j in range(2):
                        for c in range(4):
                            ins = nc.tensor.transpose(AT[:, 2 * t + j, c * P:(c + 1) * P], src(t, 4 * j + c), ident)
                        ins.then_inc(tr_done, 1)

            def three(o, n_k, t, hi, lo, start, stop):
                a, b = hT_hi[:, n_k, rows_of(t)], hT_lo[:, n_k, rows_of(t)]
                mm(o, a, hi, start=start, stop=False)
                mm(o, a, lo, start=False, stop=False)
                return mm(o, b, hi, start=False, stop=stop)

            def tile_of(pb, s0, i, n=512):
                s = s0 + i
                pe.wait_ge(raw_done, raw_of(s) + 1)
                if i == 0 and pb >= 2:
                    pe.wait_ge(bank_free[pb % 2], 2 * (pb // 2))
                for t in range(NT):
                    for kk in range(KPT):
                        k = KPT * i + kk
                        ins = three(bank(pb, t)[:, 0:n], k, t, whi[:, s % SPL, 512 * kk:512 * kk + n],
                                    wlo[:, s % SPL, 512 * kk:512 * kk + n], k == 0, k == KC - 1)
                ins.then_inc(w_used, 1)

            def small(n, o, done):
                for t in range(NT):
                    for k in range(KC):
                        ins = three(AT[:, 0, n * t:n * (t + 1)], k, t, wsm_hi[:, k, 0:n], wsm_lo[:, k, 0:n],
                                    k == 0, k == KC - 1)
                ins.then_inc(done, 1)

            def mod_bcast(n, i, bank0):
                for j in range(2):
                    ins = mm(AT[:, bank0 + j, :], cst[:, C_TRI + P:C_TRI + 2 * P],
                             acc[:, i * D + 512 * j:i * D + 512 * (j + 1)], start=True, stop=True)
                    ins.then_inc(mod_mm, 1)

            def mlp(m, s0, pb):
                r0, j0 = raw_of(s0), m * MLP_STEPS

                def up(j, k0, i=None):
                    at = (lambda v, d: v if i is None else i * d + v)
                    if j0 + j >= 2:
                        pe.wait_ge(relu_done, at(j0 + j - 1, 2))
                    for half in range(2):
                        s, r = s0 + k0 + half, r0 + k0 + half
                        pe.wait_ge(raw_done, at(r + 1, 8))
                        for kk in range(4):
                            k = 4 * half + kk
                            for f in range(2):
                                o = AT[:, j % 2, f * S:(f + 1) * S]
                                c = slice(kk * FFB + f * P, kk * FFB + (f + 1) * P)
                                first = k == 0 and f == 0
                                last = k == KC - 1
                                mm(o, whi[:, s % SPL, c], hT_hi[:, k, :], start=first, stop=False, skip_group_check=True)
                                mm(o, whi[:, s % SPL, c], hT_lo[:, k, :], start=False, stop=False, skip_group_check=True)
                                ins = mm(o, wlo[:, s % SPL, c], hT_hi[:, k, :], start=False, stop=last,
                                         skip_group_check=True)
                        ins.then_inc(w_used, 1)

                def down(j, k0, i=None, first=False, last=False):
                    at = (lambda v, d: v if i is None else i * d + v)
                    pe.wait_ge(ulo_done, at(j0 + j + 1, 2))
                    if first:
                        for q in range(2):
                            pe.wait_ge(bank_free[q], 2 * (pb // 2))
                    for f in range(2):
                        s, r = s0 + k0 + f, r0 + k0 + f
                        pe.wait_ge(raw_done, at(r + 1, 8))
                        for t in range(NT):
                            c = slice(f * S + t * P, f * S + (t + 1) * P)
                            for h in range(2):
                                o = bank(pb + h, t)
                                w = slice(512 * h, 512 * (h + 1))
                                mm(o, uhi[:, j % 2, c], whi[:, s % SPL, w], start=first and f == 0, stop=False)
                                mm(o, uhi[:, j % 2, c], wlo[:, s % SPL, w], start=False, stop=False)
                                ins = mm(o, ulo[:, j % 2, c], whi[:, s % SPL, w], start=False, stop=last and f == 1)
                        ins.then_inc(w_used, 1)

                up(0, 0)
                up(1, 2)
                down(0, 4, first=True)
                with pe.Fori(0, (MLP_STEPS - 2) // 2) as i:
                    for q in range(2):
                        up(2 + q, 6 + 4 * q, i)
                        down(1 + q, 8 + 4 * q, i)
                down(MLP_STEPS - 1, MLP_TILES - 2, last=True)

            def softmax_scores(g, groups, base):
                t, heads = groups[g]
                n = base + g
                if g >= 2:
                    pe.wait_ge(at_exp, n - 1)
                kw = P * (t + 1)
                u = 0
                for h in heads:
                    if groups is FOX:
                        pairs = [(qT[0:104, h * S + t * P:h * S + (t + 1) * P], kT[0:104, h * S:h * S + kw])]
                    else:
                        q = qT[0:64, h * S + t * P:h * S + (t + 1) * P]
                        pairs = [(q, kT[0:64, b + S * (h // 4):b + S * (h // 4) + kw]) for b in (1024, 1536)]
                    for q, k in pairs:
                        o = AT[:, g % 2, u * kw:(u + 1) * kw]
                        mm(o, q, k, start=True, stop=False)
                        ins = mm(o[:, kw - P:kw], identb[:, :], negb[:, :], start=False, stop=True)
                        u += 1
                ins.then_inc(at_mm, 1)

            def prob_transposes(g, base):
                n = base + g
                pe.wait_ge(at_exp, n + 1)
                if n >= 1:
                    pe.wait_ge(at_trd, n)
                for c in range(4):
                    ins = nc.tensor.transpose(AT[:, 2, c * P:(c + 1) * P], pr[:, n % 2, c * P:(c + 1) * P], ident)
                ins.then_inc(at_tr, 1)

            def weighted_values(g, groups, base, v):
                t, heads = groups[g]
                n = base + g
                pe.wait_ge(at_trd, n + 1)
                brs = 1 if groups is FOX else 2
                b = 0
                for h in heads:
                    for br in range(brs):
                        col = 64 * h if brs == 1 else 256 * br + 64 * (h % 4)
                        for kt in range(t + 1):
                            ins = mm(AT[:, 3, col:col + 64], prT[:, n % 2, b * P:(b + 1) * P], v(h, br, kt),
                                     start=kt == 0, stop=kt == t)
                            b += 1
                ins.then_inc(at_pv, 1)

            pe.wait_ge(ld_cst, 16)
            pe.wait_ge(raw_done, KC)
            mod_bcast(0, 1, 0)
            pe.wait_ge(raw_done, 2 * KC)
            mod_bcast(1, 0, 2)
            transposes(0, lambda t, c: qT[:, t * D + c * P:t * D + (c + 1) * P], ([(mod_row, 2)], [(mod_row, 4)]))
            pe.wait_ge(hTlo_done, 4)
            pe.wait_ge(wsm_done, 1)
            small(8, AT, ff_mm)

            def cumulate():
                pe.wait_ge(ff_done, 1)
                for p0, c0 in ((64, 0), (96, S)):
                    mm(AT[p0:p0 + 8, 1, c0:c0 + S], lf[:, 4, 0:8], cst[:, C_TRI:C_TRI + S], start=True, stop=False)
                    ins = mm(AT[p0:p0 + 8, 1, c0 + P:c0 + S], lf[:, 4, 8:16], cst[:, C_TRI:C_TRI + P],
                             start=False, stop=True)
                ins.then_inc(cum_mm, 1)

            def head_transposes(f):
                t, j = (f // 2) % 2, f % 2
                pe.wait_ge(qk_norm, 2 * (f // 4) + t + 1)
                if f >= 2:
                    pe.wait_ge(hd_done, f - 1)
                c0 = FQ if f < 4 else FK
                for a in range(4):
                    h = 4 * j + a
                    ins = nc.tensor.transpose(AT[0:64, 2 + f % 2, a * P:(a + 1) * P],
                                              proj[:, t, c0 + 64 * h:c0 + 64 * (h + 1)], ident)
                ins.then_inc(hd_tr, 1)

            fox_v = lambda h, br, kt: proj[:, kt, FV + 64 * h:FV + 64 * (h + 1)]

            def fox(step, g):
                if step == "S":
                    if g == 0:
                        pe.wait_ge(hd_done, 8)
                        pe.wait_ge(cum_done, 2)
                        pe.wait_ge(ld_sel, 32)
                        pe.wait_ge(cast_done, 3)
                    softmax_scores(g, FOX, 0)
                elif step == "T":
                    prob_transposes(g, 0)
                else:
                    if g == 0:
                        pe.wait_ge(bank_free[0], 4)
                    if g == 2:
                        pe.wait_ge(at_out, 1)
                    weighted_values(g, FOX, 0, fox_v)

            def turn(f):
                t = f % 2
                if f == 0:
                    pe.wait_ge(at_exp, 6)
                pe.wait_ge(rope_done, f // 2 + 1)
                if f >= 2:
                    pe.wait_ge(rt_done, f - 1)
                c0 = RQ if f < 2 else RK
                for h in range(4):
                    ins = nc.tensor.transpose(AT[:, f % 2, h * P:(h + 1) * P], proj[:, t, c0 + h * P:c0 + (h + 1) * P],
                                              ident)
                ins.then_inc(rt_tr, 1)

            def ret_scores(h):
                pe.wait_ge(rt_done, 4)
                if h >= 2:
                    pe.wait_ge(rp_done, h - 1)
                q, k = rows[:, 0, h * S:(h + 1) * S], rows[:, 1, h * S:(h + 1) * S]
                mm(AT[:, h % 2, 0:S], k[:, 0:P], q, start=True, stop=True)
                mm(AT[:, h % 2, S:S + P], k[:, P:S], q[:, P:S], start=True, stop=True).then_inc(rs_mm, 1)

            def ret_values(h):
                pe.wait_ge(rp_done, h + 1)
                if h == 0:
                    pe.wait_ge(bank_free[1], 6)
                    pe.wait_ge(at_trd, 6)
                    pe.wait_ge(at_out, 2)
                v = lambda t: proj[:, t, RV + h * P:RV + (h + 1) * P]
                o = slice(h * P, (h + 1) * P)
                mm(AT[:, 2, o], pr[:, h % 2, 0:P], v(0), start=True, stop=True)
                mm(AT[:, 3, o], pr[:, h % 2, P:S], v(0), start=True, stop=False)
                mm(AT[:, 3, o], pr[:, h % 2, S:S + P], v(1), start=False, stop=True).then_inc(rv_mm, 1)

            def gate_row():
                pe.wait_ge(rp_done, 4)
                pe.wait_ge(raw_done, raw_of(KC - 1) + 2)
                mod_bcast(2, 2, 0)

            between = {
                5: [cumulate],
                9: [lambda f=f: head_transposes(f) for f in range(4)],
                13: [lambda f=f: head_transposes(f) for f in range(4, 8)],
                23: [lambda: turn(0), lambda: turn(1)], 24: [lambda: turn(2), lambda: turn(3)],
                25: [lambda: ret_scores(0), lambda: ret_scores(1)],
                26: [lambda: ret_values(0), lambda: ret_scores(2)],
                27: [lambda: ret_values(1), lambda: ret_scores(3)],
                28: [lambda: ret_values(2)], 29: [lambda: ret_values(3)], 30: [gate_row],
            }
            steps = "S0 S1 T0 S2 V0 T1 S3 V1 T2 S4 V2 T3 S5 V3 T4 V4 T5 V5".split()
            for n, st in enumerate(steps):
                between.setdefault(14 + n // 2, []).append(lambda a=st[0], g=int(st[1]): fox(a, g))
            for b in range(len(W_IN)):
                for i in range(BLK):
                    tile_of(B_IN + b, T_IN + BLK * b, i)
                    for step in between.get(BLK * b + i, ()):
                        step()
            transposes(1, lambda t, c: proj[:, t, c * P:(c + 1) * P], ([(mod_row, 6)], []))
            pe.wait_ge(hTlo_done, 8)
            for h in range(2):
                for i in range(BLK):
                    tile_of(B_OUT + h, T_OUT + BLK * h, i)
                    if (h, i) == (0, 2):
                        pe.wait_ge(raw_done, raw_of(31) + 2)
                        mod_bcast(3, 4, 0)
                        mod_bcast(4, 3, 2)
                    if (h, i) == (1, 1):
                        pe.wait_ge(mod_row, 8)
                        mod_bcast(5, 5, 0)
            transposes(2, lambda t, c: qT[:, t * D + c * P:t * D + (c + 1) * P], ([(mod_row, 12)], []))
            pe.wait_ge(hTlo_done, 12)
            mlp(0, T_MLP0, B_MLP0)

            transposes(3, lambda t, c: x[:, t, c * P:(c + 1) * P])
            pe.wait_ge(hTlo_done, 16)

            def nsa_transposes(f):
                if f < 3:
                    pe.wait_ge(bank_free[0], 2 * (B_AIN // 2) + 2)
                    srcs = [proj[:, t, 512 + P * f + 64 * g:512 + P * f + 64 * (g + 1)] for g in range(2) for t in range(NT)]
                elif f < 7:
                    t, j = (f - 3) // 2, (f - 3) % 2
                    pe.wait_ge(bank_free[1], 2 * ((B_AIN + 1) // 2) + 2)
                    if f == 3:
                        pe.wait_ge(c_mm, 1)
                    srcs = [proj[:, t, 64 * (4 * j + a):64 * (4 * j + a + 1)] for a in range(4)]
                else:
                    pe.wait_ge(bank_free[0], 2 * ((B_AIN + 2) // 2) + 2)
                    srcs = [proj[:, t, 1024 + 64 * g:1024 + 64 * (g + 1)] for g in range(2) for t in range(NT)]
                if f >= 2:
                    pe.wait_ge(nt_done, f - 1)
                for c, a in enumerate(srcs):
                    ins = nc.tensor.transpose(AT[0:64, 2 + f % 2, c * P:(c + 1) * P], a, ident)
                ins.then_inc(nt_tr, 1)

            def compress():
                for i in range(2):
                    pe.wait_ge(kb_done, i + 1)
                    kb = (acc if i == 0 else qT)[0:64, (KB if i == 0 else 0):(KB if i == 0 else 0) + 960]
                    for j in range(32):
                        ins = mm(AT[0:64, 0, 32 * i:32 * i + 30], acc[0:64, 2048 * i + 64 * j:2048 * i + 64 * (j + 1)],
                                 kb[:, 30 * j:30 * (j + 1)], start=j == 0, stop=j == 31)
                ins.then_inc(c_mm, 1)

            def compress2():
                pe.wait_ge(c_gel, 2)
                mm(AT[0:64, 1, 0:30], nsm[:, 66:130], gel[:, 5, 0:30], start=True, stop=True)
                mm(AT[0:HC, 1, 64:128], proj[0:64, 1, GVR:GVR + HC], nsm[:, 130:194], start=True, stop=True)\
                    .then_inc(c2_mm, 1)

            def cmp_scores():
                pe.wait_ge(c2_done, 2)
                pe.wait_ge(nt_done, 7)
                for t in range(NT):
                    for h in range(8):
                        ins = mm(AT[:, 0, HC * t + NCMP * h:HC * t + NCMP * (h + 1)],
                                 qT[0:64, h * S + t * P:h * S + (t + 1) * P],
                                 gel[:, 0, NCMP * (h // 4):NCMP * (h // 4 + 1)], start=True, stop=True)
                ins.then_inc(cs_mm, 1)

            nsa_v = lambda h, br, kt: proj[:, kt, (896, 1152)[br] + 64 * (h // 4):(896, 1152)[br] + 64 * (h // 4 + 1)]

            def nsa(step, g):
                if step == "S":
                    if g == 0:
                        pe.wait_ge(nt_done, 8)
                        pe.wait_ge(cs_p, 1)
                    softmax_scores(g, NSA, NF)
                elif step == "T":
                    if g == 0:
                        pe.wait_ge(ct_done, 1)
                    prob_transposes(g, NF)
                else:
                    if g == 0:
                        pe.wait_ge(cv_done, 2)
                    if g in (2, 4, 8):
                        pe.wait_ge(at_out, 2 + (2, 4, 8).index(g) + 1)
                    weighted_values(g, NSA, NF, nsa_v)

            def cmp_values():
                pe.wait_ge(cs_p, 2)
                for t in range(NT):
                    ins = nc.tensor.transpose(AT[0:HC, 2, t * P:(t + 1) * P], proj[:, 0, CSB + HC * t:CSB + HC * (t + 1)],
                                              ident)
                ins.then_inc(ct_tr, 1)
                pe.wait_ge(ct_done, 1)
                for t in range(NT):
                    if t:
                        pe.wait_ge(cv_done, 1)
                    mm(AT[:, 3, :], proj[0:HC, 0, PCT + t * P:PCT + (t + 1) * P], proj[0:HC, 0, VCB:VCB + 512],
                       start=True, stop=True).then_inc(cv_mm, 1)

            def pool_bands():
                pe.wait_ge(n_ev, 2)
                pe.wait_ge(ld_tab, 16)
                for g in range(4):
                    o = PJ[:, g // 2, (g % 2) * S:(g % 2 + 1) * S]
                    u = lambda t: proj[:, t, N_U + P * g:N_U + P * (g + 1)]
                    mm(o, u(0), tab[:, 384 * g:384 * g + S], start=True, stop=False)
                    ins = mm(o[:, P:S], u(1), tab[:, 384 * g + S:384 * (g + 1)], start=False, stop=True)
                    if g % 2:
                        ins.then_inc(pm_mm, 1)

            def pool_mix():
                pe.wait_ge(pm_done, 2)
                for t in range(NT):
                    for g in range(4):
                        ins = mm(PJ[:, 2 + t, P * g:P * (g + 1)], proj[:, 1, RT_ + S * g + P * t:RT_ + S * g + P * (t + 1)],
                                 acc[:, POOLW + P * g:POOLW + P * (g + 1)], start=True, stop=True)
                    ins.then_inc(py_mm, 1)

            between = {
                5: [lambda: nsa_transposes(0)], 6: [lambda: nsa_transposes(1)], 7: [lambda: nsa_transposes(2)],
                9: [compress], 10: [lambda: nsa_transposes(3), lambda: nsa_transposes(4)],
                11: [lambda: nsa_transposes(5), lambda: nsa_transposes(6)],
                12: [compress2], 13: [lambda: nsa_transposes(7)], 14: [cmp_scores],
            }
            for b, (col, n) in enumerate(A_IN):
                for i in range(BLK):
                    tile_of(B_AIN + b, T_AIN + BLK * b, i, n)
                    for step in between.get(BLK * b + i, ()):
                        step()
            nsa("S", 0)
            nsa("S", 1)
            cmp_values()
            for g in range(NN):
                nsa("T", g)
                if g + 2 < NN:
                    nsa("S", g + 2)
                nsa("V", g)
                if g == 0:
                    pool_bands()
                if g == 3:
                    pool_mix()
            transposes(4, lambda t, c: proj[:, t, c * P:(c + 1) * P] if c < 4 else
                       proj[:, t, N_U + (c - 4) * P:N_U + (c - 3) * P])
            pe.wait_ge(hTlo_done, 20)
            for h in range(2):
                for i in range(BLK):
                    tile_of(B_AOUT + h, T_AOUT + BLK * h, i)
            transposes(5, lambda t, c: x[:, t, c * P:(c + 1) * P])
            pe.wait_ge(hTlo_done, 24)
            mlp(1, T_MLP1, B_MLP1)

            transposes(6, lambda t, c: x[:, t, c * P:(c + 1) * P])
            pe.wait_ge(hTlo_done, 28)
            pe.wait_ge(wsm_done, 2)
            small(16, AT, a_mm)

            def gate_rank():
                pe.wait_ge(a_ev, 1)
                for t in range(NT):
                    ins = nc.tensor.transpose(AT[0:16, 1, t * P:(t + 1) * P], lf[:, t, :], ident)
                ins.then_inc(aT_tr, 1)

            def gate_logits():
                pe.wait_ge(aT_done, 1)
                pe.wait_ge(ld_gla, 64)
                for t in range(NT):
                    mm(AT[:, 2 + t, :], aT[:, rows_of(t)], acc[0:16, GW2:GW2 + 512], start=True, stop=True)\
                        .then_inc(z_mm, 1)

            def cumulated():
                for t in range(NT):
                    pe.wait_ge(loga_done, 2)
                    la = acc[:, LOGA + 512 * t:LOGA + 512 * (t + 1)]
                    mm(AT[:, 2 * t, :], cst[:, C_TRC:C_TRC + P], la, start=True, stop=True)
                    mm(AT[:, 2 * t + 1, :], cst[:, C_SUF:C_SUF + P], la, start=True, stop=True).then_inc(b_mm, 1)

            def chunk_decay():
                pe.wait_ge(eb_done, 2)
                for t in range(NT):
                    for h in range(4):
                        ins = mm(AT[:, 0, 4 * h + 2 * t:4 * h + 2 * t + 2],
                                 acc[:, LOGA + 512 * t + P * h:LOGA + 512 * t + P * (h + 1)],
                                 cst[:, C_IND:C_IND + 2], start=True, stop=True)
                ins.then_inc(b_mm, 1)

            def gla_transposes(f):
                t = f // 2
                pe.wait_ge(kz_done, t + 1)
                if f == 0:
                    pe.wait_ge(eb_done, 7)
                if f == 3:
                    pe.wait_ge(g_trd, 1)
                for h in range(4):
                    c0 = 512 * (f % 2) + P * h
                    ins = nc.tensor.transpose(AT[:, (1, 2, 3, 1)[f], h * P:(h + 1) * P], proj[:, t, c0:c0 + P], ident)
                ins.then_inc(g_tr, 1)

            def gla_scores(t):
                pe.wait_ge(g_trd, 4)
                for h in range(4):
                    c = slice(h * S + t * P, h * S + (t + 1) * P)
                    ins = mm(AT[:, (2, 3)[t], h * P:(h + 1) * P], kT[:, c], qT[:, c], start=True, stop=True)
                ins.then_inc(ga_mm, 1)

            def gla_update(n):
                if n == 0:
                    pe.wait_ge(bank_free[0], 2 * ((B_CIN + 2) // 2) + 2)
                    pe.wait_ge(bank_free[1], 2 * ((B_CIN + 3) // 2) + 2)
                t, p0 = n // 2, 64 * (n % 2)
                for j in range(2):
                    if n:
                        pe.wait_ge(st_done, 2 * (n - 1) + j + 1)
                    for h in (2 * j, 2 * j + 1):
                        ins = mm(AT[:, j, 256 * (h % 2):256 * (h % 2 + 1)],
                                 kT[p0:p0 + 64, D + 512 * t + P * h:D + 512 * t + P * (h + 1)],
                                 proj[p0:p0 + 64, t, 1024 + 256 * h:1024 + 256 * (h + 1)], start=True, stop=True)
                    ins.then_inc(up_st, 1)

            def gla_out(t):
                pe.wait_ge(st_done, 6)
                pe.wait_ge(ga_done, 2)
                for h in range(4):
                    o = AT[:, 2 * t + h // 2, 256 * (h % 2):256 * (h % 2 + 1)]
                    ins = mm(o, prT[:, t, h * P:(h + 1) * P], proj[:, t, 1024 + 256 * h:1024 + 256 * (h + 1)],
                             start=True, stop=False, skip_group_check=True)
                    for half in range(2):
                        n = 2 * t + half
                        if n:
                            c0 = h * S + 64 * n
                            ins = mm(o[64 * half:64 * half + 64, :], qT[:, c0:c0 + 64],
                                     acc[:, ST + D * (n - 1) + 256 * h:ST + D * (n - 1) + 256 * (h + 1)],
                                     start=False, stop=True, skip_group_check=True)
                ins.then_inc(go_mm, 1)

            between = {
                3: [gate_rank], 5: [gate_logits], 9: [cumulated], 11: [chunk_decay],
                14: [lambda f=f: gla_transposes(f) for f in range(3)], 15: [lambda: gla_transposes(3)],
                16: [lambda: gla_scores(0)], 17: [lambda: gla_scores(1)],
                18: [lambda: gla_update(0)], 19: [lambda: gla_update(1)], 20: [lambda: gla_update(2)],
                22: [lambda: gla_out(0)], 23: [lambda: gla_out(1)],
            }
            for b in range(len(C_IN)):
                for i in range(BLK):
                    tile_of(B_CIN + b, T_CIN + BLK * b, i)
                    for step in between.get(BLK * b + i, ()):
                        step()
            transposes(7, lambda t, c: proj[:, t, c * P:(c + 1) * P])
            pe.wait_ge(hTlo_done, 32)
            for h in range(2):
                for i in range(BLK):
                    tile_of(B_COUT + h, T_COUT + BLK * h, i)
            transposes(8, lambda t, c: x[:, t, c * P:(c + 1) * P])
            pe.wait_ge(hTlo_done, 36)
            mlp(2, T_MLP2, B_MLP2)


_INS = ['x', 'c', 'w_ada', 'b_ada', 'w_in', 'b_forget', 'q_norm_gain', 'k_norm_gain', 'fox_out_gain', 'ret_out_gain',
        'w_out', 'w_mlp_in', 'w_mlp_out', 'a_w_in_2', 'a_cmp_pos_2', 'a_cmp_w1_2', 'a_cmp_b1_2', 'a_cmp_w2_2',
        'a_pool_w_2', 'a_pool_scale_2', 'a_w_out_2', 'c_w_in_2', 'c_gate_w2_2', 'c_gate_b_2', 'c_norm_g_2',
        'c_w_out_2', 'ln1_g_2', 'ln1_b_2', 'ln2_g_2', 'ln2_b_2', 'mlp_w1_2', 'mlp_w2_2']


def kernel(**inputs):
    import numpy as _np
    import concourse.bacc as _bacc
    from concourse import mybir as _mybir
    from concourse.bass_utils import run_bass_kernel_spmd as _run

    nc = _bacc.Bacc("TRN2", target_bir_lowering=False, num_devices=1)
    arrays, dram = {}, {}
    for name, a in list(((n, inputs[n]) for n in _INS)) + list(constants().items()):
        a = _np.ascontiguousarray(a)
        arrays[f"in_{name}_dram"] = a
        dram[name] = nc.dram_tensor(f"in_{name}_dram", a.shape, _mybir.dt.from_np(a.dtype), kind="ExternalInput").ap()
    out = nc.dram_tensor("out_0_dram", (1, S, D), F32, kind="ExternalOutput").ap()
    block_program(nc, dram, out)
    r = _run(nc, [arrays], core_ids=[0])
    return r.results[0]["out_0_dram"]
```

```python
from contextlib import ExitStack

import concourse.bass as bass
from concourse import mybir

F32 = mybir.dt.float32
F32R = mybir.dt.float32r
BF16 = mybir.dt.bfloat16
ACT = mybir.ActivationFunctionType
ALU = mybir.AluOpType
AX = mybir.AxisListType.X

P = 128
D = 1024
S = 256
NT = S // P
KC = D // P
FF = 4 * D
EPS = 1e-6
LN_EPS = 1e-5
ALPHA = 4.0 ** 0.25
GELU_C = 1.5957691216057308

TW = 1024
RAW = 4
SPL = 6
LEAD = 3
BLK = 4
KPT = 2
FFB = 256
MLP_STEPS = FF // FFB
MLP_TILES = 4 * MLP_STEPS
TURN = 6
TURNS = 2
W_IN = [0, 512, 1024, 1536, 2056, 2568, 3080, 3592]
FF_COL = 2048
A_IN = [(512, 512), (0, 512), (1024, 280), (1304, 512)]
C_IN = [0, 512, 1024, 1536, 2048, 2560]
A16_COL = 3072
T_IN = 0
T_OUT = T_IN + BLK * len(W_IN)
T_MLP0 = T_OUT + 2 * BLK
T_AIN = T_MLP0 + MLP_TILES
T_AOUT = T_AIN + BLK * len(A_IN)
T_MLP1 = T_AOUT + 2 * BLK
T_CIN = T_MLP1 + MLP_TILES
T_COUT = T_CIN + BLK * len(C_IN)
T_MLP2 = T_COUT + 2 * BLK
T_END = T_MLP2 + MLP_TILES
ADA_ORDER = [1, 0, 2, 4, 3, 5]
ADA_FIRST = 2 * KC


def raw_plan():
    seq = [("ada", n) for n in range(ADA_FIRST)]
    n = ADA_FIRST
    for s in range(T_END):
        seq.append(("w", s))
        k = s - T_MLP0
        if (4 <= s < 36 and s % 4 != 3) or k in (2, 3, 4, 5, 56, 57, 58, 59):
            seq.append(("ada", n))
            n += 1
    assert n == 6 * KC
    return seq


RAW_SEQ = raw_plan()
W_AT = [r for r, (kind, n) in enumerate(RAW_SEQ) if kind == "w"]
ADA_AT = [r for r, (kind, n) in enumerate(RAW_SEQ) if kind == "ada"]


def raw_of(s):
    return W_AT[s]


def units(n):
    return 4 * n - (2 if n > 4 else 0)


QUARTERS = {n: [(0, 0), (0, 1), (1, 0), (1, 1)] for n in (0, 2, 3, 5, 6, 8)}
QUARTERS[1] = QUARTERS[7] = [(0, 0), (1, 0), (0, 1), (1, 1)]
QUARTERS[4] = [(0, 0), (1, 0)]


C_ID, C_TRI, C_TRC, C_SUF, C_IND, C_CAU, C_NEG = 0, 128, 384, 512, 640, 642, 770
C_COS, C_SIN, C_M01, C_MNG, C_HM = 898, 1154, 1410, 1440, 1470
C_ALL = 1478
NCMP = 15
HC = 8 * NCMP


def constants():
    import numpy as np
    c = np.zeros((P, C_ALL), np.float32)
    i = np.arange(P)
    s, t = i[:, None], i[None, :]
    same = (s // 64) == (t // 64)
    c[:, C_ID:C_ID + P] = np.eye(P)
    c[:, C_TRI:C_TRI + P] = s <= t
    c[:, C_TRI + P:C_TRI + 2 * P] = 1.0
    c[:, C_TRC:C_TRC + P] = (same & (s <= t)) / 16.0
    c[:, C_SUF:C_SUF + P] = (same & (s > t)) / 16.0
    c[:, C_IND:C_IND + 2] = (i[:, None] // 64 == np.arange(2)) / 16.0
    c[:, C_CAU:C_CAU + P] = same & (s <= t)
    c[:, C_NEG:C_NEG + P] = np.where(s >= t, 0.0, -1e30)
    freq = 10000.0 ** (-np.arange(0, P, 2, dtype=np.float32) / np.float32(P))
    for tile in range(NT):
        ang = (np.arange(P, dtype=np.float32) + P * tile)[:, None] * freq[None].astype(np.float32)
        c[:, C_COS + P * tile:C_COS + P * (tile + 1)] = np.tile(np.cos(ang), 2)
        c[:, C_SIN + P * tile:C_SIN + P * (tile + 1)] = np.concatenate([-np.sin(ang), np.sin(ang)], 1)
        seen = (np.arange(NCMP) * 16 + 31)[None, :] <= (i + P * tile)[:, None]
        c[:, C_M01 + NCMP * tile:C_M01 + NCMP * (tile + 1)] = seen
        c[:, C_MNG + NCMP * tile:C_MNG + NCMP * (tile + 1)] = np.where(seen, 0.0, -1e30)
    c[:, C_HM:C_HM + 8] = i[:, None] // NCMP == np.arange(8)
    decay = np.zeros((P, 4, 384), np.float64)
    q = np.arange(S)
    for h in range(4):
        lg = np.log(1.0 - 2.0 ** (-5.0 - h))
        d0, d1 = q[None, :] - s, t - s
        decay[:, h, 0:S] = np.where(d0 >= 0, np.exp(np.maximum(d0, 0) * lg), 0) * P ** -0.5
        decay[:, h, S:] = np.where(d1 >= 0, np.exp(np.maximum(d1, 0) * lg), 0) * P ** -0.5
    bands = np.zeros((P, 4, 384), np.float64)
    for g, w in enumerate((2, 4, 8, 16)):
        full = np.zeros((S, S))
        for a in range(S):
            full[max(0, a - w + 1):a + 1, a] = 1.0 / min(a + 1, w)
        full -= np.eye(S)
        bands[:, g, 0:S] = full[0:P]
        bands[:, g, S:] = full[P:, P:]
    sel = np.zeros((8, 8, S), np.float32)
    sel[np.arange(8), np.arange(8)] = 1.0
    return {"const_c": c, "decay_c": decay.reshape(P, -1).astype(np.float32),
            "bands_c": bands.reshape(P, -1).astype(np.float32), "sel_c": sel.reshape(8, -1)}


def block_program(nc, dram, out):
    with ExitStack() as ctx:
        def sb(name, shape, dt=F32):
            return ctx.enter_context(nc.sbuf_tensor(name, shape, dt))

        def sem(name):
            return ctx.enter_context(nc.semaphore(name))

        raw = sb("raw", [P, RAW, TW])
        whi = sb("whi", [P, SPL, TW], F32R)
        wlo = sb("wlo", [P, SPL, TW], F32R)
        x = sb("x", [P, NT, D])
        hT_hi = sb("hT_hi", [P, KC, S], F32R)
        hT_lo = sb("hT_lo", [P, KC, S], F32R)
        acc = sb("acc", [P, 6 * D])
        rows = sb("rows", [P, 2, D])
        proj = sb("proj", [P, NT, 3072])
        qT = sb("qT", [P, 2 * D])
        kT = sb("kT", [P, 2 * D])
        uhi = sb("uhi", [P, 2, 512], F32R)
        ulo = sb("ulo", [P, 2, 512], F32R)
        sc = sb("sc", [P, 2, 512])
        pr = sb("pr", [P, 2, 512])
        prT = sb("prT", [P, 2, 512])
        cst = sb("cst", [P, C_ALL])
        tab = sb("tab", [P, 1536])
        identb = sb("identb", [P, P], BF16)
        negb = sb("negb", [P, P], BF16)
        wsm = sb("wsm", [P, KC, 16])
        wsm_hi = sb("wsm_hi", [P, KC, 16], F32R)
        wsm_lo = sb("wsm_lo", [P, KC, 16], F32R)
        cvec = sb("cvec", [P, 4, KC])
        pscale = sb("pscale", [P, 4])
        fgain = sb("fgain", [P, 512])
        rgain = sb("rgain", [P, 512])
        qkgain = sb("qkgain", [64, 3])
        bfor = sb("bfor", [P, 8])
        lf = sb("lf", [P, 6, 16])
        stat = sb("stat", [P, 160])
        rstd = sb("rstd", [P, 160])
        bn = sb("bn", [P, NT, 16])
        nhalf = sb("nhalf", [P, 8])
        nmax = sb("nmax", [P, 2, 4])
        rsum = sb("rsum", [P, NT, 16])
        rinv = sb("rinv", [P, NT, 16])
        nsm = sb("nsm", [64, 200])
        gel = sb("gel", [64, 6, 60])
        cred = sb("cred", [P, 4, 16])
        aT = sb("aT", [16, S])
        dec = sb("dec", [P, 4, 4])

        PJ = ctx.enter_context(nc.psum_tensor("PJ", [P, 4, 512], F32))
        AT = ctx.enter_context(nc.psum_tensor("AT", [P, 4, 512], F32))

        ident = cst[:, C_ID:C_ID + P]

        raw_full = [sem(f"raw_full{i}") for i in range(RAW)]
        hi_done = sem("hi_done")
        raw_done = sem("raw_done")
        w_used = sem("w_used")
        prod_done = sem("prod_done")
        bank_free = [sem("bank_free0"), sem("bank_free1")]
        ld_c, ld_x, ld_cst, ld_row, ld_tab, ld_sel, ld_sm = [sem(n) for n in (
            "ld_c", "ld_x", "ld_cst", "ld_row", "ld_tab", "ld_sel", "ld_sm")]
        acc_zero, ld_bada = sem("acc_zero"), sem("ld_bada")
        exp_c = sem("exp_c")
        cast_done = sem("cast_done")
        mod_mm, mod_row = sem("mod_mm"), sem("mod_row")
        var_ready, rstd_ready = sem("var_ready"), sem("rstd_ready")
        sq_done = sem("sq_done")
        sc_free = sem("sc_free")
        src_ready = sem("src_ready")
        tr_done, hThi_done, hTlo_done = sem("tr_done"), sem("hThi_done"), sem("hTlo_done")
        wsm_hi_done, wsm_done = sem("wsm_hi_done"), sem("wsm_done")
        dseq, aseq = sem("dseq"), sem("aseq")
        gt_ln, gt_min, gt_sig = sem("gt_ln"), sem("gt_min"), sem("gt_sig")
        ff_mm, ff_abs, ff_ln, ff_done, cum_mm, cum_done = [sem(n) for n in (
            "ff_mm", "ff_abs", "ff_ln", "ff_done", "cum_mm", "cum_done")]
        qk_norm, hd_tr, hd_done = sem("qk_norm"), sem("hd_tr"), sem("hd_done")
        at_mm, at_max, at_exp, at_tr, at_trd, at_pv, at_out = [sem(n) for n in (
            "at_mm", "at_max", "at_exp", "at_tr", "at_trd", "at_pv", "at_out")]
        rope_done, rt_tr, rt_done, rs_mm, rp_done, rv_mm = [sem(n) for n in (
            "rope_done", "rt_tr", "rt_done", "rs_mm", "rp_done", "rv_mm")]
        x_upd = sem("x_upd")
        relu_done, uhi_done, ulo_done, usq = [sem(n) for n in (
            "relu_done", "uhi_done", "ulo_done", "usq")]
        gate_exp = sem("gate_exp")
        nt_tr, nt_done, kb_done, c_mm, c_z, c_e, c_gel, c2_mm, c2_done, cs_mm, cs_sub, cs_exp, cs_p = [sem(n) for n in (
            "nt_tr", "nt_done", "kb_done", "c_mm", "c_z", "c_e", "c_gel", "c2_mm", "c2_done", "cs_mm", "cs_sub",
            "cs_exp", "cs_p")]
        ct_tr, ct_done, cv_mm, cv_done, pm_mm, pm_done, py_mm, pl_hi, pl_lo = [sem(n) for n in (
            "ct_tr", "ct_done", "cv_mm", "cv_done", "pm_mm", "pm_done", "py_mm", "pl_hi", "pl_lo")]
        ld_nsa, ld_gla = sem("ld_nsa"), sem("ld_gla")
        a_mm, a_ev, aT_tr, aT_done, z_mm, z_abs, z_ln, loga_done, b_mm, eb_done, kz_done = [sem(n) for n in (
            "a_mm", "a_ev", "aT_tr", "aT_done", "z_mm", "z_abs", "z_ln", "loga_done", "b_mm", "eb_done",
            "kz_done")]
        g_tr, g_trd, ga_mm, ga_done, up_st, st_done, go_mm, gv_done = [sem(n) for n in (
            "g_tr", "g_trd", "ga_mm", "ga_done", "up_st", "st_done", "go_mm", "gv_done")]
        stored = sem("stored")

        def bank(pb, t):
            return PJ[:, 2 * (pb % 2) + t, :]

        B_IN, B_OUT = 0, 8
        B_MLP0, B_AIN = 10, 12
        B_AOUT, B_MLP1, B_CIN = 16, 18, 20
        B_COUT, B_MLP2 = 26, 28
        PROD = {B_OUT: 0, B_MLP0: 1, B_AOUT: 2, B_MLP1: 3, B_COUT: 4, B_MLP2: 5}
        FQ, FK, FV, OG, RV, RG = 0, 512, 1024, 1536, 2048, 2560
        RQ, RK = RG, OG
        VCB, PCT, CSB = 1816, 2328, 2584
        RT_, GVR = 1816, 2840
        N_U = 1304
        N_GT = 1280
        KB, POOLW = 4096, 5056
        LOGA, ST, GB, NG, GW2 = 0, 1024, 4096, 4608, 4864
        S_N1, S_FQ, S_FK, S_FO, S_RO, S_N2, S_LN, S_GO = 0, 2, 18, 34, 50, 58, 62, 70
        GRP = [(0, [0, 1, 2, 3]), (0, [4, 5, 6, 7]), (1, [0, 1]), (1, [2, 3]), (1, [4, 5]), (1, [6, 7])]
        GROUPS = [(br, t, heads) for br in (0, 0, 1) for t, heads in GRP]
        NF = len(GRP)
        S_BANK = [0, 1, 0, 1, 0, 1] + [1] * 6 + [0, 1, 0, 1, 0, 1]
        PV_DONE = {(0, 0, 0): 2, (0, 0, 1): 6, (1, 0, 0): 8, (1, 0, 1): 12, (1, 1, 0): 14, (1, 1, 1): 18}

        def rows_of(t):
            return slice(t * P, (t + 1) * P)

        def tr_bank(n, t, j):
            if n == 0:
                return (PJ[:, 2, :], PJ[:, 3, :], AT[:, 0, :], AT[:, 1, :])[2 * t + j]
            if n == 1:
                return AT[:, 2 + t, :]
            if n in (4, 7):
                return AT[:, 2 * j + t, :]
            return AT[:, 2 * t + j, :]

        u4 = lambda a: a[:, :, :].rearrange("p a (b s) -> p (a b) s", b=2)

        def split_dst(n, j):
            if n in (1, 7) and j == 0:
                return u4(uhi), u4(ulo)
            return hT_hi[:, 4 * j:4 * j + 4, :], hT_lo[:, 4 * j:4 * j + 4, :]

        def in_hT(n, j):
            return not (n in (1, 7) and j == 0)

        T_LAST = {1: T_OUT, 4: T_AOUT, 7: T_COUT}

        GLA_E = [(sc[:, 0, :], sc[:, 1, :], pr[:, 0, :]), (prT[:, 0, :], prT[:, 1, :], pr[:, 1, :])]

        raw_slot = lambda r: raw[:, r % RAW, :]
        block = ctx.enter_context(nc.Block())

        @block.sync
        def _(sp):
            def fetch(r, src, view=None):
                if r >= RAW:
                    sp.wait_ge(raw_done, r - RAW + 1)
                dst = raw_slot(r)
                sp.dma_start(dst if view is None else view(dst), src).then_inc(raw_full[r % RAW], 16)

            def fetch_w(s, src, view=None):
                fetch(raw_of(s), src, view)
                r = raw_of(s) + 1
                while r < len(RAW_SEQ) and RAW_SEQ[r][0] == "ada":
                    fetch_ada(r)
                    r += 1

            def fetch_ada(r):
                n = RAW_SEQ[r][1]
                col = ADA_ORDER[n // KC] * D
                k = n % KC
                fetch(r, dram["w_ada"][0, k * P:(k + 1) * P, col:col + D])

            def proj_tile(w, row, col, n=512):
                src = w[row:row + KPT * P, col:col + n].rearrange("(k p) n -> p k n", p=P)
                return src, lambda d: d.rearrange("p (k n) -> p k n", k=KPT)[:, :, 0:n]

            def fetch_block(w, s0, col, n=512):
                for i in range(BLK):
                    fetch_w(s0 + i, *proj_tile(w, i * KPT * P, col, n))

            def fetch_out(w, s0, row0):
                q = 0
                for half in range(2):
                    for h in range(2):
                        for i in range(2):
                            fetch_w(s0 + q, *proj_tile(w, (row0 + 512 * half) % D + i * KPT * P, 512 * h))
                            q += 1

            w1_view = lambda d: d.rearrange("p (k n) -> p k n", k=4)

            def fetch_mlp(w1, w2, s0):
                at = lambda v, n: bass.ds(v, n) if not isinstance(v, int) else slice(v, v + n)

                def up(j, half):
                    src = w1[half * 512:(half + 1) * 512, at(j * FFB, FFB)]
                    return src.rearrange("(k p) n -> p k n", p=P), w1_view

                def down(j, f):
                    return w2[at(j * FFB + f * P, P), :], None

                def steps(m):
                    return [down(m + 1, 0), down(m + 1, 1), up(m + 3, 0), up(m + 3, 1)]

                for k, f in enumerate([up(0, 0), up(0, 1), up(1, 0), up(1, 1), down(0, 0), down(0, 1), up(2, 0), up(2, 1)]):
                    fetch_w(s0 + k, *f)
                with sp.Fori(0, TURNS) as i:
                    for q in range(TURN):
                        for k, (src, view) in enumerate(steps(i * TURN + q)):
                            r = raw_of(s0 + 8 + 4 * q + k)
                            sp.wait_ge(raw_done, i * (4 * TURN) + (r - RAW + 1))
                            dst = raw_slot(r)
                            sp.dma_start(dst if view is None else view(dst), src).then_inc(raw_full[r % RAW], 16)
                for k, f in enumerate([down(13, 0), down(13, 1), up(15, 0), up(15, 1),
                                       down(14, 0), down(14, 1), down(15, 0), down(15, 1)]):
                    fetch_w(s0 + MLP_TILES - 8 + k, *f)

            for r in range(ADA_FIRST):
                fetch_ada(r)
            for b, col in enumerate(W_IN):
                fetch_block(dram["w_in"][0], T_IN + BLK * b, col)
            fetch_out(dram["w_out"][0], T_OUT, 0)
            fetch_mlp(dram["w_mlp_in"][0], dram["w_mlp_out"][0], T_MLP0)
            for b, (col, n) in enumerate(A_IN):
                fetch_block(dram["a_w_in_2"][0], T_AIN + BLK * b, col, n)
            fetch_out(dram["a_w_out_2"][0], T_AOUT, 512)
            fetch_mlp(dram["mlp_w1_2"][0], dram["mlp_w2_2"][0], T_MLP1)
            for b, col in enumerate(C_IN):
                fetch_block(dram["c_w_in_2"][0], T_CIN + BLK * b, col)
            fetch_out(dram["c_w_out_2"][0], T_COUT, 0)
            fetch_mlp(dram["mlp_w1_2"][1], dram["mlp_w2_2"][1], T_MLP2)
            for t in range(NT):
                for j in range(2):
                    sp.wait_ge(src_ready, units(9) + 2 * t + j + 1)
                    sp.dma_start(out[0, rows_of(t), 512 * j:512 * (j + 1)],
                                 x[:, t, 512 * j:512 * (j + 1)]).then_inc(stored, 16)
            sp.wait_ge(stored, 16 * 2 * NT)

        @block.gpsimd
        def _(pool):
            asked = [0]

            def rsqrt(col, n):
                asked[0] += 1
                pool.wait_ge(var_ready, asked[0])
                nc.gpsimd.tensor_tensor(rstd[:, col:col + n], stat[:, col:col + n], nhalf[:, 0:n],
                                        ALU.pow).then_inc(rstd_ready, 1)

            def bcast(dst, src):
                return pool.dma_start(dst, src.unsqueeze(0).broadcast_to([P, src.shape[0]]))

            nc.gpsimd.memset(acc[:, :], 0.0).then_inc(acc_zero, 1)
            nc.gpsimd.memset(nhalf[:, :], -0.5).then_inc(acc_zero, 1)
            pool.wait_ge(acc_zero, 2)
            pool.dma_start(acc[0:1, :], dram["b_ada"]).then_inc(ld_bada, 16)
            rsqrt(S_N1, 1)
            rsqrt(S_N1 + 1, 1)
            pool.wait_ge(rstd_ready, 2)
            nc.gpsimd.memset(kT[64:P, :], 0.0).then_inc(acc_zero, 1)
            pool.wait_ge(tr_done, units(1))
            pool.wait_ge(acc_zero, 3)
            nc.gpsimd.memset(qT[64:P, :], 0.0).then_inc(acc_zero, 1)
            pool.wait_ge(acc_zero, 4)
            pool.dma_start(qT[64:72, :], dram["sel_c"]).then_inc(ld_sel, 16)
            pool.dma_start(kT[96:104, :], dram["sel_c"]).then_inc(ld_sel, 16)
            for c in (S_FQ, S_FK):
                rsqrt(c, 8)
                rsqrt(c + 8, 8)
            for t in range(NT):
                rsqrt(S_FO + 8 * t, 8)
            for t in range(NT):
                rsqrt(S_RO + 4 * t, 4)
            pool.wait_ge(rp_done, 4)
            pool.dma_start(tab[:, :], dram["bands_c"]).then_inc(ld_tab, 16)

            def load_ln(n):
                g, b = (("ln1_g_2", "ln1_b_2"), ("ln2_g_2", "ln2_b_2"))[n % 2]
                bcast(rows[:, 0, :], dram[g][n // 2]).then_inc(ld_row, 16)
                bcast(rows[:, 1, :], dram[b][n // 2]).then_inc(ld_row, 16)

            load_ln(0)
            rsqrt(S_N2, 1)
            rsqrt(S_N2 + 1, 1)
            pool.wait_ge(src_ready, units(4))
            pool.dma_start(acc[0:64, 0:4096].rearrange("d (i j e) -> d i j e", i=2, j=32),
                           dram["a_cmp_w1_2"][0].rearrange("i (j d) e -> d i j e", d=64)).then_inc(ld_nsa, 16)
            pool.dma_start(acc[:, POOLW:POOLW + 512].rearrange("c (g d) -> c g d", g=4),
                           dram["a_pool_w_2"][0].rearrange("g c d -> c g d")).then_inc(ld_nsa, 16)
            for t in range(NT):
                rsqrt(S_LN + t, 1)
            pool.wait_ge(pl_lo, 4)
            pool.wait_ge(src_ready, units(5))
            bcast(acc[:, GB:GB + 512], dram["c_gate_b_2"][0]).then_inc(ld_gla, 16)
            bcast(acc[:, NG:NG + 256], dram["c_norm_g_2"][0]).then_inc(ld_gla, 16)
            pool.dma_start(acc[0:16, GW2:GW2 + 512], dram["c_gate_w2_2"][0]).then_inc(ld_gla, 16)
            pool.wait_ge(wsm_done, 1)
            pool.wait_ge(ff_mm, 1)
            pool.dma_start(wsm[:, :, :], dram["c_w_in_2"][0][:, A16_COL:A16_COL + 16].rearrange(
                "(k p) n -> p k n", p=P)).then_inc(ld_gla, 16)
            pool.wait_ge(src_ready, units(6))
            load_ln(1)
            for t in range(NT):
                rsqrt(S_LN + 2 + t, 1)
            pool.wait_ge(src_ready, units(7))
            load_ln(2)
            for t in range(NT):
                rsqrt(S_GO + 4 * t, 4)
            for t in range(NT):
                rsqrt(S_LN + 4 + t, 1)
            pool.wait_ge(src_ready, units(9))
            load_ln(3)
            for t in range(NT):
                rsqrt(S_LN + 6 + t, 1)

        @block.scalar
        def _(act):
            order = [0]

            def link(ins):
                order[0] += 1
                ins.then_inc(aseq, 1)
                act.wait_ge(aseq, order[0])

            nxt = [0]

            def hi_to(s1):
                while nxt[0] <= s1:
                    s = nxt[0]
                    r = raw_of(s)
                    act.wait_ge(raw_full[r % RAW], 16 * (r // RAW + 1))
                    if s >= SPL:
                        act.wait_ge(w_used, s - SPL + 1)
                    nc.scalar.activation(whi[:, s % SPL, :], raw_slot(r), ACT.Copy).then_inc(hi_done, 1)
                    nxt[0] += 1

            def tiles(s0, s1, after):
                for s in range(s0, s1):
                    hi_to(s + LEAD)
                    for step in after.get(s - s0, ()):
                        step()

            def quarter_hi(n, q):
                t, j = QUARTERS[n][q]
                act.wait_ge(tr_done, units(n) + q + 1)
                if n in T_LAST and in_hT(n, j):
                    act.wait_ge(w_used, T_LAST[n])
                nc.scalar.activation(split_dst(n, j)[0][:, :, rows_of(t)],
                                     tr_bank(n, t, j).rearrange("p (c s) -> p c s", c=4),
                                     ACT.Copy).then_inc(hThi_done, 1)

            def mod_row_out(n):
                for j in range(2):
                    act.wait_ge(mod_mm, 2 * n + 2)
                    i = ADA_ORDER[n]
                    nc.scalar.activation(acc[:, i * D + 512 * j:i * D + 512 * (j + 1)],
                                         AT[:, (0, 2, 0, 0, 0, 2)[n] + j, :], ACT.Copy).then_inc(mod_row, 1)

            def gate_ln(z, e):
                link(nc.scalar.activation(e, z, ACT.Abs))
                link(nc.scalar.activation(e, e, ACT.Exp, scale=-1.0))
                nc.scalar.activation(e, e, ACT.Ln, bias=1.0).then_inc(gt_ln, 1)

            def gate_sig(k, e):
                act.wait_ge(gt_min, k + 1)
                nc.scalar.activation(e, e, ACT.Exp).then_inc(gt_sig, 1)

            def mlp(m, s0):
                j0 = m * MLP_STEPS

                def hi(k, i):
                    s, r = s0 + k, raw_of(s0 + k)
                    act.wait_ge(raw_full[r % RAW], i * (4 * TURN // RAW * 16) + 16 * (r // RAW + 1))
                    act.wait_ge(w_used, i * (4 * TURN) + (s - SPL + 1))
                    nc.scalar.activation(whi[:, s % SPL, :], raw_slot(r), ACT.Copy).then_inc(hi_done, 1)

                def relu(j, i=None):
                    n = j0 + j
                    at = lambda v, d: v if i is None else i * d + v
                    used = s0 + (2 + 2 * j if j < 2 else 4 * j)
                    act.wait_ge(w_used, at(used, 4 * TURN))
                    if n >= 1:
                        act.wait_ge(usq, at(n, TURN))
                        act.wait_ge(uhi_done, at(n, TURN))
                    nc.scalar.activation(pr[:, 0, :], AT[:, j % 2, :], ACT.Relu).then_inc(relu_done, 1)
                    act.wait_ge(relu_done, at(n + 1, TURN))
                    nc.scalar.activation(uhi[:, j % 2, :], pr[:, 0, :], ACT.Square).then_inc(uhi_done, 1)

                hi_to(s0 + 5)
                relu(0)
                hi_to(s0 + 7)
                relu(1)
                with act.Fori(0, TURNS) as i:
                    for q in range(TURN):
                        for k in range(4):
                            hi(8 + 4 * q + k, i)
                        relu(2 + q, i)
                nxt[0] = s0 + MLP_TILES - 8
                hi_to(s0 + MLP_TILES - 5)
                relu(MLP_STEPS - 2)
                hi_to(s0 + MLP_TILES - 1)
                relu(MLP_STEPS - 1)

            act.dma_start(cvec[:, 0, :], dram["c"].rearrange("a (k p) -> p (a k)", p=P),
                          allow_slow_non_contiguous=True).then_inc(ld_c, 16)
            for t in range(NT):
                act.dma_start(x[:, t, :], dram["x"][0, rows_of(t), :]).then_inc(ld_x, 16)
            act.dma_start(cst[:, 0:C_COS], dram["const_c"][:, 0:C_COS]).then_inc(ld_cst, 16)
            act.wait_ge(ld_c, 16)
            nc.scalar.activation(cvec[:, 1, :], cvec[:, 0, :], ACT.Exp, scale=-1.0).then_inc(exp_c, 1)
            act.wait_ge(ld_x, 16 * NT)
            for t in range(NT):
                nc.scalar.activation(kT[:, t * D:(t + 1) * D], x[:, t, :], ACT.Square,
                                     accum_out=stat[:, S_N1 + t:S_N1 + t + 1]).then_inc(sq_done, 1)
            act.wait_ge(ld_cst, 16)
            nc.scalar.activation(identb[:, :], ident, ACT.Copy).then_inc(cast_done, 1)
            nc.scalar.activation(negb[:, :], cst[:, C_NEG:C_NEG + P], ACT.Copy).then_inc(cast_done, 1)
            act.wait_ge(raw_done, ADA_FIRST - 4)
            act.dma_start(wsm[:, :, 0:8], dram["w_in"][0][:, FF_COL:FF_COL + 8].rearrange(
                "(k p) n -> p k n", p=P)).then_inc(ld_sm, 16)
            act.dma_start(bfor[:, :], dram["b_forget"].broadcast_to([P, 8])).then_inc(ld_sm, 16)
            act.dma_start(qkgain[:, 0:1], dram["q_norm_gain"].rearrange("a d -> d a"),
                          allow_slow_non_contiguous=True).then_inc(ld_sm, 16)
            act.dma_start(qkgain[:, 1:2], dram["k_norm_gain"].rearrange("a d -> d a"),
                          allow_slow_non_contiguous=True).then_inc(ld_sm, 16)
            hi_to(1)
            for q in range(4):
                quarter_hi(0, q)
                hi_to(3) if q == 1 else None
            act.wait_ge(ld_sm, 64)
            nc.scalar.activation(qkgain[:, 2:3], qkgain[:, 0:1], ACT.Copy, scale=0.125).then_inc(cast_done, 1)
            nc.scalar.activation(wsm_hi[:, :, 0:8], wsm[:, :, 0:8], ACT.Copy).then_inc(wsm_hi_done, 1)
            act.dma_start(cst[:, C_COS:], dram["const_c"][:, C_COS:]).then_inc(ld_cst, 16)
            act.dma_start(fgain[:, :], dram["fox_out_gain"].rearrange("a h d -> a (h d)").broadcast_to(
                [P, 512])).then_inc(ld_sm, 16)
            act.dma_start(rgain[:, :], dram["ret_out_gain"].rearrange("a h d -> a (h d)").broadcast_to(
                [P, 512])).then_inc(ld_sm, 16)
            act.dma_start(tab[:, :], dram["decay_c"]).then_inc(ld_sm, 16)
            act.dma_start(nsm[:, 0:64].rearrange("d (i j) -> d i j", i=2),
                          dram["a_cmp_pos_2"][0].rearrange("i j d -> d i j"), allow_slow_non_contiguous=True).then_inc(ld_sm, 16)
            act.dma_start(nsm[:, 64:66], dram["a_cmp_b1_2"][0].rearrange("i e -> e i"),
                          allow_slow_non_contiguous=True).then_inc(ld_sm, 16)
            act.dma_start(nsm[:, 66:194].rearrange("e (i d) -> e i d", i=2),
                          dram["a_cmp_w2_2"][0].rearrange("i e d -> e i d")).then_inc(ld_sm, 16)
            act.dma_start(pscale[:, :], dram["a_pool_scale_2"].rearrange("a (g d) -> d (a g)", d=P),
                          allow_slow_non_contiguous=True).then_inc(ld_sm, 16)

            def ff_logs():
                act.wait_ge(ff_abs, 1)
                link(nc.scalar.activation(lf[:, 2, :], lf[:, 1, :], ACT.Exp, scale=-1.0))
                nc.scalar.activation(lf[:, 3, :], lf[:, 2, :], ACT.Ln, bias=1.0).then_inc(ff_ln, 1)

            def head_squares(b):
                act.wait_ge(w_used, T_IN + BLK * (b + 1))
                for t in range(NT):
                    if b > 0:
                        act.wait_ge(sc_free, 2 * (b - 1) + t + 1)
                    nc.scalar.activation(sc[:, t, :], bank(b, t), ACT.Square).then_inc(sq_done, 1)

            def minus_cum():
                act.wait_ge(cum_mm, 1)
                act.wait_ge(acc_zero, 3)
                nc.scalar.activation(kT[64:72, :].rearrange("r (h s) -> r h s", h=8),
                                     AT[64:72, 1, 0:S].unsqueeze(1).broadcast_to([8, 8, S]), ACT.Copy,
                                     scale=-1.0).then_inc(cum_done, 1)

            def heads_out(f):
                t, j = (f // 2) % 2, f % 2
                act.wait_ge(hd_tr, f + 1)
                if f == 0:
                    act.wait_ge(cast_done, 3)
                dst = (qT if f < 4 else kT)[0:64, :].rearrange("d (h s) -> d h s", h=8)
                gain = qkgain[:, 2:3] if f < 4 else qkgain[:, 1:2]
                nc.scalar.activation(dst[:, 4 * j:4 * j + 4, rows_of(t)],
                                     AT[0:64, 2 + f % 2, :].rearrange("d (h s) -> d h s", h=4), ACT.Copy,
                                     scale=gain).then_inc(hd_done, 1)

            def block_out(pb, s_end, col, n=512, scale=1.0):
                act.wait_ge(w_used, s_end)
                for t in range(NT):
                    nc.scalar.activation(proj[:, t, col:col + n], bank(pb, t)[:, 0:n], ACT.Copy, scale=scale)\
                        .then_inc(bank_free[pb % 2], 1)

            def exps(n):
                br, t, heads = GROUPS[n]
                act.wait_ge(at_max, n + 1)
                if n >= 2:
                    act.wait_ge(at_tr, n - 1)
                w = 512 // len(heads)
                for u, h in enumerate(heads):
                    ins = nc.scalar.activation(pr[:, n % 2, u * w:(u + 1) * w], AT[:, S_BANK[n], u * w:(u + 1) * w],
                                               ACT.Exp, bias=nmax[:, n % 2, u:u + 1],
                                               accum_out=rsum[:, t, 8 * br + h:8 * br + h + 1])
                ins.then_inc(at_exp, 1)

            def fox_squares(t):
                act.wait_ge(at_out, t + 1)
                act.wait_ge(sc_free, 4 + t)
                nc.scalar.activation(sc[:, 0, :], proj[:, t, FQ:FQ + 512], ACT.Square).then_inc(sq_done, 1)

            def turned_out(f):
                t = f % 2
                act.wait_ge(rt_tr, f + 1)
                nc.scalar.activation(rows[:, f // 2, :].rearrange("d (h s) -> d h s", h=4)[:, :, rows_of(t)],
                                     AT[:, f % 2, :].rearrange("d (h s) -> d h s", h=4),
                                     ACT.Copy).then_inc(rt_done, 1)

            def ret_squares(t):
                act.wait_ge(rv_mm, 4)
                act.wait_ge(sc_free, 6 + t)
                nc.scalar.activation(sc[:, 0, :], AT[:, 2 + t, :], ACT.Square).then_inc(sq_done, 1)

            def gates_ln(b, col):
                act.wait_ge(w_used, T_IN + BLK * (b + 1))
                for t in range(NT):
                    gate_ln(bank(b, t), proj[:, t, col:col + 512])

            tiles(T_IN, T_OUT, {
                3: [ff_logs, lambda: head_squares(0)], 5: [minus_cum],
                6: [lambda f=f: heads_out(f) for f in range(4)],
                7: [lambda: head_squares(1)],
                10: [lambda f=f: heads_out(f) for f in range(4, 8)],
                11: [lambda: block_out(2, T_IN + 12, FV), lambda: exps(0)],
                12: [lambda: exps(1)], 13: [lambda: exps(2)], 14: [lambda: exps(3), lambda: fox_squares(0)],
                15: [lambda: exps(4), lambda: gates_ln(3, OG)], 16: [lambda: exps(5)],
                17: [lambda: gate_sig(0, proj[:, 0, OG:OG + 512]), lambda: gate_sig(1, proj[:, 1, OG:OG + 512])],
                18: [lambda: fox_squares(1)],
                21: [lambda: turned_out(0), lambda: turned_out(1)],
                22: [lambda: quarter_hi(1, 0), lambda: quarter_hi(1, 1), lambda: mod_row_out(2)],
                25: [lambda: turned_out(2), lambda: turned_out(3)],
                27: [lambda: block_out(6, T_IN + 28, RV)],
                28: [lambda: ret_squares(0), lambda: ret_squares(1)],
                30: [lambda: mod_row_out(3)],
                31: [lambda: gates_ln(7, RG)],
            })
            tiles(T_OUT, T_OUT + 4, {
                0: [lambda: gate_sig(2, proj[:, 0, RG:RG + 512]), lambda: gate_sig(3, proj[:, 1, RG:RG + 512])],
                1: [lambda: mod_row_out(4)], 2: [lambda: quarter_hi(1, 2), lambda: quarter_hi(1, 3)],
            })
            hi_to(T_MLP0 + 1)
            for t in range(NT):
                for h in range(2):
                    act.wait_ge(x_upd, 2 * t + h + 1)
                    nc.scalar.activation(kT[:, (2 * t + h) * 512:(2 * t + h + 1) * 512], x[:, t, 512 * h:512 * (h + 1)],
                                         ACT.Square, accum_out=stat[:, S_N2 + 2 * h + t:S_N2 + 2 * h + t + 1])\
                        .then_inc(sq_done, 1)
            for q in range(4):
                quarter_hi(2, q)
            mlp(0, T_MLP0)
            mod_row_out(5)
            hi_to(T_AIN + 1)
            for q in range(4):
                quarter_hi(3, q)
                hi_to(T_AIN + 3) if q == 1 else None

            def nt_out(f, dst):
                act.wait_ge(nt_tr, f + 1)
                b = AT[0:64, 2 if f == 7 else 2 + f % 2, :]
                nc.scalar.activation(dst, b if len(dst.shape) == 2 else b.rearrange("d (h s) -> d h s", h=4),
                                     ACT.Copy).then_inc(nt_done, 1)

            def q_out(f):
                t, j = (f - 3) // 2, (f - 3) % 2
                nt_out(f, qT[0:64, :].rearrange("d (h s) -> d h s", h=8)[:, 4 * j:4 * j + 4, rows_of(t)])

            def hidden_bias():
                act.wait_ge(c_mm, 1)
                act.wait_ge(ld_sm, 16 * 11)
                for i in range(2):
                    ins = nc.scalar.activation(gel[:, 0, 30 * i:30 * i + 30], AT[0:64, 0, 32 * i:32 * i + 30], ACT.Identity,
                                               bias=nsm[:, 64 + i:65 + i])
                ins.then_inc(c_z, 1)

            def gelu_exp():
                act.wait_ge(c_e, 1)
                nc.scalar.activation(gel[:, 3, :], gel[:, 2, :], ACT.Exp, scale=-GELU_C).then_inc(c_gel, 1)

            def branch_gates():
                act.wait_ge(bank_free[0], 2 * ((B_AIN + 2) // 2) + 2)
                nc.scalar.activation(proj[:, :, N_GT:N_GT + 24], proj[:, :, N_GT:N_GT + 24], ACT.Exp,
                                     scale=-1.0).then_inc(gate_exp, 1)

            def cmp_exp():
                act.wait_ge(cs_sub, 1)
                nc.scalar.activation(proj[:, 0, CSB:CSB + 240], proj[:, 0, CSB:CSB + 240], ACT.Exp).then_inc(cs_exp, 1)

            def cmp_out():
                act.wait_ge(ct_tr, 1)
                nc.scalar.activation(proj[0:HC, 0, PCT:PCT + S], AT[0:HC, 0, 0:S], ACT.Copy).then_inc(ct_done, 1)

            def u_out():
                act.wait_ge(w_used, T_AIN + 16)
                for t in range(NT):
                    nc.scalar.activation(proj[:, t, N_U:N_U + 512], bank(B_AIN + 3, t), ACT.Copy).then_inc(bank_free[1], 1)

            def means_out():
                for k in range(2):
                    act.wait_ge(pm_mm, k + 1)
                    nc.scalar.activation(proj[:, 1, RT_ + 512 * k:RT_ + 512 * (k + 1)], PJ[:, k, :],
                                         ACT.Copy).then_inc(pm_done, 1)

            def pooled_hi():
                for g in range(4):
                    act.wait_ge(py_mm, g // 2 + 1)
                    nc.scalar.activation(u4(uhi)[:, g, :], PJ[:, 2 + g // 2, (g % 2) * S:(g % 2 + 1) * S], ACT.Copy,
                                         scale=pscale[:, g:g + 1]).then_inc(pl_hi, 1)

            tiles(T_AIN, T_AOUT, {
                3: [lambda: block_out(B_AIN, T_AIN + 4, 512)],
                4: [lambda f=f: nt_out(f, kT[0:64, f * 512:(f + 1) * 512]) for f in range(2)],
                5: [lambda: nt_out(2, kT[0:64, 1024:1536])],
                7: [lambda: block_out(B_AIN + 1, T_AIN + 8, 0, scale=0.125), hidden_bias],
                8: [gelu_exp] + [lambda f=f: q_out(f) for f in (3, 4)],
                9: [lambda f=f: q_out(f) for f in (5, 6)],
                10: [lambda: exps(6)],
                11: [lambda: exps(7), lambda: block_out(B_AIN + 2, T_AIN + 12, 1024, 280), branch_gates, cmp_exp],
                12: [lambda: exps(8)],
                13: [lambda: nt_out(7, kT[0:64, 1536:2048]), cmp_out],
                14: [lambda: exps(9)],
                15: [lambda: exps(10), u_out, means_out, lambda: exps(11), pooled_hi, lambda: exps(12)],
            })
            tiles(T_AOUT, T_AOUT + 4, {n: [lambda n=n: exps(13 + n)] for n in range(4)})
            exps(17)
            for q in range(2):
                quarter_hi(4, q)
            hi_to(T_MLP1 + 1)
            for q in range(4):
                quarter_hi(5, q)
            mlp(1, T_MLP1)
            act.wait_ge(ld_gla, 64)
            act.wait_ge(ff_mm, 1)
            nc.scalar.activation(wsm_hi[:, :, :], wsm[:, :, :], ACT.Copy).then_inc(wsm_hi_done, 1)
            hi_to(T_CIN + 1)
            for q in range(4):
                quarter_hi(6, q)
                hi_to(T_CIN + 3) if q == 1 else None

            def rank_out():
                act.wait_ge(aT_tr, 1)
                nc.scalar.activation(aT[:, :], AT[0:16, 1, 0:S], ACT.Copy).then_inc(aT_done, 1)

            def gla_ln():
                for t in range(NT):
                    act.wait_ge(z_abs, t + 1)
                    link(nc.scalar.activation(pr[:, t, :], prT[:, t, :], ACT.Exp, scale=-1.0))
                    nc.scalar.activation(prT[:, t, :], pr[:, t, :], ACT.Ln, bias=1.0).then_inc(z_ln, 1)

            def gla_exps(t):
                act.wait_ge(b_mm, t + 1)
                a, b, c = GLA_E[t]
                nc.scalar.activation(a, AT[:, 2 * t, :], ACT.Exp).then_inc(eb_done, 1)
                nc.scalar.activation(b, AT[:, 2 * t, :], ACT.Exp, scale=-1.0).then_inc(eb_done, 1)
                nc.scalar.activation(c, AT[:, 2 * t + 1, :], ACT.Exp).then_inc(eb_done, 1)

            def decays():
                act.wait_ge(b_mm, 3)
                nc.scalar.activation(dec[:, :, :].rearrange("p a b -> p (a b)"), AT[:, 0, 0:16], ACT.Exp)\
                    .then_inc(eb_done, 1)

            def g_out(f):
                act.wait_ge(g_tr, f + 1)
                nc.scalar.activation((qT, kT)[f % 2][:, 0:D].rearrange("d (h s) -> d h s", h=4)[:, :, rows_of(f // 2)],
                                     AT[:, (1, 2, 3, 1)[f], :].rearrange("d (h s) -> d h s", h=4),
                                     ACT.Copy).then_inc(g_trd, 1)

            def gla_squares(t):
                act.wait_ge(go_mm, t + 1)
                if t:
                    act.wait_ge(gv_done, 1)
                for j in range(2):
                    nc.scalar.activation(sc[:, j, :], AT[:, 2 * t + j, :], ACT.Square).then_inc(sq_done, 1)

            r_at = lambda j, t: proj[:, t, 2048 + 512 * j:2048 + 512 * (j + 1)]

            def r_ln(j):
                act.wait_ge(w_used, T_CIN + 20 + 4 * j)
                for t in range(NT):
                    gate_ln(bank(B_CIN + 4 + j, t), r_at(j, t))

            def r_sig(j):
                for t in range(NT):
                    gate_sig(4 + 2 * j + t, r_at(j, t))

            tiles(T_CIN, T_COUT, {
                3: [lambda: block_out(B_CIN, T_CIN + 4, 0, scale=P ** -0.5)], 4: [rank_out],
                5: [gla_ln], 7: [lambda: block_out(B_CIN + 1, T_CIN + 8, 512)],
                8: [lambda: gla_exps(0), lambda: gla_exps(1)], 9: [decays],
                11: [lambda: block_out(B_CIN + 2, T_CIN + 12, 1024)] + [lambda f=f: g_out(f) for f in range(3)],
                12: [lambda: g_out(3)], 15: [lambda: block_out(B_CIN + 3, T_CIN + 16, 1536)],
                19: [lambda: r_ln(0), lambda: gla_squares(0)],
                20: [lambda: gla_squares(1)],
                21: [lambda: r_sig(0)],
                23: [lambda: r_ln(1), lambda: quarter_hi(7, 0), lambda: quarter_hi(7, 1)],
            })
            tiles(T_COUT, T_COUT + 4, {
                0: [lambda: r_sig(1)], 2: [lambda: quarter_hi(7, 2), lambda: quarter_hi(7, 3)],
            })
            hi_to(T_MLP2 + 1)
            for q in range(4):
                quarter_hi(8, q)
            mlp(2, T_MLP2)

        @block.vector
        def _(dve):
            order = [0]

            def link(ins):
                order[0] += 1
                ins.then_inc(dseq, 1)
                dve.wait_ge(dseq, order[0])

            tt, ts, stt = nc.vector.tensor_tensor, nc.vector.tensor_scalar, nc.vector.scalar_tensor_tensor
            ada_at = lambda n: acc[:, ADA_ORDER[n // KC] * D:(ADA_ORDER[n // KC] + 1) * D]
            heads8 = lambda a: a.rearrange("p (h d) -> p h d", h=8)
            wide = lambda a, d: a.unsqueeze(2).broadcast_to([P, a.shape[1], d])

            nxt = [0]

            def lo_to(s1):
                end = W_AT[s1 + 1] if s1 + 1 < T_END else len(RAW_SEQ)
                while nxt[0] < end:
                    r = nxt[0]
                    kind, n = RAW_SEQ[r]
                    if kind == "w":
                        dve.wait_ge(hi_done, n + 1)
                        tt(wlo[:, n % SPL, :], raw_slot(r), whi[:, n % SPL, :].bitcast(F32),
                           ALU.subtract).then_inc(raw_done, 1)
                    else:
                        dve.wait_ge(raw_full[r % RAW], 16 * (r // RAW + 1))
                        if r >= 1:
                            dve.wait_ge(raw_done, r)
                        stt(ada_at(n), raw_slot(r), cvec[:, 3, n % KC:n % KC + 1], ada_at(n), ALU.mult, ALU.add)\
                            .then_inc(raw_done, 1)
                    nxt[0] += 1

            def tiles(s0, s1, after):
                for s in range(s0, s1):
                    lo_to(s + LEAD)
                    for step in after.get(s - s0, ()):
                        step()

            def quarter_lo(n, q):
                t, j = QUARTERS[n][q]
                dve.wait_ge(hThi_done, units(n) + q + 1)
                hi, lo = split_dst(n, j)
                tt(lo[:, :, rows_of(t)], tr_bank(n, t, j).rearrange("p (c s) -> p c s", c=4),
                   hi[:, :, rows_of(t)].bitcast(F32), ALU.subtract).then_inc(hTlo_done, 1)

            asked = [0]

            def rstd_wait():
                asked[0] += 1
                dve.wait_ge(rstd_ready, asked[0])

            def variance(col, n, width, eps=EPS):
                ts(stat[:, col:col + n], stat[:, col:col + n], 1.0 / width, eps, ALU.mult, ALU.add).then_inc(var_ready, 1)

            mod = lambda i: acc[:, i * D:(i + 1) * D]
            half = lambda j: slice(512 * j, 512 * (j + 1))

            def product_wait(pb, t, h, s_end):
                if t == 0:
                    dve.wait_ge(prod_done, 2 * PROD[pb] + h + 1)
                else:
                    dve.wait_ge(w_used, s_end[h])

            def add_gated(pb, t, h, s_end, gate):
                product_wait(pb, t, h, s_end)
                tmp = sc[:, h, :]
                xs = x[:, t, half(h)]
                ins = tt(tmp, bank(pb + h, t), gate[:, half(h)], ALU.mult)
                ins.then_inc(bank_free[(pb + h) % 2], 1)
                dve.wait_ge(bank_free[(pb + h) % 2], 2 * ((pb + h) // 2) + t + 1)
                return tt(xs, xs, tmp, ALU.add)

            def layer_norm(n, pb, t, s_end):
                c = S_LN + 2 * n + t
                for h in range(2):
                    product_wait(pb, t, h, s_end)
                    xs = x[:, t, half(h)]
                    stt(xs, xs, ALPHA, bank(pb + h, t), ALU.mult, ALU.add).then_inc(bank_free[(pb + h) % 2], 1)
                    dve.wait_ge(bank_free[(pb + h) % 2], 2 * ((pb + h) // 2) + t + 1)
                    link(nc.vector.bn_stats(bn[:, t, 6 * h:6 * h + 6], xs))
                link(nc.vector.bn_aggr(bn[:, t, 12:14], bn[:, t, 0:12].rearrange("p (a b) -> p a b", a=2)))
                ts(stat[:, c:c + 1], bn[:, t, 13:14], LN_EPS, None, ALU.add).then_inc(var_ready, 1)
                dve.wait_ge(ld_row, 32 * (n + 1))
                link(stt(x[:, t, :], x[:, t, :], bn[:, t, 12:13], rows[:, 0, :], ALU.subtract, ALU.mult))
                rstd_wait()
                for j in range(2):
                    xs = x[:, t, half(j)]
                    stt(xs, xs, rstd[:, c:c + 1], rows[:, 1, half(j)], ALU.mult, ALU.add).then_inc(src_ready, 1)

            def gate_min(k, z, e):
                dve.wait_ge(gt_ln, k + 1)
                return stt(e, z, 0.0, e, ALU.min, ALU.subtract).then_inc(gt_min, 1)

            def mlp(m, s0):
                j0 = m * MLP_STEPS

                def lo(k, i):
                    s, r = s0 + k, raw_of(s0 + k)
                    dve.wait_ge(hi_done, i * (4 * TURN) + (s + 1))
                    tt(wlo[:, s % SPL, :], raw_slot(r), whi[:, s % SPL, :].bitcast(F32), ALU.subtract)\
                        .then_inc(raw_done, 1)

                def square(j, i=None):
                    n = j0 + j
                    at = lambda v: v if i is None else i * TURN + v
                    dve.wait_ge(relu_done, at(n + 1))
                    if n >= 1:
                        dve.wait_ge(ulo_done, at(n))
                    tt(pr[:, 1, :], pr[:, 0, :], pr[:, 0, :], ALU.mult).then_inc(usq, 1)
                    dve.wait_ge(usq, at(n + 1))
                    dve.wait_ge(uhi_done, at(n + 1))
                    tt(ulo[:, j % 2, :], pr[:, 1, :], uhi[:, j % 2, :].bitcast(F32), ALU.subtract).then_inc(ulo_done, 1)

                lo_to(s0 + 5)
                square(0)
                lo_to(s0 + 7)
                square(1)
                with dve.Fori(0, TURNS) as i:
                    for q in range(TURN):
                        for k in range(4):
                            lo(8 + 4 * q + k, i)
                        square(2 + q, i)
                nxt[0] = raw_of(s0 + MLP_TILES - 8)
                lo_to(s0 + MLP_TILES - 5)
                square(MLP_STEPS - 2)
                lo_to(s0 + MLP_TILES - 1)
                square(MLP_STEPS - 1)

            dve.wait_ge(exp_c, 1)
            link(ts(cvec[:, 1, :], cvec[:, 1, :], 1.0, None, ALU.add))
            link(nc.vector.reciprocal(cvec[:, 2, :], cvec[:, 1, :]))
            link(tt(cvec[:, 3, :], cvec[:, 2, :], cvec[:, 0, :], ALU.mult))
            dve.wait_ge(ld_bada, 16)
            lo_to(-1)
            for t in range(NT):
                dve.wait_ge(sq_done, t + 1)
                variance(S_N1 + t, 1, D)
            dve.wait_ge(mod_mm, 2)
            for t in range(NT):
                for j in range(2):
                    ins = stt(qT[:, t * D + 512 * j:t * D + 512 * (j + 1)], AT[:, j, :], 1.0, x[:, t, half(j)],
                              ALU.add, ALU.mult)
            link(ins)
            dve.wait_ge(mod_mm, 4)

            def shifted(t):
                rstd_wait()
                for j in range(2):
                    h = qT[:, t * D + 512 * j:t * D + 512 * (j + 1)]
                    stt(h, h, rstd[:, S_N1 + t:S_N1 + t + 1], AT[:, 2 + j, :], ALU.mult, ALU.add).then_inc(src_ready, 1)

            shifted(0)
            shifted(1)
            lo_to(0)
            quarter_lo(0, 0)
            quarter_lo(0, 1)
            lo_to(2)
            quarter_lo(0, 2)
            quarter_lo(0, 3)
            dve.wait_ge(wsm_hi_done, 1)
            tt(wsm_lo[:, :, 0:8], wsm[:, :, 0:8], wsm_hi[:, :, 0:8].bitcast(F32), ALU.subtract).then_inc(wsm_done, 1)

            def ff_start():
                dve.wait_ge(ff_mm, 1)
                lf2 = lambda k: lf[:, k, :].rearrange("p (t h) -> p t h", t=NT)
                link(tt(lf2(0), AT[:, 0, 0:16].rearrange("p (t h) -> p t h", t=NT),
                        bfor[:, :].unsqueeze(1).broadcast_to([P, NT, 8]), ALU.add))
                stt(lf[:, 1, :], lf[:, 0, :], -1.0, lf[:, 0, :], ALU.mult, ALU.max).then_inc(ff_abs, 1)

            def ff_end():
                dve.wait_ge(ff_ln, 1)
                stt(lf[:, 4, :], lf[:, 0, :], 0.0, lf[:, 3, :], ALU.min, ALU.subtract).then_inc(ff_done, 1)

            def head_norm(b, col, sq0):
                for t in range(NT):
                    c = col + 8 * t
                    dve.wait_ge(sq_done, sq0 + t + 1)
                    ins = nc.vector.tensor_reduce(stat[:, c:c + 8], heads8(sc[:, t, :]), AX, ALU.add)
                    ins.then_inc(sc_free, 1)
                    dve.wait_ge(sc_free, 2 * b + t + 1)
                    variance(c, 8, 64)
                for t in range(NT):
                    c = col + 8 * t
                    rstd_wait()
                    tt(heads8(proj[:, t, FQ + 512 * b:FQ + 512 * (b + 1)]), heads8(bank(b, t)),
                       wide(rstd[:, c:c + 8], 64), ALU.mult).then_inc(qk_norm, 1)
                    dve.wait_ge(qk_norm, 2 * b + t + 1)
                    dve.nop().then_inc(bank_free[b % 2], 1)

            def cum_rows():
                dve.wait_ge(cum_done, 1)
                dve.wait_ge(ld_sel, 32)
                nc.vector.tensor_copy(qT[96:104, :].rearrange("r (h s) -> r h s", h=8),
                                      AT[96:104, 1, S:2 * S].unsqueeze(1).broadcast_to([8, 8, S])).then_inc(cum_done, 1)

            def maxima(n):
                u = len(GROUPS[n][2])
                dve.wait_ge(at_mm, n + 1)
                if n >= 2:
                    dve.wait_ge(at_exp, n - 1)
                nc.vector.tensor_reduce(nmax[:, n % 2, 0:u], AT[:, S_BANK[n], :].rearrange("p (u k) -> p u k", u=u),
                                        AX, ALU.max, negate=True).then_inc(at_max, 1)

            def probs_out(n):
                dve.wait_ge(at_tr, n + 1)
                if n >= 2:
                    dve.wait_ge(at_pv, n - 1)
                nc.vector.tensor_copy(prT[:, n % 2, :], AT[:, 2, :]).then_inc(at_trd, 1)

            def fox_out(t):
                dve.wait_ge(at_pv, PV_DONE[0, 0, t])
                link(nc.vector.reciprocal(rinv[:, t, 0:8], rsum[:, t, 0:8]))
                dve.wait_ge(hd_tr, 4)
                tt(heads8(proj[:, t, FQ:FQ + 512]), heads8(AT[:, 3, :]), wide(rinv[:, t, 0:8], 64), ALU.mult)\
                    .then_inc(at_out, 1)

            def squares_summed(sq, col, n, width, k):
                dve.wait_ge(sq_done, sq)
                ins = nc.vector.tensor_reduce(stat[:, col:col + n], sc[:, 0, :].rearrange("p (h d) -> p h d", h=n),
                                              AX, ALU.add)
                ins.then_inc(sc_free, 1)
                dve.wait_ge(sc_free, k)
                variance(col, n, width)

            def fox_final(t):
                rstd_wait()
                o = proj[:, t, FQ:FQ + 512]
                link(tt(heads8(o), heads8(o), wide(rstd[:, S_FO + 8 * t:S_FO + 8 * t + 8], 64), ALU.mult))
                dve.wait_ge(ld_sm, 16 * 11)
                link(tt(o, o, fgain[:, :], ALU.mult))
                dve.wait_ge(gt_sig, t + 1)
                tt(o, o, proj[:, t, OG:OG + 512], ALU.mult).then_inc(src_ready, 1)

            def out_gates():
                for t in range(NT):
                    ins = gate_min(t, bank(3, t), proj[:, t, OG:OG + 512])
                    dve.wait_ge(gt_min, t + 1)
                    dve.nop().then_inc(bank_free[1], 1)

            def rotate(b, dst, k):
                dve.wait_ge(w_used, T_IN + BLK * (b + 1))
                dve.wait_ge(ld_cst, 32)
                for t in range(NT):
                    xh = bank(b, t).rearrange("p (h d) -> p h d", h=4)
                    cos = cst[:, C_COS + P * t:C_COS + P * (t + 1)].unsqueeze(1).broadcast_to([P, 4, P])
                    sin = cst[:, C_SIN + P * t:C_SIN + P * (t + 1)].unsqueeze(1).broadcast_to([P, 4, P])
                    a = sc[:, 0, :].rearrange("p (h d) -> p h d", h=4)
                    c = sc[:, 1, :].rearrange("p (h d) -> p h d", h=4)
                    tt(a, xh, cos, ALU.mult)
                    tt(c[:, :, 0:64], xh[:, :, 64:P], sin[:, :, 0:64], ALU.mult)
                    ins = tt(c[:, :, 64:P], xh[:, :, 0:64], sin[:, :, 64:P], ALU.mult)
                    ins.then_inc(bank_free[b % 2], 1)
                    dve.wait_ge(bank_free[b % 2], 2 * (b // 2) + t + 1)
                    link(tt(proj[:, t, dst:dst + 512], sc[:, 0, :], sc[:, 1, :], ALU.add))
                dve.nop().then_inc(rope_done, 1)

            def decayed(h):
                dve.wait_ge(rs_mm, h + 1)
                if h >= 2:
                    dve.wait_ge(rv_mm, h - 1)
                tt(pr[:, h % 2, 0:384], AT[:, h % 2, 0:384], tab[:, 384 * h:384 * (h + 1)], ALU.mult).then_inc(rp_done, 1)

            def ret_norm():
                for t in range(NT):
                    squares_summed(8 + t + 1, S_RO + 4 * t, 4, P, 6 + t + 1)
                dve.wait_ge(hd_tr, 8)
                for t in range(NT):
                    rstd_wait()
                    link(tt(proj[:, t, FK:FK + 512].rearrange("p (h d) -> p h d", h=4),
                            AT[:, 2 + t, :].rearrange("p (h d) -> p h d", h=4),
                            wide(rstd[:, S_RO + 4 * t:S_RO + 4 * t + 4], P), ALU.mult))
                    link(tt(proj[:, t, FK:FK + 512], proj[:, t, FK:FK + 512], rgain[:, :], ALU.mult))

            def ret_gates():
                for t in range(NT):
                    o = proj[:, t, FK:FK + 512]
                    gate_min(2 + t, bank(7, t), proj[:, t, RG:RG + 512])
                    tt(o, o, bank(7, t), ALU.mult).then_inc(bank_free[1], 1)

            def ret_final():
                for t in range(NT):
                    o = proj[:, t, FK:FK + 512]
                    dve.wait_ge(bank_free[1], 2 * 3 + t + 1)
                    dve.wait_ge(gt_sig, 2 + t + 1)
                    tt(o, o, proj[:, t, RG:RG + 512], ALU.mult).then_inc(src_ready, 1)

            tiles(T_IN, T_OUT, {
                3: [ff_start, ff_end, lambda: head_norm(0, S_FQ, 2)], 5: [cum_rows],
                7: [lambda: head_norm(1, S_FK, 4)],
                11: [lambda: maxima(0)], 12: [lambda: probs_out(0), lambda: maxima(1)],
                13: [lambda: probs_out(1), lambda: maxima(2)],
                14: [lambda: fox_out(0), lambda: probs_out(2), lambda: maxima(3),
                     lambda: squares_summed(7, S_FO, 8, 64, 5)],
                15: [lambda: probs_out(3), lambda: maxima(4), out_gates],
                16: [lambda: probs_out(4), lambda: maxima(5), lambda: fox_final(0)],
                17: [lambda: probs_out(5)], 18: [lambda: fox_out(1), lambda: squares_summed(8, S_FO + 8, 8, 64, 6)],
                19: [lambda: rotate(4, RQ, 0)], 20: [lambda: fox_final(1)],
                22: [lambda: quarter_lo(1, 0), lambda: quarter_lo(1, 1)],
                23: [lambda: rotate(5, RK, 1)],
                26: [lambda: decayed(0), lambda: decayed(1)], 27: [lambda: decayed(2), lambda: decayed(3)],
                28: [ret_norm], 31: [ret_gates],
            })
            tiles(T_OUT, T_OUT + 4, {
                0: [ret_final], 2: [lambda: quarter_lo(1, 2), lambda: quarter_lo(1, 3)],
            })
            lo_to(T_MLP0 + 1)
            s_end = (T_OUT + 6, T_OUT + 8)

            def norm2(t):
                for h in range(2):
                    ins = add_gated(B_OUT, t, h, s_end, mod(2))
                    ins.then_inc(x_upd, 1)
                    dve.wait_ge(x_upd, 2 * t + h + 1)
                    dve.wait_ge(mod_row, 4)
                    stt(qT[:, t * D + 512 * h:t * D + 512 * (h + 1)], mod(4)[:, half(h)], 1.0, x[:, t, half(h)],
                        ALU.add, ALU.mult)
                dve.wait_ge(sq_done, 10 + 2 * t + 2)
                c = S_N2 + t
                link(tt(stat[:, c:c + 1], stat[:, c:c + 1], stat[:, c + 2:c + 3], ALU.add))
                variance(c, 1, D)
                rstd_wait()
                dve.wait_ge(mod_row, 6)
                for j in range(2):
                    h = qT[:, t * D + 512 * j:t * D + 512 * (j + 1)]
                    stt(h, h, rstd[:, c:c + 1], mod(3)[:, half(j)], ALU.mult, ALU.add).then_inc(src_ready, 1)

            dve.wait_ge(mod_row, 2)
            norm2(0)
            norm2(1)
            for q in range(4):
                quarter_lo(2, q)
            mlp(0, T_MLP0)
            lo_to(T_AIN + 1)
            dve.wait_ge(mod_row, 8)
            for t in range(NT):
                for h in range(2):
                    add_gated(B_MLP0, t, h, (T_AIN, T_AIN), mod(5)).then_inc(src_ready, 1)
                for j in range(2):
                    quarter_lo(3, 2 * t + j)
                lo_to(T_AIN + 3)

            def block_keys():
                dve.wait_ge(ld_nsa, 32)
                for i in range(2):
                    dve.wait_ge(nt_done, i + 1)
                    src = kT[0:64, i * 512:(i + 1) * 512].rearrange("d (g c j) -> d j g c", g=2, j=16)
                    dst = (acc if i == 0 else qT)[0:64, (KB if i == 0 else 0):(KB if i == 0 else 0) + 960]
                    dst = dst.rearrange("d (b j g c) -> d b j g c", b=2, j=16, g=2)
                    for b in range(2):
                        pos = nsm[:, 32 * i + 16 * b:32 * i + 16 * b + 16]
                        ins = tt(dst[:, b], src[:, :, :, b:b + NCMP],
                                 pos.unsqueeze(2).unsqueeze(3).broadcast_to([64, 16, 2, NCMP]), ALU.add)
                    ins.then_inc(kb_done, 1)

            def gelu_start():
                dve.wait_ge(c_z, 1)
                link(tt(gel[:, 1, :], gel[:, 0, :], gel[:, 0, :], ALU.mult))
                link(ts(gel[:, 1, :], gel[:, 1, :], 0.044715, 1.0, ALU.mult, ALU.add))
                tt(gel[:, 2, :], gel[:, 1, :], gel[:, 0, :], ALU.mult).then_inc(c_e, 1)

            def gelu_end():
                dve.wait_ge(c_gel, 1)
                link(ts(gel[:, 3, :], gel[:, 3, :], 1.0, None, ALU.add))
                link(nc.vector.reciprocal(gel[:, 4, :], gel[:, 3, :]))
                link(tt(gel[:, 5, :], gel[:, 4, :], gel[:, 0, :], ALU.mult))
                nc.vector.tensor_copy(proj[0:64, 1, GVR:GVR + HC].rearrange("e (g a c) -> e g a c", g=2, a=4),
                                      gel[:, 5, 30:60].rearrange("e (g c) -> e g c", g=2).unsqueeze(2).broadcast_to(
                                          [64, 2, 4, NCMP])).then_inc(c_gel, 1)

            def compressed_out():
                dve.wait_ge(c2_mm, 1)
                nc.vector.tensor_copy(gel[:, 0, 0:30], AT[0:64, 0, 64:94]).then_inc(c2_done, 1)
                tt(proj[0:HC, 0, VCB:VCB + 512].rearrange("r (h d) -> r h d", h=8),
                   AT[0:HC, 0, 96:160].unsqueeze(1).broadcast_to([HC, 8, 64]),
                   cst[0:HC, C_HM:C_HM + 8].unsqueeze(2).broadcast_to([HC, 8, 64]), ALU.mult).then_inc(c2_done, 1)

            gate = lambda t, br: proj[:, t, N_GT:N_GT + 24].rearrange("p (h b) -> p h b", b=3)[:, :, br]

            def gates_out():
                dve.wait_ge(gate_exp, 1)
                gt = proj[:, :, N_GT:N_GT + 24]
                link(ts(gt, gt, 1.0, None, ALU.add))
                link(nc.vector.reciprocal(gt, gt))

            csf = proj[:, 0, CSB:CSB + 240]
            cs = csf.rearrange("p (t h c) -> p t h c", t=NT, h=8)
            csr = csf.rearrange("p (r c) -> p r c", c=NCMP)
            m01 = cst[:, C_M01:C_M01 + 30].rearrange("p (t c) -> p t c", t=NT).unsqueeze(2).broadcast_to([P, NT, 8, NCMP])
            mng = cst[:, C_MNG:C_MNG + 30].rearrange("p (t c) -> p t c", t=NT).unsqueeze(2).broadcast_to([P, NT, 8, NCMP])

            def cmp_max():
                dve.wait_ge(cs_mm, 1)
                link(tt(cs, AT[:, 0, 256:496].rearrange("p (t h c) -> p t h c", t=NT, h=8), m01, ALU.mult))
                link(tt(cs, cs, mng, ALU.add))
                link(nc.vector.tensor_reduce(cred[:, 0, :], csr, AX, ALU.max))
                tt(csr, csr, wide(cred[:, 0, :], NCMP), ALU.subtract).then_inc(cs_sub, 1)

            def cmp_probs():
                dve.wait_ge(cs_exp, 1)
                link(tt(cs, cs, m01, ALU.mult))
                link(nc.vector.tensor_reduce(cred[:, 1, :], csr, AX, ALU.add))
                link(ts(cred[:, 1, :], cred[:, 1, :], 1e-30, None, ALU.max))
                link(nc.vector.reciprocal(cred[:, 2, :], cred[:, 1, :]))
                tt(csr, csr, wide(cred[:, 2, :], NCMP), ALU.mult).then_inc(cs_p, 1)

            def cmp_branch(t):
                dve.wait_ge(cv_mm, t + 1)
                tt(heads8(proj[:, t, 0:512]), heads8(AT[:, 0, :]), wide(gate(t, 0), 64), ALU.mult).then_inc(cv_done, 1)
                dve.wait_ge(cv_done, t + 1)

            def branch_out(br, t):
                dve.wait_ge(at_pv, PV_DONE[1, br, t])
                v = rinv[:, t, 8 * br:8 * br + 8]
                link(ts(v, rsum[:, t, 8 * br:8 * br + 8], 1e-30, None, ALU.max))
                link(nc.vector.reciprocal(v, v))
                link(tt(v, v, gate(t, 1 + br), ALU.mult))
                link(tt(heads8(sc[:, 0, :]), heads8(AT[:, 3, :]), wide(v, 64), ALU.mult))
                dve.nop().then_inc(at_out, 1)
                o = proj[:, t, 0:512]
                ins = tt(o, o, sc[:, 0, :], ALU.add)
                if br:
                    ins.then_inc(src_ready, 1)
                else:
                    link(ins)

            def pooled_lo():
                for g in range(4):
                    dve.wait_ge(pl_hi, 2 * (g // 2) + 2)
                    stt(u4(ulo)[:, g, :], PJ[:, 2 + g // 2, (g % 2) * S:(g % 2 + 1) * S], pscale[:, g:g + 1],
                        u4(uhi)[:, g, :].bitcast(F32), ALU.mult, ALU.subtract).then_inc(pl_lo, 1)

            tiles(T_AIN, T_AOUT, {
                5: [block_keys], 7: [gelu_start], 8: [gelu_end], 9: [compressed_out],
                10: [lambda: maxima(6), cmp_max],
                11: [lambda: probs_out(6), lambda: maxima(7), gates_out, cmp_probs],
                12: [lambda: probs_out(7), lambda: maxima(8)],
                13: [lambda: probs_out(8)],
                14: [lambda: maxima(9), lambda: cmp_branch(0), lambda: branch_out(0, 0)],
                15: [lambda: probs_out(9), lambda: maxima(10), lambda: cmp_branch(1), lambda: probs_out(10),
                     lambda: maxima(11), pooled_lo, lambda: maxima(12)],
            })
            tiles(T_AOUT, T_AOUT + 4, {
                0: [lambda: probs_out(11), lambda: maxima(13)],
                1: [lambda: branch_out(0, 1), lambda: probs_out(12), lambda: maxima(14)],
                2: [lambda: probs_out(13), lambda: maxima(15)],
                3: [lambda: branch_out(1, 0), lambda: probs_out(14), lambda: maxima(16)],
            })
            probs_out(15)
            maxima(17)
            probs_out(16)
            probs_out(17)
            branch_out(1, 1)
            quarter_lo(4, 0)
            quarter_lo(4, 1)
            lo_to(T_MLP1 + 1)
            for t in range(NT):
                layer_norm(0, B_AOUT, t, (T_AOUT + 6, T_AOUT + 8))
            for q in range(4):
                quarter_lo(5, q)
            mlp(1, T_MLP1)
            dve.wait_ge(wsm_hi_done, 2)
            tt(wsm_lo[:, :, :], wsm[:, :, :], wsm_hi[:, :, :].bitcast(F32), ALU.subtract).then_inc(wsm_done, 1)
            lo_to(T_CIN + 1)
            for t in range(NT):
                layer_norm(1, B_MLP1, t, (T_CIN, T_CIN))
                quarter_lo(6, 2 * t)
                quarter_lo(6, 2 * t + 1)
                lo_to(T_CIN + 3)

            la = lambda t: acc[:, LOGA + 512 * t:LOGA + 512 * (t + 1)]

            def rank_in():
                dve.wait_ge(a_mm, 1)
                nc.vector.tensor_copy(lf[:, 0:2, :], AT[:, 0, 0:32].rearrange("p (t a) -> p t a", t=NT)).then_inc(a_ev, 1)

            def gla_abs():
                for t in range(NT):
                    dve.wait_ge(z_mm, t + 1)
                    link(tt(la(t), AT[:, 2 + t, :], acc[:, GB:GB + 512], ALU.add))
                    stt(prT[:, t, :], la(t), -1.0, la(t), ALU.mult, ALU.max).then_inc(z_abs, 1)

            def gla_log():
                for t in range(NT):
                    dve.wait_ge(z_ln, t + 1)
                    stt(la(t), la(t), 0.0, prT[:, t, :], ALU.min, ALU.subtract).then_inc(loga_done, 1)

            def gla_qk():
                for t in range(NT):
                    q, k = proj[:, t, 0:512], proj[:, t, 512:1024]
                    a, b, c = GLA_E[t]
                    dve.wait_ge(eb_done, 3 * t + 3)
                    tt(q, q, a, ALU.mult)
                    link(tt(kT[:, D + 512 * t:D + 512 * (t + 1)], k, c, ALU.mult))
                    tt(k, k, b, ALU.mult).then_inc(kz_done, 1)

            def gla_causal():
                for t in range(NT):
                    dve.wait_ge(ga_mm, t + 1)
                    tt(prT[:, t, :].rearrange("p (h s) -> p h s", h=4),
                       AT[:, 2 + t, :].rearrange("p (h s) -> p h s", h=4),
                       cst[:, C_CAU:C_CAU + P].unsqueeze(1).broadcast_to([P, 4, P]), ALU.mult).then_inc(ga_done, 1)

            st = lambda n, h: acc[:, ST + D * n + 256 * h:ST + D * n + 256 * (h + 1)]

            def state(n):
                dve.wait_ge(eb_done, 7)
                for j in range(2):
                    dve.wait_ge(up_st, 2 * n + j + 1)
                    for h in (2 * j, 2 * j + 1):
                        ups = AT[:, j, 256 * (h % 2):256 * (h % 2 + 1)]
                        if n == 0:
                            ins = nc.vector.tensor_copy(st(0, h), ups)
                        else:
                            ins = stt(st(n, h), st(n - 1, h), dec[:, h, n:n + 1], ups, ALU.mult, ALU.add)
                    ins.then_inc(st_done, 1)
                    dve.wait_ge(st_done, 2 * n + j + 1)

            two = lambda a: a.rearrange("p (h d) -> p h d", h=2)

            def gla_norm(t):
                c = S_GO + 4 * t
                dve.wait_ge(sq_done, 14 + 2 * t + 2)
                ins = nc.vector.tensor_reduce(stat[:, c:c + 4], sc[:, :, :].rearrange("p j (h d) -> p (j h) d", h=2),
                                              AX, ALU.add)
                ins.then_inc(gv_done, 1)
                dve.wait_ge(gv_done, t + 1)
                variance(c, 4, 256, LN_EPS)
                rstd_wait()
                for j in range(2):
                    o = proj[:, t, half(j)]
                    link(tt(two(o), two(AT[:, 2 * t + j, :]), wide(rstd[:, c + 2 * j:c + 2 * j + 2], 256), ALU.mult))
                    link(tt(two(o), two(o), acc[:, NG:NG + 256].unsqueeze(1).broadcast_to([P, 2, 256]), ALU.mult))

            r_at = lambda j, t: proj[:, t, 2048 + 512 * j:2048 + 512 * (j + 1)]

            def r_min(j):
                for t in range(NT):
                    gate_min(4 + 2 * j + t, bank(B_CIN + 4 + j, t), r_at(j, t))

            def r_logit(j):
                for t in range(NT):
                    o = proj[:, t, half(j)]
                    tt(o, o, bank(B_CIN + 4 + j, t), ALU.mult).then_inc(bank_free[j], 1)

            def r_final(j):
                for t in range(NT):
                    o = proj[:, t, half(j)]
                    dve.wait_ge(bank_free[j], 2 * ((B_CIN + 4 + j) // 2) + t + 1)
                    dve.wait_ge(gt_sig, 4 + 2 * j + t + 1)
                    tt(o, o, r_at(j, t), ALU.mult).then_inc(src_ready, 1)

            tiles(T_CIN, T_COUT, {
                3: [rank_in], 5: [gla_abs, gla_log], 8: [gla_qk], 13: [gla_causal],
                16: [lambda: state(0)], 17: [lambda: state(1)], 18: [lambda: state(2)],
                19: [lambda: r_min(0), lambda: gla_norm(0)], 20: [lambda: gla_norm(1)],
                21: [lambda: r_logit(0), lambda: r_final(0)],
                23: [lambda: quarter_lo(7, 0), lambda: quarter_lo(7, 1), lambda: r_min(1), lambda: r_logit(1)],
            })
            tiles(T_COUT, T_COUT + 4, {
                0: [lambda: r_final(1)], 2: [lambda: quarter_lo(7, 2), lambda: quarter_lo(7, 3)],
            })
            lo_to(T_MLP2 + 1)
            for t in range(NT):
                layer_norm(2, B_COUT, t, (T_COUT + 6, T_COUT + 8))
            for q in range(4):
                quarter_lo(8, q)
            mlp(2, T_MLP2)
            for t in range(NT):
                layer_norm(3, B_MLP2, t, (T_END, T_END))

        @block.tensor
        def _(pe):
            mm = nc.tensor.matmul

            def transposes(n, q, src, waits=()):
                t, j = QUARTERS[n][q]
                pe.wait_ge(src_ready, units(n) + q + 1)
                for s, v in waits:
                    pe.wait_ge(s, v)
                for c in range(4):
                    ins = nc.tensor.transpose(tr_bank(n, t, j)[:, c * P:(c + 1) * P], src(t, 4 * j + c), ident)
                ins.then_inc(tr_done, 1)

            from_x = lambda t, c: x[:, t, c * P:(c + 1) * P]
            from_q = lambda t, c: qT[:, t * D + c * P:t * D + (c + 1) * P]
            from_proj = lambda t, c: proj[:, t, c * P:(c + 1) * P]

            def three(o, a, b, hi, lo, start, stop):
                mm(o, a, hi, start=start, stop=False)
                mm(o, a, lo, start=False, stop=False)
                return mm(o, b, hi, start=False, stop=stop)

            def tile_part(o, s, t, hi, lo, k0, n=512, start=False, stop=False):
                for kk in range(KPT):
                    w = slice(512 * kk, 512 * kk + n)
                    ins = three(o[:, 0:n], hi[:, k0 + kk, rows_of(t)], lo[:, k0 + kk, rows_of(t)], whi[:, s % SPL, w],
                                wlo[:, s % SPL, w], start and kk == 0, stop and kk == KPT - 1)
                return ins

            def bank_wait(pb, t):
                if pb >= 2:
                    pe.wait_ge(bank_free[pb % 2], 2 * (pb // 2) - 1 + t)

            def tile_of(pb, s0, i, n=512):
                s = s0 + i
                pe.wait_ge(raw_done, raw_of(s) + 1)
                for t in range(NT):
                    if i == 0:
                        bank_wait(pb, t)
                    ins = tile_part(bank(pb, t), s, t, hT_hi, hT_lo, KPT * i, n, i == 0, i == BLK - 1)
                ins.then_inc(w_used, 1)

            def first_block(pb, s0, stage):
                for t in range(NT):
                    bank_wait(pb, t)
                    for i in range(BLK):
                        if i % 2 == 0:
                            pe.wait_ge(hTlo_done, units(stage) + 2 * t + i // 2 + 1)
                        if t == 0:
                            pe.wait_ge(raw_done, raw_of(s0 + i) + 1)
                        ins = tile_part(bank(pb, t), s0 + i, t, hT_hi, hT_lo, KPT * i, 512, i == 0, i == BLK - 1)
                        if t == NT - 1:
                            ins.then_inc(w_used, 1)

            def out_first(pb, s0, q):
                h, i = q // 2, q % 2
                pe.wait_ge(raw_done, raw_of(s0 + q) + 1)
                for t in range(NT):
                    if i == 0:
                        bank_wait(pb + h, t)
                    ins = tile_part(bank(pb + h, t), s0 + q, t, u4(uhi), u4(ulo), KPT * i, start=i == 0)
                ins.then_inc(w_used, 1)

            def out_second(pb, s0, k0, ready):
                for t in range(NT):
                    pe.wait_ge(hTlo_done, ready + t + 1)
                    for q in range(4):
                        h, i = q // 2, q % 2
                        s = s0 + 4 + q
                        if t == 0:
                            pe.wait_ge(raw_done, raw_of(s) + 1)
                        ins = tile_part(bank(pb + h, t), s, t, hT_hi, hT_lo, k0 + KPT * i, stop=i == 1)
                        if t == NT - 1:
                            ins.then_inc(w_used, 1)
                        elif i == 1:
                            ins.then_inc(prod_done, 1)

            def small(n, o, done):
                for t in range(NT):
                    for k in range(KC):
                        ins = three(AT[:, 0, n * t:n * (t + 1)], hT_hi[:, k, rows_of(t)], hT_lo[:, k, rows_of(t)],
                                    wsm_hi[:, k, 0:n], wsm_lo[:, k, 0:n], k == 0, k == KC - 1)
                ins.then_inc(done, 1)

            def mod_bcast(n, bank0):
                pe.wait_ge(raw_done, ADA_AT[KC * n + KC - 1] + 1)
                i = ADA_ORDER[n]
                for j in range(2):
                    ins = mm(AT[:, bank0 + j, :], cst[:, C_TRI + P:C_TRI + 2 * P],
                             acc[:, i * D + 512 * j:i * D + 512 * (j + 1)], start=True, stop=True)
                    ins.then_inc(mod_mm, 1)

            def mlp(m, s0, pb, early=None, spare=None):
                j0 = m * MLP_STEPS

                def up(j, k0, i=None):
                    at = lambda v, d: v if i is None else i * d + v
                    if j0 + j >= 2:
                        pe.wait_ge(relu_done, at(j0 + j - 1, TURN))
                    for half in range(2):
                        s = s0 + k0 + half
                        pe.wait_ge(raw_done, at(raw_of(s) + 1, 4 * TURN))
                        for kk in range(4):
                            k = 4 * half + kk
                            for f in range(2):
                                o = AT[:, j % 2, f * S:(f + 1) * S]
                                c = slice(kk * FFB + f * P, kk * FFB + (f + 1) * P)
                                first = k == 0 and f == 0
                                last = k == KC - 1
                                mm(o, whi[:, s % SPL, c], hT_hi[:, k, :], start=first, stop=False, skip_group_check=True)
                                mm(o, whi[:, s % SPL, c], hT_lo[:, k, :], start=False, stop=False, skip_group_check=True)
                                ins = mm(o, wlo[:, s % SPL, c], hT_hi[:, k, :], start=False, stop=last,
                                         skip_group_check=True)
                        ins.then_inc(w_used, 1)

                def down_part(j, s, f, t, h, first=False, last=False):
                    c = slice(f * S + t * P, f * S + (t + 1) * P)
                    w = slice(512 * h, 512 * (h + 1))
                    return three(bank(pb + h, t), uhi[:, j % 2, c], ulo[:, j % 2, c], whi[:, s % SPL, w],
                                 wlo[:, s % SPL, w], first, last)

                def down(j, k0, i=None, first=False):
                    at = lambda v, d: v if i is None else i * d + v
                    pe.wait_ge(ulo_done, at(j0 + j + 1, TURN))
                    for f in range(2):
                        s = s0 + k0 + f
                        pe.wait_ge(raw_done, at(raw_of(s) + 1, 4 * TURN))
                        for t in range(NT):
                            for h in range(2):
                                if first and f == 0:
                                    bank_wait(pb + h, t)
                                ins = down_part(j, s, f, t, h, first and f == 0)
                        ins.then_inc(w_used, 1)

                up(0, 0)
                up(1, 2)
                down(0, 4, first=True)
                with pe.Fori(0, TURNS) as i:
                    for q in range(TURN):
                        up(2 + q, 6 + 4 * q, i)
                        down(1 + q, 8 + 4 * q, i)
                up(14, 54)
                down(13, 56)
                up(15, 58)
                if spare:
                    spare()
                for t in range(NT):
                    for j, k0 in ((14, 60), (15, 62)):
                        for f in range(2):
                            s = s0 + k0 + f
                            last = j == MLP_STEPS - 1 and f == 1
                            if t == 0:
                                if f == 0:
                                    pe.wait_ge(ulo_done, j0 + j + 1)
                                pe.wait_ge(raw_done, raw_of(s) + 1)
                            elif last and early:
                                early()
                            for h in range(2):
                                ins = down_part(j, s, f, t, h, last=last)
                                if t == 0 and last:
                                    ins.then_inc(prod_done, 1)
                            if t == NT - 1:
                                ins.then_inc(w_used, 1)

            def softmax_scores(n):
                br, t, heads = GROUPS[n]
                fox = n < NF
                before = [g for g in range(0 if fox else NF, n) if S_BANK[g] == S_BANK[n]]
                if before:
                    pe.wait_ge(at_exp, before[-1] + 1)
                kw = P * (t + 1)
                for u, h in enumerate(heads):
                    rows = slice(0, 104) if fox else slice(0, 64)
                    q = qT[rows, h * S + t * P:h * S + (t + 1) * P]
                    k0 = h * S if fox else (1024, 1536)[br] + S * (h // 4)
                    o = AT[:, S_BANK[n], u * kw:(u + 1) * kw]
                    mm(o, q, kT[rows, k0:k0 + kw], start=True, stop=False)
                    ins = mm(o[:, kw - P:kw], identb[:, :], negb[:, :], start=False, stop=True)
                ins.then_inc(at_mm, 1)

            def prob_transposes(n):
                pe.wait_ge(at_exp, n + 1)
                if n >= 1:
                    pe.wait_ge(at_trd, n)
                for c in range(4):
                    ins = nc.tensor.transpose(AT[:, 2, c * P:(c + 1) * P], pr[:, n % 2, c * P:(c + 1) * P], ident)
                ins.then_inc(at_tr, 1)

            def weighted_values(n):
                br, t, heads = GROUPS[n]
                pe.wait_ge(at_trd, n + 1)
                b = 0
                for h in heads:
                    for kt in range(t + 1):
                        v0 = FV + 64 * h if n < NF else (896, 1152)[br] + 64 * (h // 4)
                        ins = mm(AT[:, 3, 64 * h:64 * h + 64], prT[:, n % 2, b * P:(b + 1) * P], proj[:, kt, v0:v0 + 64],
                                 start=kt == 0, stop=kt == t)
                        b += 1
                ins.then_inc(at_pv, 1)

            def mixer(pb, s0, stage, cols, between):
                first_block(pb, s0, stage)
                for b, n in enumerate(cols):
                    for i in range(BLK):
                        if b:
                            tile_of(pb + b, s0 + BLK * b, i, n)
                        if b or i == BLK - 1:
                            for step in between.get(BLK * b + i, ()):
                                step()

            pe.wait_ge(ld_cst, 16)
            mod_bcast(0, 0)
            mod_bcast(1, 2)
            transposes(0, 0, from_q)
            transposes(0, 1, from_q)
            for q in (2, 3):
                transposes(0, q, from_q, [(src_ready, 4)])

            def forget_logits():
                pe.wait_ge(wsm_done, 1)
                small(8, AT, ff_mm)

            def cumulate():
                pe.wait_ge(ff_done, 1)
                for p0, c0 in ((64, 0), (96, S)):
                    mm(AT[p0:p0 + 8, 1, c0:c0 + S], lf[:, 4, 0:8], cst[:, C_TRI:C_TRI + S], start=True, stop=False)
                    ins = mm(AT[p0:p0 + 8, 1, c0 + P:c0 + S], lf[:, 4, 8:16], cst[:, C_TRI:C_TRI + P],
                             start=False, stop=True)
                ins.then_inc(cum_mm, 1)

            def head_transposes(f):
                t, j = (f // 2) % 2, f % 2
                pe.wait_ge(qk_norm, 2 * (f // 4) + t + 1)
                if f >= 2:
                    pe.wait_ge(hd_done, f - 1)
                c0 = FQ if f < 4 else FK
                for a in range(4):
                    h = 4 * j + a
                    ins = nc.tensor.transpose(AT[0:64, 2 + f % 2, a * P:(a + 1) * P],
                                              proj[:, t, c0 + 64 * h:c0 + 64 * (h + 1)], ident)
                ins.then_inc(hd_tr, 1)

            def fox_scores(n):
                if n == 0:
                    pe.wait_ge(hd_done, 8)
                    pe.wait_ge(cum_done, 2)
                    pe.wait_ge(ld_sel, 32)
                    pe.wait_ge(cast_done, 3)
                softmax_scores(n)

            def fox_values(n):
                if n == 0:
                    pe.wait_ge(bank_free[0], 4)
                if n == 2:
                    pe.wait_ge(at_out, 1)
                weighted_values(n)

            def turn(f):
                t = f % 2
                pe.wait_ge(at_exp, NF)
                if f >= 2:
                    pe.wait_ge(mod_row, 2)
                pe.wait_ge(rope_done, f // 2 + 1)
                c0 = RQ if f < 2 else RK
                for h in range(4):
                    ins = nc.tensor.transpose(AT[:, f % 2, h * P:(h + 1) * P], proj[:, t, c0 + h * P:c0 + (h + 1) * P],
                                              ident)
                ins.then_inc(rt_tr, 1)

            def fox_quarters():
                transposes(1, 0, from_proj, [(at_trd, NF)])
                transposes(1, 1, from_proj, [(at_out, 2)])

            def gate_row():
                pe.wait_ge(rt_done, 2)
                mod_bcast(2, 0)

            def ret_scores(h):
                pe.wait_ge(rt_done, 4)
                if h >= 2:
                    pe.wait_ge(rp_done, h - 1)
                q, k = rows[:, 0, h * S:(h + 1) * S], rows[:, 1, h * S:(h + 1) * S]
                mm(AT[:, h % 2, 0:S], k[:, 0:P], q, start=True, stop=True)
                mm(AT[:, h % 2, S:S + P], k[:, P:S], q[:, P:S], start=True, stop=True).then_inc(rs_mm, 1)

            def ret_values(h):
                pe.wait_ge(rp_done, h + 1)
                if h == 0:
                    pe.wait_ge(bank_free[0], 8)
                    pe.wait_ge(hTlo_done, units(1) + 2)
                v = lambda t: proj[:, t, RV + h * P:RV + (h + 1) * P]
                o = slice(h * P, (h + 1) * P)
                mm(AT[:, 2, o], pr[:, h % 2, 0:P], v(0), start=True, stop=True)
                mm(AT[:, 3, o], pr[:, h % 2, P:S], v(0), start=True, stop=False)
                mm(AT[:, 3, o], pr[:, h % 2, S:S + P], v(1), start=False, stop=True).then_inc(rv_mm, 1)

            def scale_row():
                pe.wait_ge(rp_done, 4)
                mod_bcast(3, 0)

            def shift_row():
                pe.wait_ge(mod_row, 4)
                mod_bcast(4, 0)

            S_, T_, V_ = fox_scores, prob_transposes, fox_values
            between = {
                3: [forget_logits], 5: [cumulate],
                6: [lambda f=f: head_transposes(f) for f in range(4)],
                10: [lambda f=f: head_transposes(f) for f in range(4, 8)],
                11: [lambda: S_(0)], 12: [lambda: T_(0), lambda: S_(1)],
                13: [lambda: V_(0), lambda: T_(1), lambda: S_(2)], 14: [lambda: V_(1), lambda: T_(2), lambda: S_(3)],
                15: [lambda: V_(2), lambda: T_(3), lambda: S_(4)], 16: [lambda: V_(3), lambda: T_(4), lambda: S_(5)],
                17: [lambda: V_(4), lambda: T_(5)], 18: [lambda: V_(5)],
                21: [lambda: turn(0), lambda: turn(1)], 22: [fox_quarters, gate_row],
                25: [lambda: turn(2), lambda: turn(3)],
                26: [lambda: ret_scores(0), lambda: ret_scores(1)],
                27: [lambda: ret_values(0), lambda: ret_scores(2), lambda: ret_values(1), lambda: ret_scores(3)],
                28: [lambda: ret_values(2), lambda: ret_values(3)],
                30: [scale_row],
            }

            mixer(B_IN, T_IN, 0, [512] * len(W_IN), between)
            for q in range(4):
                if q == 0:
                    pe.wait_ge(hTlo_done, units(1) + 2)
                out_first(B_OUT, T_OUT, q)
                if q == 1:
                    shift_row()
                if q == 2:
                    for k in (2, 3):
                        transposes(1, k, from_proj)
            out_second(B_OUT, T_OUT, 4, units(1) + 2)
            for q in range(4):
                transposes(2, q, from_q, [(mod_row, 6)])
            pe.wait_ge(hTlo_done, units(3))

            def early3():
                for q in (0, 1):
                    transposes(3, q, from_x)

            def gate_f_row():
                mod_bcast(5, 2)

            mlp(0, T_MLP0, B_MLP0, early3, gate_f_row)
            for q in (2, 3):
                transposes(3, q, from_x, [(mod_row, 8)])

            def nsa_transposes(f):
                if f < 3:
                    pe.wait_ge(bank_free[0], 2 * (B_AIN // 2) + 2)
                    srcs = [proj[:, t, 512 + P * f + 64 * g:512 + P * f + 64 * (g + 1)] for g in range(2) for t in range(NT)]
                elif f < 7:
                    t, j = (f - 3) // 2, (f - 3) % 2
                    pe.wait_ge(bank_free[1], 2 * ((B_AIN + 1) // 2) + 2)
                    if f == 3:
                        pe.wait_ge(c_mm, 1)
                    srcs = [proj[:, t, 64 * (4 * j + a):64 * (4 * j + a + 1)] for a in range(4)]
                else:
                    pe.wait_ge(bank_free[0], 2 * ((B_AIN + 2) // 2) + 2)
                    pe.wait_ge(at_trd, NF + 2)
                    srcs = [proj[:, t, 1024 + 64 * g:1024 + 64 * (g + 1)] for g in range(2) for t in range(NT)]
                if 2 <= f < 7:
                    pe.wait_ge(nt_done, f - 1)
                for c, a in enumerate(srcs):
                    ins = nc.tensor.transpose(AT[0:64, 2 if f == 7 else 2 + f % 2, c * P:(c + 1) * P], a, ident)
                ins.then_inc(nt_tr, 1)

            def compress():
                for i in range(2):
                    pe.wait_ge(kb_done, i + 1)
                    kb = (acc if i == 0 else qT)[0:64, (KB if i == 0 else 0):(KB if i == 0 else 0) + 960]
                    for j in range(32):
                        ins = mm(AT[0:64, 0, 32 * i:32 * i + 30], acc[0:64, 2048 * i + 64 * j:2048 * i + 64 * (j + 1)],
                                 kb[:, 30 * j:30 * (j + 1)], start=j == 0, stop=j == 31)
                ins.then_inc(c_mm, 1)

            def compress2():
                pe.wait_ge(c_gel, 2)
                mm(AT[0:64, 0, 64:94], nsm[:, 66:130], gel[:, 5, 0:30], start=True, stop=True)
                mm(AT[0:HC, 0, 96:160], proj[0:64, 1, GVR:GVR + HC], nsm[:, 130:194], start=True, stop=True)\
                    .then_inc(c2_mm, 1)

            def cmp_scores():
                pe.wait_ge(c2_done, 2)
                pe.wait_ge(nt_done, 7)
                for t in range(NT):
                    for h in range(8):
                        ins = mm(AT[:, 0, 256 + HC * t + NCMP * h:256 + HC * t + NCMP * (h + 1)],
                                 qT[0:64, h * S + t * P:h * S + (t + 1) * P],
                                 gel[:, 0, NCMP * (h // 4):NCMP * (h // 4 + 1)], start=True, stop=True)
                ins.then_inc(cs_mm, 1)

            def cmp_transposes():
                pe.wait_ge(cs_p, 1)
                for t in range(NT):
                    ins = nc.tensor.transpose(AT[0:HC, 0, t * P:(t + 1) * P], proj[:, 0, CSB + HC * t:CSB + HC * (t + 1)],
                                              ident)
                ins.then_inc(ct_tr, 1)

            def cmp_values(t):
                pe.wait_ge(ct_done, 1)
                if t:
                    pe.wait_ge(cv_done, 1)
                mm(AT[:, 0, :], proj[0:HC, 0, PCT + t * P:PCT + (t + 1) * P], proj[0:HC, 0, VCB:VCB + 512],
                   start=True, stop=True).then_inc(cv_mm, 1)

            def nsa_scores(n):
                if n == NF:
                    pe.wait_ge(nt_done, 7)
                if n == 2 * NF:
                    pe.wait_ge(cv_done, 2)
                softmax_scores(n)

            def nsa_probs(n):
                if n == NF + 2:
                    pe.wait_ge(nt_done, 8)
                prob_transposes(n)

            def nsa_values(n):
                starts = (NF, NF + 2, 2 * NF, 2 * NF + 2)
                if n in starts[1:]:
                    pe.wait_ge(at_out, 2 + starts.index(n))
                weighted_values(n)

            def pool_bands():
                pe.wait_ge(bank_free[0], 2 * ((B_AIN + 2) // 2) + 2)
                pe.wait_ge(bank_free[1], 2 * ((B_AIN + 3) // 2) + 2)
                pe.wait_ge(ld_tab, 16)
                for g in range(4):
                    o = PJ[:, g // 2, (g % 2) * S:(g % 2 + 1) * S]
                    u = lambda t: proj[:, t, N_U + P * g:N_U + P * (g + 1)]
                    mm(o, u(0), tab[:, 384 * g:384 * g + S], start=True, stop=False)
                    ins = mm(o[:, P:S], u(1), tab[:, 384 * g + S:384 * (g + 1)], start=False, stop=True)
                    if g % 2:
                        ins.then_inc(pm_mm, 1)

            def pool_mix():
                pe.wait_ge(pm_done, 2)
                for g in range(4):
                    ins = mm(PJ[:, 2 + g // 2, (g % 2) * S:(g % 2 + 1) * S], acc[:, POOLW + P * g:POOLW + P * (g + 1)],
                             proj[:, 1, RT_ + S * g:RT_ + S * (g + 1)], start=True, stop=True)
                    if g % 2:
                        ins.then_inc(py_mm, 1)

            S_, T_, V_ = nsa_scores, nsa_probs, nsa_values
            between = {
                4: [lambda: nsa_transposes(0), lambda: nsa_transposes(1)], 5: [lambda: nsa_transposes(2)],
                7: [compress], 8: [lambda: nsa_transposes(3), lambda: nsa_transposes(4)],
                9: [lambda: nsa_transposes(5), lambda: nsa_transposes(6), compress2],
                10: [lambda: S_(6), cmp_scores],
                11: [lambda: T_(6), lambda: S_(7)],
                12: [lambda: V_(6), lambda: T_(7), lambda: S_(8)],
                13: [lambda: V_(7), lambda: nsa_transposes(7), lambda: T_(8), cmp_transposes],
                14: [lambda: S_(9), lambda: cmp_values(0)],
                15: [lambda: V_(8), lambda: T_(9), lambda: S_(10), lambda: cmp_values(1), pool_bands,
                     lambda: V_(9), lambda: T_(10), lambda: S_(11), pool_mix, lambda: S_(12)],
            }
            mixer(B_AIN, T_AIN, 3, [n for _, n in A_IN], between)
            between = {0: [lambda: V_(10), lambda: T_(11), lambda: S_(13)],
                       1: [lambda: V_(11), lambda: T_(12), lambda: S_(14)],
                       2: [lambda: V_(12), lambda: T_(13), lambda: S_(15)],
                       3: [lambda: V_(13), lambda: T_(14), lambda: S_(16)]}
            for q in range(4):
                if q == 0:
                    pe.wait_ge(pl_lo, 4)
                out_first(B_AOUT, T_AOUT, q)
                for step in between[q]:
                    step()
            V_(14)
            T_(15)
            S_(17)
            V_(15)
            T_(16)
            V_(16)
            T_(17)
            V_(17)
            for q in range(2):
                transposes(4, q, from_proj, [(at_exp, 3 * NF)])
            out_second(B_AOUT, T_AOUT, 0, units(4))
            for q in range(4):
                transposes(5, q, from_x)
            pe.wait_ge(hTlo_done, units(6))

            def early6():
                for q in (0, 1):
                    transposes(6, q, from_x)

            mlp(1, T_MLP1, B_MLP1, early6)

            for q in (2, 3):
                transposes(6, q, from_x)

            def gate_inputs():
                pe.wait_ge(wsm_done, 2)
                small(16, AT, a_mm)

            def gate_rank():
                pe.wait_ge(a_ev, 1)
                for t in range(NT):
                    ins = nc.tensor.transpose(AT[0:16, 1, t * P:(t + 1) * P], lf[:, t, :], ident)
                ins.then_inc(aT_tr, 1)

            def gate_logits():
                pe.wait_ge(aT_done, 1)
                pe.wait_ge(ld_gla, 64)
                for t in range(NT):
                    mm(AT[:, 2 + t, :], aT[:, rows_of(t)], acc[0:16, GW2:GW2 + 512], start=True, stop=True)\
                        .then_inc(z_mm, 1)

            def cumulated():
                for t in range(NT):
                    pe.wait_ge(loga_done, 2)
                    la = acc[:, LOGA + 512 * t:LOGA + 512 * (t + 1)]
                    mm(AT[:, 2 * t, :], cst[:, C_TRC:C_TRC + P], la, start=True, stop=True)
                    mm(AT[:, 2 * t + 1, :], cst[:, C_SUF:C_SUF + P], la, start=True, stop=True).then_inc(b_mm, 1)

            def chunk_decay():
                pe.wait_ge(eb_done, 2)
                for t in range(NT):
                    for h in range(4):
                        ins = mm(AT[:, 0, 4 * h + 2 * t:4 * h + 2 * t + 2],
                                 acc[:, LOGA + 512 * t + P * h:LOGA + 512 * t + P * (h + 1)],
                                 cst[:, C_IND:C_IND + 2], start=True, stop=True)
                ins.then_inc(b_mm, 1)

            def gla_transposes(f):
                t = f // 2
                pe.wait_ge(kz_done, t + 1)
                if f == 0:
                    pe.wait_ge(eb_done, 7)
                if f == 3:
                    pe.wait_ge(g_trd, 1)
                for h in range(4):
                    c0 = 512 * (f % 2) + P * h
                    ins = nc.tensor.transpose(AT[:, (1, 2, 3, 1)[f], h * P:(h + 1) * P], proj[:, t, c0:c0 + P], ident)
                ins.then_inc(g_tr, 1)

            def gla_scores(t):
                pe.wait_ge(g_trd, 4)
                for h in range(4):
                    c = slice(h * S + t * P, h * S + (t + 1) * P)
                    ins = mm(AT[:, (2, 3)[t], h * P:(h + 1) * P], kT[:, c], qT[:, c], start=True, stop=True)
                ins.then_inc(ga_mm, 1)

            def gla_update(n):
                if n == 0:
                    pe.wait_ge(bank_free[0], 2 * ((B_CIN + 2) // 2) + 2)
                    pe.wait_ge(bank_free[1], 2 * ((B_CIN + 3) // 2) + 2)
                t, p0 = n // 2, 64 * (n % 2)
                for j in range(2):
                    if n:
                        pe.wait_ge(st_done, 2 * (n - 1) + j + 1)
                    for h in (2 * j, 2 * j + 1):
                        ins = mm(AT[:, j, 256 * (h % 2):256 * (h % 2 + 1)],
                                 kT[p0:p0 + 64, D + 512 * t + P * h:D + 512 * t + P * (h + 1)],
                                 proj[p0:p0 + 64, t, 1024 + 256 * h:1024 + 256 * (h + 1)], start=True, stop=True)
                    ins.then_inc(up_st, 1)

            def gla_out(t):
                pe.wait_ge(st_done, 6)
                pe.wait_ge(ga_done, 2)
                for h in range(4):
                    o = AT[:, 2 * t + h // 2, 256 * (h % 2):256 * (h % 2 + 1)]
                    ins = mm(o, prT[:, t, h * P:(h + 1) * P], proj[:, t, 1024 + 256 * h:1024 + 256 * (h + 1)],
                             start=True, stop=False, skip_group_check=True)
                    for half in range(2):
                        n = 2 * t + half
                        if n:
                            c0 = h * S + 64 * n
                            ins = mm(o[64 * half:64 * half + 64, :], qT[:, c0:c0 + 64],
                                     acc[:, ST + D * (n - 1) + 256 * h:ST + D * (n - 1) + 256 * (h + 1)],
                                     start=False, stop=True, skip_group_check=True)
                ins.then_inc(go_mm, 1)

            between = {
                3: [gate_inputs], 4: [gate_rank], 5: [gate_logits], 8: [cumulated], 9: [chunk_decay],
                11: [lambda f=f: gla_transposes(f) for f in range(3)], 12: [lambda: gla_transposes(3), lambda: gla_scores(0)],
                13: [lambda: gla_scores(1)],
                16: [lambda: gla_update(0)], 17: [lambda: gla_update(1)], 18: [lambda: gla_update(2)],
                19: [lambda: gla_out(0)], 20: [lambda: gla_out(1)],
                23: [lambda: transposes(7, 0, from_proj), lambda: transposes(7, 1, from_proj)],
            }
            mixer(B_CIN, T_CIN, 6, [512] * len(C_IN), between)
            for q in range(4):
                if q == 0:
                    pe.wait_ge(hTlo_done, units(7) + 2)
                out_first(B_COUT, T_COUT, q)
                if q == 2:
                    for k in (2, 3):
                        transposes(7, k, from_proj)
            out_second(B_COUT, T_COUT, 4, units(7) + 2)
            for q in range(4):
                transposes(8, q, from_x)
            pe.wait_ge(hTlo_done, units(9))
            mlp(2, T_MLP2, B_MLP2)


_INS = ['x', 'c', 'w_ada', 'b_ada', 'w_in', 'b_forget', 'q_norm_gain', 'k_norm_gain', 'fox_out_gain', 'ret_out_gain',
        'w_out', 'w_mlp_in', 'w_mlp_out', 'a_w_in_2', 'a_cmp_pos_2', 'a_cmp_w1_2', 'a_cmp_b1_2', 'a_cmp_w2_2',
        'a_pool_w_2', 'a_pool_scale_2', 'a_w_out_2', 'c_w_in_2', 'c_gate_w2_2', 'c_gate_b_2', 'c_norm_g_2',
        'c_w_out_2', 'ln1_g_2', 'ln1_b_2', 'ln2_g_2', 'ln2_b_2', 'mlp_w1_2', 'mlp_w2_2']


def kernel(**inputs):
    import numpy as _np
    import concourse.bacc as _bacc
    from concourse import mybir as _mybir
    from concourse.bass_utils import run_bass_kernel_spmd as _run

    nc = _bacc.Bacc("TRN2", target_bir_lowering=False, num_devices=1)
    arrays, dram = {}, {}
    for name, a in list(((n, inputs[n]) for n in _INS)) + list(constants().items()):
        a = _np.ascontiguousarray(a)
        arrays[f"in_{name}_dram"] = a
        dram[name] = nc.dram_tensor(f"in_{name}_dram", a.shape, _mybir.dt.from_np(a.dtype), kind="ExternalInput").ap()
    out = nc.dram_tensor("out_0_dram", (1, S, D), F32, kind="ExternalOutput").ap()
    block_program(nc, dram, out)
    r = _run(nc, [arrays], core_ids=[0])
    return r.results[0]["out_0_dram"]
```

```python
from contextlib import ExitStack

import concourse.bass as bass
from concourse import mybir

F32 = mybir.dt.float32
F32R = mybir.dt.float32r
BF16 = mybir.dt.bfloat16
ACT = mybir.ActivationFunctionType
ALU = mybir.AluOpType
AX = mybir.AxisListType.X

P = 128
D = 1024
S = 256
NT = S // P
KC = D // P
FF = 4 * D
EPS = 1e-6
LN_EPS = 1e-5
ALPHA = 4.0 ** 0.25
GELU_C = 1.5957691216057308

TW = 1024
RAW = 6
SPL = 6
LEAD = 3
BLK = 4
KPT = 2
FFB = 256
MLP_STEPS = FF // FFB
MLP_TILES = 4 * MLP_STEPS
TURN = 6
TURNS = 2
W_IN = [0, 512, 1024, 1536, 2056, 2568, 3080, 3592]
FF_COL = 2048
A_IN = [(512, 512), (0, 512), (1024, 280), (1304, 512)]
C_IN = [0, 512, 1024, 1536, 2048, 2560]
A16_COL = 3072
T_IN = 0
T_OUT = T_IN + BLK * len(W_IN)
T_MLP0 = T_OUT + 2 * BLK
T_AIN = T_MLP0 + MLP_TILES
T_AOUT = T_AIN + BLK * len(A_IN)
T_MLP1 = T_AOUT + 2 * BLK
T_CIN = T_MLP1 + MLP_TILES
T_COUT = T_CIN + BLK * len(C_IN)
T_MLP2 = T_COUT + 2 * BLK
T_END = T_MLP2 + MLP_TILES
FIRST = [(0, 0), (0, 1), (1, 0), (1, 1), (0, 2), (0, 3), (1, 2), (1, 3)]
ADA_ORDER = [1, 0, 2, 4, 3, 5]
ADA_FIRST = 2 * KC
ADA_PE = (4, 6, 15)

ADA_AFTER = [8, 9, 10] + list(range(12, 21)) + list(range(24, 36))


def raw_plan():
    seq = [("ada", n) for n in range(KC)] + [("w", s) for s in range(4)] + [("ada", n) for n in range(KC, ADA_FIRST)]
    n = ADA_FIRST
    for s in range(4, T_END):
        seq.append(("w", s))
        k = s - T_MLP0
        if s in ADA_AFTER or k in (2, 3, 4, 5, 56, 57, 58, 59):
            seq.append(("ada", n))
            n += 1
    assert n == 6 * KC
    return seq


RAW_SEQ = raw_plan()
W_AT = [r for r, (kind, n) in enumerate(RAW_SEQ) if kind == "w"]
ADA_AT = [r for r, (kind, n) in enumerate(RAW_SEQ) if kind == "ada"]


def raw_of(s):
    return W_AT[s]


def units(n):
    return 4 * n - (4 if n > 4 else 0)


QUARTERS = {n: [(0, 0), (0, 1), (1, 0), (1, 1)] for n in (2, 3, 5, 6, 8)}
QUARTERS[0] = QUARTERS[1] = QUARTERS[7] = [(0, 0), (1, 0), (0, 1), (1, 1)]


C_ID, C_TRI, C_NEG, C_M01, C_MNG, C_HM = 0, 128, 384, 512, 542, 572
C_MIX = 580
C_COS, C_SIN = C_MIX, C_MIX + 256
C_SBUF = C_MIX + 512
C_TRC, C_SUF, C_IND, C_CAU = C_MIX, C_MIX + 128, C_MIX + 256, C_MIX + 258
C_GLA = 386
C_ALL = C_SBUF + C_GLA
NCMP = 15
HC = 8 * NCMP


def constants():
    import numpy as np
    c = np.zeros((P, C_ALL), np.float32)
    i = np.arange(P)
    s, t = i[:, None], i[None, :]
    same = (s // 64) == (t // 64)
    c[:, C_ID:C_ID + P] = np.eye(P)
    c[:, C_TRI:C_TRI + P] = s <= t
    c[:, C_TRI + P:C_TRI + 2 * P] = 1.0
    g = c[:, C_SBUF - C_MIX:]
    g[:, C_TRC:C_TRC + P] = (same & (s <= t)) / 16.0
    g[:, C_SUF:C_SUF + P] = (same & (s > t)) / 16.0
    g[:, C_IND:C_IND + 2] = (i[:, None] // 64 == np.arange(2)) / 16.0
    g[:, C_CAU:C_CAU + P] = same & (s <= t)
    c[:, C_NEG:C_NEG + P] = np.where(s >= t, 0.0, -1e30)
    freq = 10000.0 ** (-np.arange(0, P, 2, dtype=np.float32) / np.float32(P))
    for tile in range(NT):
        ang = (np.arange(P, dtype=np.float32) + P * tile)[:, None] * freq[None].astype(np.float32)
        c[:, C_COS + P * tile:C_COS + P * (tile + 1)] = np.tile(np.cos(ang), 2)
        c[:, C_SIN + P * tile:C_SIN + P * (tile + 1)] = np.concatenate([-np.sin(ang), np.sin(ang)], 1)
        seen = (np.arange(NCMP) * 16 + 31)[None, :] <= (i + P * tile)[:, None]
        c[:, C_M01 + NCMP * tile:C_M01 + NCMP * (tile + 1)] = seen
        c[:, C_MNG + NCMP * tile:C_MNG + NCMP * (tile + 1)] = np.where(seen, 0.0, -1e30)
    c[:, C_HM:C_HM + 8] = i[:, None] // NCMP == np.arange(8)
    decay = np.zeros((P, 4, S), np.float64)
    q = np.arange(S)
    for h in range(4):
        lg = np.log(1.0 - 2.0 ** (-5.0 - h))
        d0 = q[None, :] - s
        decay[:, h] = np.where(d0 >= 0, np.exp(np.maximum(d0, 0) * lg), 0) * P ** -0.5
    bands = np.zeros((P, 4, 384), np.float64)
    for g, w in enumerate((2, 4, 8, 16)):
        full = np.zeros((S, S))
        for a in range(S):
            full[max(0, a - w + 1):a + 1, a] = 1.0 / min(a + 1, w)
        full -= np.eye(S)
        bands[:, g, 0:S] = full[0:P]
        bands[:, g, S:] = full[P:, P:]
    sel = np.zeros((8, 8, S), np.float32)
    sel[np.arange(8), np.arange(8)] = 1.0
    return {"const_c": c, "decay_c": decay.reshape(P, -1).astype(np.float32),
            "bands_c": bands.reshape(P, -1).astype(np.float32), "sel_c": sel.reshape(8, -1)}


def block_program(nc, dram, out):
    with ExitStack() as ctx:
        def sb(name, shape, dt=F32):
            return ctx.enter_context(nc.sbuf_tensor(name, shape, dt))

        def sem(name):
            return ctx.enter_context(nc.semaphore(name))

        raw = sb("raw", [P, RAW, TW])
        whi = sb("whi", [P, SPL, TW], F32R)
        wlo = sb("wlo", [P, SPL, TW], F32R)
        x = sb("x", [P, NT, D])
        hT_hi = sb("hT_hi", [P, KC, S], F32R)
        hT_lo = sb("hT_lo", [P, KC, S], F32R)
        acc = sb("acc", [P, 6 * D])
        rows = sb("rows", [P, 2, D])
        proj = sb("proj", [P, NT, 3072])
        qT = sb("qT", [P, 2 * D])
        kT = sb("kT", [P, 2 * D])
        uhi = sb("uhi", [P, 2, 512], F32R)
        ulo = sb("ulo", [P, 2, 512], F32R)
        sc = sb("sc", [P, 2, 512])
        pr = sb("pr", [P, 2, 512])
        prT = sb("prT", [P, 2, 512])
        cst = sb("cst", [P, C_SBUF])
        tab = sb("tab", [P, 1536])
        identb = sb("identb", [P, P], BF16)
        negb = sb("negb", [P, P], BF16)
        wsm = sb("wsm", [P, KC, 16])
        wsm_hi = sb("wsm_hi", [P, KC, 16], F32R)
        wsm_lo = sb("wsm_lo", [P, KC, 16], F32R)
        cvec = sb("cvec", [P, 4, KC])
        pscale = sb("pscale", [P, 4])
        fgain = acc[:, 0:512]
        rgain = tab[:, 1024:1536]
        bada = rows[0:1, :, :].rearrange("a b n -> a (b n)")
        cspread = sc[:, :, :].rearrange("p a (b m) -> p (a b) m", b=4)
        qkgain = sb("qkgain", [64, 3])
        bfor = sb("bfor", [P, 8])
        lf = sb("lf", [P, 6, 16])
        stat = sb("stat", [P, 80])
        rstd = sb("rstd", [P, 80])
        bn = sb("bn", [P, NT, 16])
        nhalf = sb("nhalf", [P, 8])
        nmax = sb("nmax", [P, 2, 4])
        rsum = sb("rsum", [P, NT, 16])
        rinv = sb("rinv", [P, NT, 16])
        nsm = sb("nsm", [64, 194])
        gel = sc[0:64, 0, 0:360].rearrange("p (a b) -> p a b", a=6)
        cred = sb("cred", [P, 4, 16])
        aT = sc[0:16, 1, 0:S]
        dec = sb("dec", [P, 4, 4])

        PJ = ctx.enter_context(nc.psum_tensor("PJ", [P, 4, 512], F32))
        AT = ctx.enter_context(nc.psum_tensor("AT", [P, 4, 512], F32))

        ident = cst[:, C_ID:C_ID + P]

        raw_full = [sem(f"raw_full{i}") for i in range(RAW)]
        hi_done = sem("hi_done")
        raw_done = sem("raw_done")
        w_used = sem("w_used")
        half_done = sem("half_done")
        prod_done = sem("prod_done")
        bank_free = [sem("bank_free0"), sem("bank_free1")]
        ld_c, ld_x, ld_cst, ld_row, ld_tab, ld_sel, ld_sm = [sem(n) for n in (
            "ld_c", "ld_x", "ld_cst", "ld_row", "ld_tab", "ld_sel", "ld_sm")]
        acc_zero, ld_bada, ld_bada2 = sem("acc_zero"), sem("ld_bada"), sem("ld_bada2")
        cb_done, ada_mm = sem("cb_done"), sem("ada_mm")
        exp_c = sem("exp_c")
        cast_done = sem("cast_done")
        mod_mm, mod_row = sem("mod_mm"), sem("mod_row")
        var_ready, rstd_ready = sem("var_ready"), sem("rstd_ready")
        sq_done = sem("sq_done")
        sc_free = sem("sc_free")
        src_ready = sem("src_ready")
        tr_done, hThi_done, hTlo_done = sem("tr_done"), sem("hThi_done"), sem("hTlo_done")
        wsm_hi_done, wsm_done = sem("wsm_hi_done"), sem("wsm_done")
        dseq, aseq = sem("dseq"), sem("aseq")
        gt_abs, gt_ln, gt_min, gt_sig = [sem(n) for n in ("gt_abs", "gt_ln", "gt_min", "gt_sig")]
        ff_mm, ff_abs, ff_ln, ff_done, cum_mm, cum_done = [sem(n) for n in (
            "ff_mm", "ff_abs", "ff_ln", "ff_done", "cum_mm", "cum_done")]
        qk_norm, hd_tr, hd_done = sem("qk_norm"), sem("hd_tr"), sem("hd_done")
        at_mm, at_max, at_exp, at_tr, at_trd, at_pv, at_out = [sem(n) for n in (
            "at_mm", "at_max", "at_exp", "at_tr", "at_trd", "at_pv", "at_out")]
        rope_done, rt_tr, rt_done, rs_mm, rp_done, rv_mm = [sem(n) for n in (
            "rope_done", "rt_tr", "rt_done", "rs_mm", "rp_done", "rv_mm")]
        x_upd = sem("x_upd")
        relu_done, uhi_done, ulo_done, usq, up_mm, up_tr = [sem(n) for n in (
            "relu_done", "uhi_done", "ulo_done", "usq", "up_mm", "up_tr")]
        gate_exp = sem("gate_exp")
        nt_tr, nt_done, kb_done, c_mm, c_z, c_e, c_gel, c2_mm, c2_done, cs_mm, cs_sub, cs_exp, cs_p = [sem(n) for n in (
            "nt_tr", "nt_done", "kb_done", "c_mm", "c_z", "c_e", "c_gel", "c2_mm", "c2_done", "cs_mm", "cs_sub",
            "cs_exp", "cs_p")]
        ct_tr, ct_done, cv_mm, pm_mm, pm_done, py_mm, pl_hi, pl_lo, at_w, on_hi, on_lo = [sem(n) for n in (
            "ct_tr", "ct_done", "cv_mm", "pm_mm", "pm_done", "py_mm", "pl_hi", "pl_lo", "at_w", "on_hi", "on_lo")]
        ld_nsa, ld_gla = sem("ld_nsa"), sem("ld_gla")
        a_mm, a_ev, aT_tr, aT_done, z_mm, z_abs, z_ln, loga_done, b_mm, eb_done, kz_done = [sem(n) for n in (
            "a_mm", "a_ev", "aT_tr", "aT_done", "z_mm", "z_abs", "z_ln", "loga_done", "b_mm", "eb_done",
            "kz_done")]
        g_tr, g_trd, ga_mm, ga_done, up_st, st_done, go_mm = [sem(n) for n in (
            "g_tr", "g_trd", "ga_mm", "ga_done", "up_st", "st_done", "go_mm")]
        stored = sem("stored")

        def bank(pb, t):
            return PJ[:, 2 * (pb % 2) + t, :]

        B_IN, B_OUT = 0, 8
        B_MLP0, B_AIN = 10, 12
        B_AOUT, B_MLP1, B_CIN = 16, 18, 20
        B_COUT, B_MLP2 = 26, 28
        PROD = {B_OUT: 0, B_MLP0: 1, B_AOUT: 2, B_MLP1: 3, B_COUT: 4, B_MLP2: 5}
        FQ, FK, FV, OG, RV, RG = 0, 512, 1024, 1536, 2048, 2560
        RQ, RK = RG, FK
        VCB, PCT, CSB = 1816, 2328, 2584
        RT_, GVR = 1816, 2840
        N_U = 1304
        N_GT = 1280
        KB, POOLW = 4096, 5056
        LOGA, ST, GB, NG, GW2 = 0, 1024, 4096, 4608, 4864
        S_N1, S_FQ, S_FK, S_FO, S_RO, S_N2, S_LN, S_GO = 0, 2, 18, 34, 50, 58, 62, 70
        GRP = [(0, [0, 1, 2, 3]), (0, [4, 5, 6, 7]), (1, [0, 1]), (1, [2, 3]), (1, [4, 5]), (1, [6, 7])]
        GROUPS = [(br, t, heads) for br in (0, 0, 1) for t, heads in GRP]
        NF = len(GRP)
        S_BANK = [0, 1, 0, 1, 0, 1] + [1] * 12
        NSA_O = (3, 0)
        PV_DONE = [(2, 6), (14, 18)]

        def rows_of(t):
            return slice(t * P, (t + 1) * P)

        def tr_bank(n, t, j):
            if n == 0:
                return AT[:, 1 + 2 * t, :]
            if n == 1:
                return AT[:, 2 + t, :]
            return AT[:, 2 * t + j, :]

        u4 = lambda a: a[:, :, :].rearrange("p a (b s) -> p (a b) s", b=2)

        def split_dst(n, j):
            if n in (1, 7) and j == 0:
                return u4(uhi), u4(ulo)
            return hT_hi[:, 4 * j:4 * j + 4, :], hT_lo[:, 4 * j:4 * j + 4, :]

        def in_hT(n, j):
            return not (n in (1, 7) and j == 0)

        T_LAST = {1: T_OUT, 7: T_COUT}

        GLA_E = [(sc[:, 0, :], sc[:, 1, :], pr[:, 0, :]), (prT[:, 0, :], prT[:, 1, :], pr[:, 1, :])]

        raw_slot = lambda r: raw[:, r % RAW, :]
        block = ctx.enter_context(nc.Block())

        @block.sync
        def _(sp):
            def fetch(r, src, view=None):
                if r >= RAW:
                    sp.wait_ge(raw_done, r - RAW + 1)
                dst = raw_slot(r)
                sp.dma_start(dst if view is None else view(dst), src).then_inc(raw_full[r % RAW], 16)

            def fetch_w(s, src, view=None):
                fetch(raw_of(s), src, view)
                r = raw_of(s) + 1
                while r < len(RAW_SEQ) and RAW_SEQ[r][0] == "ada":
                    fetch_ada(r)
                    r += 1

            def fetch_ada(r):
                n = RAW_SEQ[r][1]
                rows = slice(n % KC * P, (n % KC + 1) * P)
                if n < ADA_FIRST:
                    fetch(r, dram["w_ada"][0, rows, 0:2 * D].rearrange("p (a b c) -> p a b c", a=2, b=2)[:, :, n // KC, :],
                          lambda d: d.rearrange("p (a c) -> p a c", a=2))
                else:
                    col = ADA_ORDER[n // KC] * D
                    fetch(r, dram["w_ada"][0, rows, col:col + D])

            def proj_tile(w, row, col, n=512):
                src = w[row:row + KPT * P, col:col + n].rearrange("(k p) n -> p k n", p=P)
                return src, lambda d: d.rearrange("p (k n) -> p k n", k=KPT)[:, :, 0:n]

            def fetch_block(w, s0, col, n=512):
                for i in range(BLK):
                    fetch_w(s0 + i, *proj_tile(w, i * KPT * P, col, n))

            def fetch_out(w, s0, row0):
                q = 0
                for half in range(2):
                    for h in range(2):
                        for i in range(2):
                            fetch_w(s0 + q, *proj_tile(w, (row0 + 512 * half) % D + i * KPT * P, 512 * h))
                            q += 1

            w1_view = lambda d: d.rearrange("p (k n) -> p k n", k=4)

            def fetch_mlp(w1, w2, s0):
                at = lambda v, n: bass.ds(v, n) if not isinstance(v, int) else slice(v, v + n)

                def up(j, half):
                    src = w1[half * 512:(half + 1) * 512, at(j * FFB, FFB)]
                    return src.rearrange("(k p) n -> p k n", p=P), w1_view

                def down(j, f):
                    return w2[at(j * FFB + f * P, P), :], None

                def steps(m):
                    return [down(m + 1, 0), down(m + 1, 1), up(m + 3, 0), up(m + 3, 1)]

                for k, f in enumerate([up(0, 0), up(0, 1), up(1, 0), up(1, 1), down(0, 0), down(0, 1), up(2, 0), up(2, 1)]):
                    fetch_w(s0 + k, *f)
                with sp.Fori(0, TURNS) as i:
                    for q in range(TURN):
                        for k, (src, view) in enumerate(steps(i * TURN + q)):
                            r = raw_of(s0 + 8 + 4 * q + k)
                            sp.wait_ge(raw_done, i * (4 * TURN) + (r - RAW + 1))
                            dst = raw_slot(r)
                            sp.dma_start(dst if view is None else view(dst), src).then_inc(raw_full[r % RAW], 16)
                for k, f in enumerate([down(13, 0), down(13, 1), up(15, 0), up(15, 1),
                                       down(14, 0), down(14, 1), down(15, 0), down(15, 1)]):
                    fetch_w(s0 + MLP_TILES - 8 + k, *f)

            for r in range(KC):
                fetch_ada(r)
            for q, (b, i) in enumerate(FIRST):
                fetch_w(T_IN + q, *proj_tile(dram["w_in"][0], i * KPT * P, W_IN[b]))
            for b, col in list(enumerate(W_IN))[2:]:
                fetch_block(dram["w_in"][0], T_IN + BLK * b, col)
            fetch_out(dram["w_out"][0], T_OUT, 0)
            fetch_mlp(dram["w_mlp_in"][0], dram["w_mlp_out"][0], T_MLP0)
            for b, (col, n) in enumerate(A_IN):
                fetch_block(dram["a_w_in_2"][0], T_AIN + BLK * b, col, n)
            fetch_out(dram["a_w_out_2"][0], T_AOUT, 512)
            fetch_mlp(dram["mlp_w1_2"][0], dram["mlp_w2_2"][0], T_MLP1)
            for b, col in enumerate(C_IN):
                fetch_block(dram["c_w_in_2"][0], T_CIN + BLK * b, col)
            fetch_out(dram["c_w_out_2"][0], T_COUT, 0)
            fetch_mlp(dram["mlp_w1_2"][1], dram["mlp_w2_2"][1], T_MLP2)
            for t in range(NT):
                for j in range(2):
                    sp.wait_ge(src_ready, units(9) + 2 * t + j + 1)
                    sp.dma_start(out[0, rows_of(t), 512 * j:512 * (j + 1)],
                                 x[:, t, 512 * j:512 * (j + 1)]).then_inc(stored, 16)
            sp.wait_ge(stored, 16 * 2 * NT)

        @block.gpsimd
        def _(pool):
            asked = [0]

            def rsqrt(col, n):
                asked[0] += 1
                pool.wait_ge(var_ready, asked[0])
                nc.gpsimd.tensor_tensor(rstd[:, col:col + n], stat[:, col:col + n], nhalf[:, 0:n],
                                        ALU.pow).then_inc(rstd_ready, 1)

            def bcast(dst, src):
                return pool.dma_start(dst, src.unsqueeze(0).broadcast_to([P, src.shape[0]]))

            nc.gpsimd.memset(nhalf[:, :], -0.5).then_inc(acc_zero, 1)
            nc.gpsimd.memset(acc[:, 2 * D:], 0.0).then_inc(acc_zero, 1)
            pool.wait_ge(acc_zero, 2)
            pool.dma_start(acc[0:1, 2 * D:], dram["b_ada"][:, 2 * D:]).then_inc(ld_bada2, 16)
            rsqrt(S_N1, 1)
            rsqrt(S_N1 + 1, 1)
            pool.wait_ge(rstd_ready, 2)
            nc.gpsimd.memset(kT[64:P, :], 0.0).then_inc(acc_zero, 1)
            pool.wait_ge(tr_done, units(1))
            pool.wait_ge(acc_zero, 3)
            nc.gpsimd.memset(qT[64:P, :], 0.0).then_inc(acc_zero, 1)
            pool.wait_ge(acc_zero, 4)
            pool.dma_start(qT[64:72, :], dram["sel_c"]).then_inc(ld_sel, 16)
            pool.dma_start(kT[96:104, :], dram["sel_c"]).then_inc(ld_sel, 16)
            for c in (S_FQ, S_FK):
                rsqrt(c, 8)
                rsqrt(c + 8, 8)
            for t in range(NT):
                rsqrt(S_FO + 8 * t, 8)
            for t in range(NT):
                rsqrt(S_RO + 4 * t, 4)
            pool.wait_ge(src_ready, units(2))
            pool.dma_start(tab[:, :], dram["bands_c"]).then_inc(ld_tab, 16)

            def load_ln(n):
                g, b = (("ln1_g_2", "ln1_b_2"), ("ln2_g_2", "ln2_b_2"))[n % 2]
                bcast(rows[:, 0, :], dram[g][n // 2]).then_inc(ld_row, 16)
                bcast(rows[:, 1, :], dram[b][n // 2]).then_inc(ld_row, 16)

            load_ln(0)
            rsqrt(S_N2, 1)
            rsqrt(S_N2 + 1, 1)
            pool.wait_ge(src_ready, units(4))
            pool.dma_start(acc[0:64, 0:4096].rearrange("d (i j e) -> d i j e", i=2, j=32),
                           dram["a_cmp_w1_2"][0].rearrange("i (j d) e -> d i j e", d=64)).then_inc(ld_nsa, 16)
            pool.dma_start(acc[:, POOLW:POOLW + 512].rearrange("c (g d) -> c g d", g=4),
                           dram["a_pool_w_2"][0].rearrange("g c d -> c g d")).then_inc(ld_nsa, 16)
            for t in range(NT):
                rsqrt(S_LN + t, 1)
            pool.wait_ge(pl_lo, 4)
            pool.wait_ge(on_lo, 2)
            bcast(acc[:, GB:GB + 512], dram["c_gate_b_2"][0]).then_inc(ld_gla, 16)
            bcast(acc[:, NG:NG + 256], dram["c_norm_g_2"][0]).then_inc(ld_gla, 16)
            pool.dma_start(acc[0:16, GW2:GW2 + 512], dram["c_gate_w2_2"][0]).then_inc(ld_gla, 16)
            pool.dma_start(cst[:, C_MIX:C_MIX + C_GLA], dram["const_c"][:, C_SBUF:]).then_inc(ld_gla, 16)
            pool.wait_ge(wsm_done, 1)
            pool.wait_ge(ff_mm, 1)
            pool.dma_start(wsm[:, :, :], dram["c_w_in_2"][0][:, A16_COL:A16_COL + 16].rearrange(
                "(k p) n -> p k n", p=P)).then_inc(ld_gla, 16)
            pool.wait_ge(src_ready, units(6))
            load_ln(1)
            for t in range(NT):
                rsqrt(S_LN + 2 + t, 1)
            pool.wait_ge(src_ready, units(7))
            load_ln(2)
            for t in range(NT):
                rsqrt(S_GO + 4 * t, 4)
            for t in range(NT):
                rsqrt(S_LN + 4 + t, 1)
            pool.wait_ge(src_ready, units(9))
            load_ln(3)
            for t in range(NT):
                rsqrt(S_LN + 6 + t, 1)

        @block.scalar
        def _(act):
            order = [0]

            def link(ins):
                order[0] += 1
                ins.then_inc(aseq, 1)
                act.wait_ge(aseq, order[0])

            nxt = [0]

            def hi_to(s1):
                while nxt[0] <= s1:
                    s = nxt[0]
                    r = raw_of(s)
                    act.wait_ge(raw_full[r % RAW], 16 * (r // RAW + 1))
                    if s >= SPL:
                        act.wait_ge(w_used, s - SPL + 1)
                    nc.scalar.activation(whi[:, s % SPL, :], raw_slot(r), ACT.Copy).then_inc(hi_done, 1)
                    nxt[0] += 1

            def tiles(s0, s1, after, first=()):
                for s in range(s0, s1):
                    if s - s0 not in first:
                        hi_to(s + LEAD)
                    for step in after.get(s - s0, ()):
                        step()
                    hi_to(s + LEAD)

            def quarter_hi(n, q):
                t, j = QUARTERS[n][q]
                act.wait_ge(tr_done, units(n) + q + 1)
                if n in T_LAST and in_hT(n, j):
                    act.wait_ge(w_used, T_LAST[n])
                nc.scalar.activation(split_dst(n, j)[0][:, :, rows_of(t)],
                                     tr_bank(n, t, j).rearrange("p (c s) -> p c s", c=4),
                                     ACT.Copy).then_inc(hThi_done, 1)

            def mod_row_out(n):
                for j in range(2):
                    act.wait_ge(mod_mm, 2 * n + 2)
                    i = ADA_ORDER[n]
                    nc.scalar.activation(acc[:, i * D + 512 * j:i * D + 512 * (j + 1)],
                                         AT[:, (0, 2, 0, 0, 0, 2)[n] + j, :], ACT.Copy).then_inc(mod_row, 1)

            gates = [0]

            def gate_ln(zs, es):
                for z, e in zip(zs, es):
                    nc.scalar.activation(e, z, ACT.Abs).then_inc(gt_abs, 1)
                gates[0] += NT
                act.wait_ge(gt_abs, gates[0])
                for e in es:
                    ins = nc.scalar.activation(e, e, ACT.Exp, scale=-1.0)
                link(ins)
                for e in es:
                    nc.scalar.activation(e, e, ACT.Ln, bias=1.0).then_inc(gt_ln, 1)

            def gate_sig(k, e):
                act.wait_ge(gt_min, k + 1)
                nc.scalar.activation(e, e, ACT.Exp).then_inc(gt_sig, 1)

            def mlp(m, s0):
                j0 = m * MLP_STEPS

                def hi(k, i):
                    s, r = s0 + k, raw_of(s0 + k)
                    act.wait_ge(raw_full[r % RAW], i * (4 * TURN // RAW * 16) + 16 * (r // RAW + 1))
                    act.wait_ge(w_used, i * (4 * TURN) + (s - SPL + 1))
                    nc.scalar.activation(whi[:, s % SPL, :], raw_slot(r), ACT.Copy).then_inc(hi_done, 1)

                def relu(j, i=None):
                    n = j0 + j
                    at = lambda v, d: v if i is None else i * d + v
                    used = s0 + (2 + 2 * j if j < 2 else 4 * j)
                    act.wait_ge(w_used, at(used, 4 * TURN))
                    if n >= 1:
                        act.wait_ge(usq, at(n, TURN))
                        act.wait_ge(uhi_done, at(n, TURN))
                    nc.scalar.activation(pr[:, 0, :], AT[:, j % 2, :], ACT.Relu).then_inc(relu_done, 1)
                    act.wait_ge(relu_done, at(n + 1, TURN))
                    nc.scalar.activation(uhi[:, j % 2, :], pr[:, 0, :], ACT.Square).then_inc(uhi_done, 1)

                hi_to(s0 + 3)
                for t in range(NT):
                    if t == 0:
                        act.wait_ge(up_mm, m + 1)
                        if m:
                            act.wait_ge(usq, j0)
                    else:
                        act.wait_ge(w_used, s0 + 2)
                    ins = nc.scalar.activation(pr[:, 0, t * FFB:(t + 1) * FFB], AT[:, 2 * t, 0:FFB], ACT.Relu)
                ins.then_inc(relu_done, 1)
                act.wait_ge(up_tr, m + 1)
                nc.scalar.activation(uhi[:, 0, :], AT[:, 3, :], ACT.Copy).then_inc(uhi_done, 1)
                hi_to(s0 + 7)
                relu(1)
                with act.Fori(0, TURNS) as i:
                    for q in range(TURN):
                        for k in range(4):
                            hi(8 + 4 * q + k, i)
                        relu(2 + q, i)
                nxt[0] = s0 + MLP_TILES - 8
                hi_to(s0 + MLP_TILES - 5)
                relu(MLP_STEPS - 2)
                hi_to(s0 + MLP_TILES - 1)
                relu(MLP_STEPS - 1)

            act.dma_start(cvec[:, 0, :], dram["c"].rearrange("a (k p) -> p (a k)", p=P),
                          allow_slow_non_contiguous=True).then_inc(ld_c, 16)
            act.dma_start(bada, dram["b_ada"][:, 0:2 * D]).then_inc(ld_bada, 16)
            act.dma_start(cst[:, 0:C_MIX], dram["const_c"][:, 0:C_MIX]).then_inc(ld_cst, 16)
            for t in range(NT):
                act.dma_start(x[:, t, :], dram["x"][0, rows_of(t), :]).then_inc(ld_x, 16)
            act.wait_ge(ld_c, 16)
            nc.scalar.activation(cvec[:, 1, :], cvec[:, 0, :], ACT.Exp, scale=-1.0).then_inc(exp_c, 1)
            act.wait_ge(ld_x, 16 * NT)
            for t in range(NT):
                nc.scalar.activation(kT[:, t * D:(t + 1) * D], x[:, t, :], ACT.Square,
                                     accum_out=stat[:, S_N1 + t:S_N1 + t + 1]).then_inc(sq_done, 1)
            act.wait_ge(ld_cst, 16)
            nc.scalar.activation(identb[:, :], ident, ACT.Copy).then_inc(cast_done, 1)
            nc.scalar.activation(negb[:, :], cst[:, C_NEG:C_NEG + P], ACT.Copy).then_inc(cast_done, 1)
            hi_to(0)
            quarter_hi(0, 0)
            hi_to(2)
            quarter_hi(0, 1)
            hi_to(3)
            act.dma_start(wsm[:, :, 0:8], dram["w_in"][0][:, FF_COL:FF_COL + 8].rearrange(
                "(k p) n -> p k n", p=P)).then_inc(ld_sm, 16)
            act.dma_start(bfor[:, :], dram["b_forget"].broadcast_to([P, 8])).then_inc(ld_sm, 16)
            act.dma_start(qkgain[:, 0:1], dram["q_norm_gain"].rearrange("a d -> d a"),
                          allow_slow_non_contiguous=True).then_inc(ld_sm, 16)
            act.dma_start(qkgain[:, 1:2], dram["k_norm_gain"].rearrange("a d -> d a"),
                          allow_slow_non_contiguous=True).then_inc(ld_sm, 16)
            hi_to(4)
            quarter_hi(0, 2)
            hi_to(5)
            quarter_hi(0, 3)
            act.wait_ge(ld_sm, 64)
            nc.scalar.activation(qkgain[:, 2:3], qkgain[:, 0:1], ACT.Copy, scale=0.125).then_inc(cast_done, 1)
            nc.scalar.activation(wsm_hi[:, :, 0:8], wsm[:, :, 0:8], ACT.Copy).then_inc(wsm_hi_done, 1)
            act.dma_start(cst[:, C_MIX:], dram["const_c"][:, C_MIX:C_SBUF]).then_inc(ld_cst, 16)
            act.wait_ge(mod_mm, 4)
            act.dma_start(fgain, dram["fox_out_gain"].rearrange("a h d -> a (h d)").broadcast_to(
                [P, 512])).then_inc(ld_sm, 16)
            act.dma_start(rgain, dram["ret_out_gain"].rearrange("a h d -> a (h d)").broadcast_to(
                [P, 512])).then_inc(ld_sm, 16)
            act.dma_start(tab[:, 0:1024], dram["decay_c"]).then_inc(ld_sm, 16)
            act.dma_start(nsm[:, 0:64].rearrange("d (i j) -> d i j", i=2),
                          dram["a_cmp_pos_2"][0].rearrange("i j d -> d i j"), allow_slow_non_contiguous=True).then_inc(ld_sm, 16)
            act.dma_start(nsm[:, 64:66], dram["a_cmp_b1_2"][0].rearrange("i e -> e i"),
                          allow_slow_non_contiguous=True).then_inc(ld_sm, 16)
            act.dma_start(nsm[:, 66:194].rearrange("e (i d) -> e i d", i=2),
                          dram["a_cmp_w2_2"][0].rearrange("i e d -> e i d")).then_inc(ld_sm, 16)
            act.dma_start(pscale[:, :], dram["a_pool_scale_2"].rearrange("a (g d) -> d (a g)", d=P),
                          allow_slow_non_contiguous=True).then_inc(ld_sm, 16)

            def ff_logs():
                act.wait_ge(ff_abs, 1)
                link(nc.scalar.activation(lf[:, 2, :], lf[:, 1, :], ACT.Exp, scale=-1.0))
                nc.scalar.activation(lf[:, 3, :], lf[:, 2, :], ACT.Ln, bias=1.0).then_inc(ff_ln, 1)

            def head_squares(b):
                act.wait_ge(w_used, T_IN + (6, 8)[b])
                for t in range(NT):
                    if b > 0:
                        act.wait_ge(sc_free, 2 * (b - 1) + t + 1)
                    nc.scalar.activation(sc[:, t, :], bank(b, t), ACT.Square).then_inc(sq_done, 1)

            def minus_cum():
                act.wait_ge(cum_mm, 1)
                act.wait_ge(acc_zero, 3)
                nc.scalar.activation(kT[64:72, :].rearrange("r (h s) -> r h s", h=8),
                                     AT[64:72, 1, 0:S].unsqueeze(1).broadcast_to([8, 8, S]), ACT.Copy,
                                     scale=-1.0).then_inc(cum_done, 1)

            def heads_out(f):
                t, j = (f // 2) % 2, f % 2
                act.wait_ge(hd_tr, f + 1)
                if f == 0:
                    act.wait_ge(cast_done, 3)
                dst = (qT if f < 4 else kT)[0:64, :].rearrange("d (h s) -> d h s", h=8)
                gain = qkgain[:, 2:3] if f < 4 else qkgain[:, 1:2]
                nc.scalar.activation(dst[:, 4 * j:4 * j + 4, rows_of(t)],
                                     AT[0:64, 2 + f % 2, :].rearrange("d (h s) -> d h s", h=4), ACT.Copy,
                                     scale=gain).then_inc(hd_done, 1)

            def block_out(pb, s_end, col, n=512, scale=1.0):
                act.wait_ge(w_used, s_end)
                for t in range(NT):
                    nc.scalar.activation(proj[:, t, col:col + n], bank(pb, t)[:, 0:n], ACT.Copy, scale=scale)\
                        .then_inc(bank_free[pb % 2], 1)

            def exps(n):
                br, t, heads = GROUPS[n]
                act.wait_ge(at_max, n + 1)
                if n >= 2:
                    act.wait_ge(at_tr, n - 1)
                w = 512 // len(heads)
                for u, h in enumerate(heads):
                    ins = nc.scalar.activation(pr[:, n % 2, u * w:(u + 1) * w], AT[:, S_BANK[n], u * w:(u + 1) * w],
                                               ACT.Exp, bias=nmax[:, n % 2, u:u + 1],
                                               accum_out=rsum[:, t, 8 * br + h:8 * br + h + 1])
                ins.then_inc(at_exp, 1)

            def fox_squares(t):
                act.wait_ge(at_out, t + 1)
                act.wait_ge(sc_free, 4 + t)
                nc.scalar.activation(sc[:, 0, :], proj[:, t, FQ:FQ + 512], ACT.Square).then_inc(sq_done, 1)

            def turned_out(f):
                t = f % 2
                act.wait_ge(rt_tr, f + 1)
                nc.scalar.activation(rows[:, f // 2, :].rearrange("d (h s) -> d h s", h=4)[:, :, rows_of(t)],
                                     AT[:, f % 2, :].rearrange("d (h s) -> d h s", h=4),
                                     ACT.Copy).then_inc(rt_done, 1)

            def ret_squares(t):
                act.wait_ge(rv_mm, 4)
                act.wait_ge(sc_free, 6)
                for h in range(4):
                    ins = nc.scalar.activation(sc[:, t, h * P:(h + 1) * P], AT[:, 2 + t, h * P:(h + 1) * P], ACT.Square,
                                               accum_out=stat[:, S_RO + 4 * t + h:S_RO + 4 * t + h + 1])
                ins.then_inc(sq_done, 1)

            def gates_ln(b, col):
                act.wait_ge(w_used, T_IN + BLK * (b + 1))
                gate_ln([bank(b, t) for t in range(NT)], [proj[:, t, col:col + 512] for t in range(NT)])

            tiles(T_IN, T_OUT, {
                5: [ff_logs, lambda: head_squares(0)], 7: [lambda: head_squares(1), minus_cum],
                8: [lambda f=f: heads_out(f) for f in range(4)],
                10: [lambda f=f: heads_out(f) for f in range(4, 8)],
                11: [lambda: block_out(2, T_IN + 12, FV), lambda: exps(0)],
                12: [lambda: exps(1)], 13: [lambda: exps(2)], 14: [lambda: exps(3), lambda: fox_squares(0)],
                15: [lambda: exps(4)], 16: [lambda: exps(5)], 17: [lambda: hi_to(T_IN + 21), lambda: gates_ln(3, OG)],
                18: [lambda: fox_squares(1)],
                19: [lambda: gate_sig(0, proj[:, 0, OG:OG + 512]), lambda: gate_sig(1, proj[:, 1, OG:OG + 512])],
                22: [lambda: turned_out(0), lambda: turned_out(1)], 23: [lambda: mod_row_out(2)],
                26: [lambda: turned_out(2), lambda: turned_out(3), lambda: quarter_hi(1, 0), lambda: quarter_hi(1, 1)],
                27: [lambda: block_out(6, T_IN + 28, RV)],
                29: [lambda: ret_squares(0), lambda: ret_squares(1)],
                30: [lambda: mod_row_out(3)],
                31: [lambda: gates_ln(7, RG), lambda: gate_sig(2, proj[:, 0, RG:RG + 512]),
                     lambda: gate_sig(3, proj[:, 1, RG:RG + 512])],
            })
            tiles(T_OUT, T_OUT + 4, {
                2: [lambda: quarter_hi(1, 2), lambda: quarter_hi(1, 3)],
            })
            def sq_half(t, h):
                act.wait_ge(x_upd, 2 * t + h + 1)
                nc.scalar.activation(kT[:, (2 * t + h) * 512:(2 * t + h + 1) * 512], x[:, t, 512 * h:512 * (h + 1)],
                                     ACT.Square, accum_out=stat[:, S_N2 + 2 * h + t:S_N2 + 2 * h + t + 1])\
                    .then_inc(sq_done, 1)

            hi_to(T_MLP0 - 1)
            mod_row_out(4)
            hi_to(T_MLP0)
            sq_half(0, 0)
            hi_to(T_MLP0 + 1)
            sq_half(0, 1)
            quarter_hi(2, 0)
            sq_half(1, 0)
            quarter_hi(2, 1)
            sq_half(1, 1)
            hi_to(T_MLP0 + 3)
            quarter_hi(2, 2)
            quarter_hi(2, 3)
            mlp(0, T_MLP0)
            mod_row_out(5)
            hi_to(T_AIN + 1)
            for q in range(4):
                quarter_hi(3, q)
                hi_to(T_AIN + 3) if q == 1 else None

            def nt_out(f, dst):
                act.wait_ge(nt_tr, f + 1)
                b = AT[0:64, 2 if f == 7 else 2 + f % 2, :]
                nc.scalar.activation(dst, b if len(dst.shape) == 2 else b.rearrange("d (h s) -> d h s", h=4),
                                     ACT.Copy).then_inc(nt_done, 1)

            def q_out(f):
                t, j = (f - 3) // 2, (f - 3) % 2
                nt_out(f, qT[0:64, :].rearrange("d (h s) -> d h s", h=8)[:, 4 * j:4 * j + 4, rows_of(t)])

            def hidden_bias():
                act.wait_ge(c_mm, 1)
                act.wait_ge(ld_sm, 16 * 11)
                for i in range(2):
                    ins = nc.scalar.activation(gel[:, 0, 30 * i:30 * i + 30], AT[0:64, 0, 32 * i:32 * i + 30], ACT.Identity,
                                               bias=nsm[:, 64 + i:65 + i])
                ins.then_inc(c_z, 1)

            def gelu_exp():
                act.wait_ge(c_e, 1)
                nc.scalar.activation(gel[:, 3, :], gel[:, 2, :], ACT.Exp, scale=-GELU_C).then_inc(c_gel, 1)

            def branch_gates():
                act.wait_ge(bank_free[0], 2 * ((B_AIN + 2) // 2) + 2)
                nc.scalar.activation(proj[:, :, N_GT:N_GT + 24], proj[:, :, N_GT:N_GT + 24], ACT.Exp,
                                     scale=-1.0).then_inc(gate_exp, 1)

            def cmp_exp():
                act.wait_ge(cs_sub, 1)
                nc.scalar.activation(proj[:, 0, CSB:CSB + 240], proj[:, 0, CSB:CSB + 240], ACT.Exp).then_inc(cs_exp, 1)

            def cmp_out():
                act.wait_ge(ct_tr, 1)
                nc.scalar.activation(proj[0:HC, 0, PCT:PCT + S], AT[0:HC, 0, 0:S], ACT.Copy).then_inc(ct_done, 1)

            def u_out():
                act.wait_ge(w_used, T_AIN + 16)
                for t in range(NT):
                    nc.scalar.activation(proj[:, t, N_U:N_U + 512], bank(B_AIN + 3, t), ACT.Copy).then_inc(bank_free[1], 1)

            def means_out():
                for k in range(2):
                    act.wait_ge(pm_mm, k + 1)
                    nc.scalar.activation(proj[:, 1, RT_ + 512 * k:RT_ + 512 * (k + 1)], PJ[:, k, :],
                                         ACT.Copy).then_inc(pm_done, 1)

            def pooled_hi():
                for g in range(4):
                    act.wait_ge(py_mm, g // 2 + 1)
                    nc.scalar.activation(u4(uhi)[:, g, :], PJ[:, 2 + g // 2, (g % 2) * S:(g % 2 + 1) * S], ACT.Copy,
                                         scale=pscale[:, g:g + 1]).then_inc(pl_hi, 1)

            def nsa_hi(t):
                act.wait_ge(at_pv, PV_DONE[1][t])
                act.wait_ge(cv_mm, 1)
                act.wait_ge(w_used, T_AOUT)
                nc.scalar.activation(hT_hi[:, 0:4, rows_of(t)], AT[:, NSA_O[t], :].rearrange("p (c s) -> p c s", c=4),
                                     ACT.Copy).then_inc(on_hi, 1)

            tiles(T_AIN, T_AOUT, {
                3: [lambda: block_out(B_AIN, T_AIN + 4, 512)],
                4: [lambda f=f: nt_out(f, kT[0:64, f * 512:(f + 1) * 512]) for f in range(2)],
                5: [lambda: nt_out(2, kT[0:64, 1024:1536])],
                7: [lambda: block_out(B_AIN + 1, T_AIN + 8, 0, scale=0.125), hidden_bias],
                8: [gelu_exp] + [lambda f=f: q_out(f) for f in (3, 4)],
                9: [lambda f=f: q_out(f) for f in (5, 6)],
                10: [lambda: exps(6)],
                11: [lambda: block_out(B_AIN + 2, T_AIN + 12, 1024, 280), branch_gates, lambda: exps(7), cmp_exp],
                12: [lambda: exps(8)],
                13: [lambda: nt_out(7, kT[0:64, 1536:2048]), cmp_out, lambda: exps(9)],
                14: [lambda: exps(10)],
                15: [u_out, lambda: exps(11), means_out, lambda: exps(12), pooled_hi, lambda: exps(13)],
            }, range(12, 15))
            tiles(T_AOUT, T_AOUT + 4, {
                0: [lambda: exps(14)], 1: [lambda: exps(15)], 2: [lambda: exps(16)],
                3: [lambda: nsa_hi(0), lambda: exps(17)],
            }, range(4))
            hi_to(T_MLP1 + 1)
            nsa_hi(1)
            for q in range(4):
                quarter_hi(5, q)
                hi_to(T_MLP1 + 3) if q == 1 else None
            mlp(1, T_MLP1)
            act.wait_ge(ld_gla, 80)
            act.wait_ge(ff_mm, 1)
            nc.scalar.activation(wsm_hi[:, :, :], wsm[:, :, :], ACT.Copy).then_inc(wsm_hi_done, 1)
            hi_to(T_CIN + 1)
            for q in range(4):
                hi_to(T_CIN + 1 + q) if q in (1, 2) else None
                quarter_hi(6, q)

            def rank_out():
                act.wait_ge(aT_tr, 1)
                nc.scalar.activation(aT, AT[0:16, 1, 0:S], ACT.Copy).then_inc(aT_done, 1)

            def gla_ln():
                for t in range(NT):
                    act.wait_ge(z_abs, t + 1)
                    ins = nc.scalar.activation(pr[:, t, :], prT[:, t, :], ACT.Exp, scale=-1.0)
                link(ins)
                for t in range(NT):
                    nc.scalar.activation(prT[:, t, :], pr[:, t, :], ACT.Ln, bias=1.0).then_inc(z_ln, 1)

            def gla_exps(t):
                act.wait_ge(b_mm, t + 1)
                a, b, c = GLA_E[t]
                nc.scalar.activation(a, AT[:, 2 * t, :], ACT.Exp).then_inc(eb_done, 1)
                nc.scalar.activation(b, AT[:, 2 * t, :], ACT.Exp, scale=-1.0).then_inc(eb_done, 1)
                nc.scalar.activation(c, AT[:, 2 * t + 1, :], ACT.Exp).then_inc(eb_done, 1)

            def decays():
                act.wait_ge(b_mm, 3)
                nc.scalar.activation(dec[:, :, :].rearrange("p a b -> p (a b)"), AT[:, 0, 0:16], ACT.Exp)\
                    .then_inc(eb_done, 1)

            def g_out(f):
                act.wait_ge(g_tr, f + 1)
                nc.scalar.activation((qT, kT)[f % 2][:, 0:D].rearrange("d (h s) -> d h s", h=4)[:, :, rows_of(f // 2)],
                                     AT[:, (1, 2, 3, 1)[f], :].rearrange("d (h s) -> d h s", h=4),
                                     ACT.Copy).then_inc(g_trd, 1)

            def gla_squares(t):
                act.wait_ge(go_mm, t + 1)
                for h in range(4):
                    c = slice(256 * (h % 2), 256 * (h % 2 + 1))
                    ins = nc.scalar.activation((sc, pr)[t][:, h // 2, c], AT[:, 2 * t + h // 2, c], ACT.Square,
                                               accum_out=stat[:, S_GO + 4 * t + h:S_GO + 4 * t + h + 1])
                ins.then_inc(sq_done, 1)

            r_at = lambda j, t: proj[:, t, 2048 + 512 * j:2048 + 512 * (j + 1)]

            def r_ln(j):
                act.wait_ge(w_used, T_CIN + 20 + 4 * j)
                gate_ln([bank(B_CIN + 4 + j, t) for t in range(NT)], [r_at(j, t) for t in range(NT)])

            def r_sig(j):
                for t in range(NT):
                    gate_sig(4 + 2 * j + t, r_at(j, t))

            tiles(T_CIN, T_COUT, {
                3: [lambda: block_out(B_CIN, T_CIN + 4, 0, scale=P ** -0.5)], 4: [rank_out],
                5: [gla_ln], 7: [lambda: block_out(B_CIN + 1, T_CIN + 8, 512)],
                8: [lambda: gla_exps(0), lambda: gla_exps(1)], 9: [decays],
                11: [lambda: block_out(B_CIN + 2, T_CIN + 12, 1024)] + [lambda f=f: g_out(f) for f in range(3)],
                12: [lambda: g_out(3)], 15: [lambda: block_out(B_CIN + 3, T_CIN + 16, 1536)],
                19: [lambda: r_ln(0), lambda: gla_squares(0)],
                20: [lambda: r_sig(0), lambda: gla_squares(1)],
                22: [lambda: quarter_hi(7, 0), lambda: quarter_hi(7, 1)],
                23: [lambda: hi_to(T_CIN + 27), lambda: r_ln(1), lambda: r_sig(1)],
            })
            tiles(T_COUT, T_COUT + 4, {
                2: [lambda: quarter_hi(7, 2), lambda: quarter_hi(7, 3)],
            })
            hi_to(T_MLP2 + 1)
            for q in range(4):
                quarter_hi(8, q)
                hi_to(T_MLP2 + 3) if q == 1 else None
            mlp(2, T_MLP2)

        @block.vector
        def _(dve):
            order = [0]

            def link(ins):
                order[0] += 1
                ins.then_inc(dseq, 1)
                dve.wait_ge(dseq, order[0])

            tt, ts, stt = nc.vector.tensor_tensor, nc.vector.tensor_scalar, nc.vector.scalar_tensor_tensor
            heads8 = lambda a: a.rearrange("p (h d) -> p h d", h=8)
            wide = lambda a, d: a.unsqueeze(2).broadcast_to([P, a.shape[1], d])

            nxt, last_ada = [0], [-1]

            def lo_to(s1):
                raw_to(W_AT[s1 + 1] if s1 + 1 < T_END else len(RAW_SEQ))

            def raw_to(end):
                while nxt[0] < end:
                    r = nxt[0]
                    kind, n = RAW_SEQ[r]
                    if kind == "w":
                        dve.wait_ge(hi_done, n + 1)
                        tt(wlo[:, n % SPL, :], raw_slot(r), whi[:, n % SPL, :].bitcast(F32),
                           ALU.subtract).then_inc(raw_done, 1)
                    else:
                        dve.wait_ge(raw_full[r % RAW], 16 * (r // RAW + 1))
                        if last_ada[0] >= 0:
                            dve.wait_ge(raw_done, last_ada[0] + 1)
                        last_ada[0] = r
                        if n in ADA_PE:
                            dve.wait_ge(ada_mm, ADA_PE.index(n) + 1)
                            dve.nop().then_inc(raw_done, 1)
                            nxt[0] += 1
                            continue
                        if n < ADA_FIRST:
                            sums = acc[:, 0:2 * D].rearrange("p (a b c) -> p a b c", a=2, b=2)[:, :, n // KC, :]
                            tile = raw_slot(r).rearrange("p (a c) -> p a c", a=2)
                        else:
                            sums, tile = acc[:, ADA_ORDER[n // KC] * D:(ADA_ORDER[n // KC] + 1) * D], raw_slot(r)
                        c = cvec[:, 3, n % KC:n % KC + 1]
                        if n % KC == 0 and n < ADA_FIRST:
                            ts(sums, tile, c, None, ALU.mult).then_inc(raw_done, 1)
                        else:
                            stt(sums, tile, c, sums, ALU.mult, ALU.add).then_inc(raw_done, 1)
                    nxt[0] += 1

            def tiles(s0, s1, after, first=()):
                for s in range(s0, s1):
                    if s - s0 not in first:
                        raw_to(raw_of(s + LEAD) + 1)
                    for step in after.get(s - s0, ()):
                        step()
                    lo_to(s + LEAD)

            def quarter_lo(n, q):
                t, j = QUARTERS[n][q]
                dve.wait_ge(hThi_done, units(n) + q + 1)
                hi, lo = split_dst(n, j)
                tt(lo[:, :, rows_of(t)], tr_bank(n, t, j).rearrange("p (c s) -> p c s", c=4),
                   hi[:, :, rows_of(t)].bitcast(F32), ALU.subtract).then_inc(hTlo_done, 1)

            asked = [0]

            def rstd_wait():
                asked[0] += 1
                dve.wait_ge(rstd_ready, asked[0])

            def variance(col, n, width, eps=EPS):
                ts(stat[:, col:col + n], stat[:, col:col + n], 1.0 / width, eps, ALU.mult, ALU.add).then_inc(var_ready, 1)

            MLP_BANKS = (B_MLP0, B_MLP1, B_MLP2)
            mod = lambda i: acc[:, i * D:(i + 1) * D]
            half = lambda j: slice(512 * j, 512 * (j + 1))

            def product_wait(pb, t, h, s_end):
                if t == 0:
                    dve.wait_ge(prod_done, 2 * PROD[pb] + h + 1)
                elif pb in MLP_BANKS and h == 0:
                    dve.wait_ge(half_done, MLP_BANKS.index(pb) + 1)
                else:
                    dve.wait_ge(w_used, s_end[h])

            def add_gated(pb, t, h, s_end, gate):
                product_wait(pb, t, h, s_end)
                tmp = sc[:, h, :]
                xs = x[:, t, half(h)]
                ins = tt(tmp, bank(pb + h, t), gate[:, half(h)], ALU.mult)
                ins.then_inc(bank_free[(pb + h) % 2], 1)
                dve.wait_ge(bank_free[(pb + h) % 2], 2 * ((pb + h) // 2) + t + 1)
                return tt(xs, xs, tmp, ALU.add)

            def ln_half(n, pb, t, h, s_end):
                product_wait(pb, t, h, s_end)
                xs = x[:, t, half(h)]
                stt(xs, xs, ALPHA, bank(pb + h, t), ALU.mult, ALU.add).then_inc(bank_free[(pb + h) % 2], 1)
                dve.wait_ge(bank_free[(pb + h) % 2], 2 * ((pb + h) // 2) + t + 1)
                link(nc.vector.bn_stats(bn[:, t, 6 * h:6 * h + 6], xs))

            def ln_end(n, t, between=None):
                c = S_LN + 2 * n + t
                link(nc.vector.bn_aggr(bn[:, t, 12:14], bn[:, t, 0:12].rearrange("p (a b) -> p a b", a=2)))
                ts(stat[:, c:c + 1], bn[:, t, 13:14], LN_EPS, None, ALU.add).then_inc(var_ready, 1)
                dve.wait_ge(ld_row, 32 * (n + 1))
                for j in range(2):
                    xs = x[:, t, half(j)]
                    link(stt(xs, xs, bn[:, t, 12:13], rows[:, 0, half(j)], ALU.subtract, ALU.mult))
                    rstd_wait() if j == 0 else None
                    stt(xs, xs, rstd[:, c:c + 1], rows[:, 1, half(j)], ALU.mult, ALU.add).then_inc(src_ready, 1)
                    between() if j == 0 and between else None

            def out_norm(n, pb, s_end, stage):
                lo_to(s_end[1] - 1)
                ln_half(n, pb, 0, 0, s_end)
                lo_to(s_end[1])
                ln_half(n, pb, 0, 1, s_end)
                lo_to(s_end[1] + 1)
                ln_end(n, 0)
                ln_half(n, pb, 1, 0, s_end)
                quarter_lo(stage, 0)
                ln_half(n, pb, 1, 1, s_end)
                ln_end(n, 1, lambda: quarter_lo(stage, 1))
                quarter_lo(stage, 2)
                quarter_lo(stage, 3)

            def gate_min(k, z, e):
                dve.wait_ge(gt_ln, k + 1)
                return stt(e, z, 0.0, e, ALU.min, ALU.subtract).then_inc(gt_min, 1)

            def mlp(m, s0):
                j0 = m * MLP_STEPS

                def lo(k, i):
                    s, r = s0 + k, raw_of(s0 + k)
                    dve.wait_ge(hi_done, i * (4 * TURN) + (s + 1))
                    tt(wlo[:, s % SPL, :], raw_slot(r), whi[:, s % SPL, :].bitcast(F32), ALU.subtract)\
                        .then_inc(raw_done, 1)

                def square(j, i=None):
                    n = j0 + j
                    at = lambda v: v if i is None else i * TURN + v
                    dve.wait_ge(relu_done, at(n + 1))
                    if n >= 1:
                        dve.wait_ge(ulo_done, at(n))
                    tt(pr[:, 1, :], pr[:, 0, :], pr[:, 0, :], ALU.mult).then_inc(usq, 1)
                    dve.wait_ge(usq, at(n + 1))
                    dve.wait_ge(uhi_done, at(n + 1))
                    tt(ulo[:, j % 2, :], pr[:, 1, :], uhi[:, j % 2, :].bitcast(F32), ALU.subtract).then_inc(ulo_done, 1)

                lo_to(s0 + 2)
                dve.wait_ge(relu_done, j0 + 1)
                tt(pr[:, 1, :], pr[:, 0, :], pr[:, 0, :], ALU.mult).then_inc(usq, 1)
                lo_to(s0 + 3)
                dve.wait_ge(uhi_done, j0 + 1)
                tt(ulo[:, 0, :], AT[:, 3, :], uhi[:, 0, :].bitcast(F32), ALU.subtract).then_inc(ulo_done, 1)
                lo_to(s0 + 7)
                square(1)
                with dve.Fori(0, TURNS) as i:
                    for q in range(TURN):
                        for k in range(4):
                            lo(8 + 4 * q + k, i)
                        square(2 + q, i)
                nxt[0] = raw_of(s0 + MLP_TILES - 8)
                lo_to(s0 + MLP_TILES - 5)
                square(MLP_STEPS - 2)
                lo_to(s0 + MLP_TILES - 1)
                square(MLP_STEPS - 1)

            dve.wait_ge(exp_c, 1)
            link(ts(cvec[:, 1, :], cvec[:, 1, :], 1.0, None, ALU.add))
            link(nc.vector.reciprocal(cvec[:, 2, :], cvec[:, 1, :]))
            link(tt(cvec[:, 3, :], cvec[:, 2, :], cvec[:, 0, :], ALU.mult))
            nc.vector.tensor_copy(cspread, cvec[:, 3, :].unsqueeze(2).broadcast_to([P, KC, P])).then_inc(cb_done, 1)
            raw_to(KC)
            for t in range(NT):
                dve.wait_ge(sq_done, t + 1)
                variance(S_N1 + t, 1, D)

            def scaled(t, j):
                dve.wait_ge(mod_mm, 2 * j + 1)
                return stt(qT[:, t * D + 512 * j:t * D + 512 * (j + 1)], AT[:, 0, :], 1.0, x[:, t, half(j)],
                           ALU.add, ALU.mult)

            def shifted(t, j):
                dve.wait_ge(mod_mm, 2 * j + 2)
                rstd_wait() if j == 0 else None
                h = qT[:, t * D + 512 * j:t * D + 512 * (j + 1)]
                stt(h, h, rstd[:, S_N1 + t:S_N1 + t + 1], AT[:, 2, :], ALU.mult, ALU.add).then_inc(src_ready, 1)

            link(scaled(0, 0))
            shifted(0, 0)
            lo_to(0)
            quarter_lo(0, 0)
            link(scaled(1, 0))
            shifted(1, 0)
            lo_to(2)
            raw_to(W_AT[3] + 2)
            quarter_lo(0, 1)
            lo_to(3)
            link(scaled(0, 1))
            shifted(0, 1)
            dve.wait_ge(ld_bada2, 16)
            lo_to(4)
            quarter_lo(0, 2)
            link(scaled(1, 1))
            shifted(1, 1)
            lo_to(5)
            quarter_lo(0, 3)
            dve.wait_ge(wsm_hi_done, 1)
            tt(wsm_lo[:, :, 0:8], wsm[:, :, 0:8], wsm_hi[:, :, 0:8].bitcast(F32), ALU.subtract).then_inc(wsm_done, 1)

            def ff_start():
                dve.wait_ge(ff_mm, 1)
                lf2 = lambda k: lf[:, k, :].rearrange("p (t h) -> p t h", t=NT)
                link(tt(lf2(0), AT[:, 0, 0:16].rearrange("p (t h) -> p t h", t=NT),
                        bfor[:, :].unsqueeze(1).broadcast_to([P, NT, 8]), ALU.add))
                stt(lf[:, 1, :], lf[:, 0, :], -1.0, lf[:, 0, :], ALU.mult, ALU.max).then_inc(ff_abs, 1)

            def ff_end():
                dve.wait_ge(ff_ln, 1)
                stt(lf[:, 4, :], lf[:, 0, :], 0.0, lf[:, 3, :], ALU.min, ALU.subtract).then_inc(ff_done, 1)

            def head_norm(b, col, sq0):
                for t in range(NT):
                    c = col + 8 * t
                    dve.wait_ge(sq_done, sq0 + t + 1)
                    ins = nc.vector.tensor_reduce(stat[:, c:c + 8], heads8(sc[:, t, :]), AX, ALU.add)
                    ins.then_inc(sc_free, 1)
                    dve.wait_ge(sc_free, 2 * b + t + 1)
                    variance(c, 8, 64)
                for t in range(NT):
                    c = col + 8 * t
                    rstd_wait()
                    tt(heads8(proj[:, t, FQ + 512 * b:FQ + 512 * (b + 1)]), heads8(bank(b, t)),
                       wide(rstd[:, c:c + 8], 64), ALU.mult).then_inc(qk_norm, 1)
                    dve.wait_ge(qk_norm, 2 * b + t + 1)
                    dve.nop().then_inc(bank_free[b % 2], 1)

            def cum_rows():
                dve.wait_ge(cum_done, 1)
                dve.wait_ge(ld_sel, 32)
                nc.vector.tensor_copy(qT[96:104, :].rearrange("r (h s) -> r h s", h=8),
                                      AT[96:104, 1, S:2 * S].unsqueeze(1).broadcast_to([8, 8, S])).then_inc(cum_done, 1)

            def maxima(n):
                u = len(GROUPS[n][2])
                dve.wait_ge(at_mm, n + 1)
                if n >= 2:
                    dve.wait_ge(at_exp, n - 1)
                nc.vector.tensor_reduce(nmax[:, n % 2, 0:u], AT[:, S_BANK[n], :].rearrange("p (u k) -> p u k", u=u),
                                        AX, ALU.max, negate=True).then_inc(at_max, 1)

            def probs_out(n):
                dve.wait_ge(at_tr, n + 1)
                if n >= 2:
                    dve.wait_ge(at_pv, n - 1)
                nc.vector.tensor_copy(prT[:, n % 2, :], AT[:, 2, :]).then_inc(at_trd, 1)

            def fox_out(t):
                dve.wait_ge(at_pv, PV_DONE[0][t])
                link(nc.vector.reciprocal(rinv[:, t, 0:8], rsum[:, t, 0:8]))
                dve.wait_ge(hd_tr, 4)
                tt(heads8(proj[:, t, FQ:FQ + 512]), heads8(AT[:, 3, :]), wide(rinv[:, t, 0:8], 64), ALU.mult)\
                    .then_inc(at_out, 1)

            def squares_summed(sq, col, n, width, k):
                dve.wait_ge(sq_done, sq)
                ins = nc.vector.tensor_reduce(stat[:, col:col + n], sc[:, 0, :].rearrange("p (h d) -> p h d", h=n),
                                              AX, ALU.add)
                ins.then_inc(sc_free, 1)
                dve.wait_ge(sc_free, k)
                variance(col, n, width)

            def fox_final(t):
                rstd_wait()
                o = proj[:, t, FQ:FQ + 512]
                link(tt(heads8(o), heads8(o), wide(rstd[:, S_FO + 8 * t:S_FO + 8 * t + 8], 64), ALU.mult))
                dve.wait_ge(ld_sm, 16 * 11)
                link(tt(o, o, fgain, ALU.mult))
                dve.wait_ge(gt_sig, t + 1)
                tt(o, o, proj[:, t, OG:OG + 512], ALU.mult).then_inc(src_ready, 1)

            def out_gates():
                for t in range(NT):
                    ins = gate_min(t, bank(3, t), proj[:, t, OG:OG + 512])
                    dve.wait_ge(gt_min, t + 1)
                    dve.nop().then_inc(bank_free[1], 1)

            def rotate(b, dst, k):
                dve.wait_ge(w_used, T_IN + BLK * (b + 1))
                dve.wait_ge(ld_cst, 32)
                dve.wait_ge(hd_tr, 8)
                for t in range(NT):
                    xh = bank(b, t).rearrange("p (h d) -> p h d", h=4)
                    cos = cst[:, C_COS + P * t:C_COS + P * (t + 1)].unsqueeze(1).broadcast_to([P, 4, P])
                    sin = cst[:, C_SIN + P * t:C_SIN + P * (t + 1)].unsqueeze(1).broadcast_to([P, 4, P])
                    a = sc[:, 0, :].rearrange("p (h d) -> p h d", h=4)
                    c = sc[:, 1, :].rearrange("p (h d) -> p h d", h=4)
                    tt(a, xh, cos, ALU.mult)
                    tt(c[:, :, 0:64], xh[:, :, 64:P], sin[:, :, 0:64], ALU.mult)
                    ins = tt(c[:, :, 64:P], xh[:, :, 0:64], sin[:, :, 64:P], ALU.mult)
                    ins.then_inc(bank_free[b % 2], 1)
                    dve.wait_ge(bank_free[b % 2], 2 * (b // 2) + t + 1)
                    link(tt(proj[:, t, dst:dst + 512], sc[:, 0, :], sc[:, 1, :], ALU.add))
                    dve.nop().then_inc(rope_done, 1)

            def decayed(h):
                dve.wait_ge(rs_mm, h + 1)
                if h >= 2:
                    dve.wait_ge(rv_mm, h - 1)
                tt(pr[:, h % 2, 0:S], AT[:, h % 2, 0:S], tab[:, S * h:S * (h + 1)], ALU.mult)
                tt(pr[:, h % 2, S:S + P], AT[:, h % 2, S:S + P], tab[:, S * h:S * h + P], ALU.mult).then_inc(rp_done, 1)

            def ret_norm():
                for t in range(NT):
                    dve.wait_ge(sq_done, 8 + t + 1)
                    variance(S_RO + 4 * t, 4, P)
                dve.wait_ge(hd_tr, 8)
                for t in range(NT):
                    rstd_wait()
                    link(tt(proj[:, t, FK:FK + 512].rearrange("p (h d) -> p h d", h=4),
                            AT[:, 2 + t, :].rearrange("p (h d) -> p h d", h=4),
                            wide(rstd[:, S_RO + 4 * t:S_RO + 4 * t + 4], P), ALU.mult))
                    link(tt(proj[:, t, FK:FK + 512], proj[:, t, FK:FK + 512], rgain, ALU.mult))

            def ret_gates():
                for t in range(NT):
                    o = proj[:, t, FK:FK + 512]
                    gate_min(2 + t, bank(7, t), proj[:, t, RG:RG + 512])
                    tt(o, o, bank(7, t), ALU.mult).then_inc(bank_free[1], 1)

            def ret_final():
                for t in range(NT):
                    o = proj[:, t, FK:FK + 512]
                    dve.wait_ge(bank_free[1], 2 * 3 + t + 1)
                    dve.wait_ge(gt_sig, 2 + t + 1)
                    tt(o, o, proj[:, t, RG:RG + 512], ALU.mult).then_inc(src_ready, 1)

            tiles(T_IN, T_OUT, {
                5: [ff_start, ff_end, lambda: head_norm(0, S_FQ, 2)],
                7: [lambda: head_norm(1, S_FK, 4), cum_rows],
                11: [lambda: maxima(0)], 12: [lambda: probs_out(0), lambda: maxima(1)],
                13: [lambda: probs_out(1), lambda: maxima(2)],
                14: [lambda: fox_out(0), lambda: probs_out(2), lambda: maxima(3),
                     lambda: squares_summed(7, S_FO, 8, 64, 5)],
                15: [lambda: probs_out(3), lambda: maxima(4)],
                16: [lambda: probs_out(4), lambda: maxima(5)],
                17: [lambda: probs_out(5)],
                18: [out_gates, lambda: fox_out(1), lambda: squares_summed(8, S_FO + 8, 8, 64, 6)],
                19: [lambda: rotate(4, RQ, 0)], 23: [lambda: fox_final(0)],
                24: [lambda: rotate(5, RK, 1), lambda: fox_final(1)],
                27: [lambda: quarter_lo(1, 0), lambda: quarter_lo(1, 1), lambda: decayed(0), lambda: decayed(1)], 28: [lambda: decayed(2), lambda: decayed(3)],
                29: [ret_norm], 
31: [ret_gates, ret_final],
            }, (11,))
            tiles(T_OUT, T_OUT + 4, {
                1: [lambda: quarter_lo(1, 2), lambda: quarter_lo(1, 3)],
            })
            s_end = (T_OUT + 6, T_OUT + 8)

            def norm2_half(t, h, between=None):
                add_gated(B_OUT, t, h, s_end, mod(2)).then_inc(x_upd, 1)
                between() if between else None
                dve.wait_ge(x_upd, 2 * t + h + 1)
                stt(qT[:, t * D + 512 * h:t * D + 512 * (h + 1)], mod(4)[:, half(h)], 1.0, x[:, t, half(h)],
                    ALU.add, ALU.mult)

            def norm2_end(t, between=None):
                dve.wait_ge(sq_done, 10 + 2 * t + 2)
                c = S_N2 + t
                link(tt(stat[:, c:c + 1], stat[:, c:c + 1], stat[:, c + 2:c + 3], ALU.add))
                variance(c, 1, D)
                between() if between else None
                rstd_wait()
                dve.wait_ge(mod_row, 6)
                for j in range(2):
                    h = qT[:, t * D + 512 * j:t * D + 512 * (j + 1)]
                    stt(h, h, rstd[:, c:c + 1], mod(3)[:, half(j)], ALU.mult, ALU.add).then_inc(src_ready, 1)

            dve.wait_ge(mod_row, 4)
            lo_to(T_MLP0 - 1)
            norm2_half(0, 0)
            lo_to(T_MLP0)
            norm2_half(0, 1)
            norm2_end(0, lambda: lo_to(T_MLP0 + 1))
            norm2_half(1, 0, lambda: quarter_lo(2, 0))
            norm2_half(1, 1)
            norm2_end(1, lambda: quarter_lo(2, 1))
            quarter_lo(2, 2)
            quarter_lo(2, 3)
            mlp(0, T_MLP0)
            lo_to(T_AIN + 1)
            dve.wait_ge(mod_row, 8)
            for t in range(NT):
                for h in range(2):
                    add_gated(B_MLP0, t, h, (T_AIN, T_AIN), mod(5)).then_inc(src_ready, 1)
                for j in range(2):
                    quarter_lo(3, 2 * t + j)
                lo_to(T_AIN + 3)

            def block_keys():
                dve.wait_ge(ld_nsa, 32)
                for i in range(2):
                    dve.wait_ge(nt_done, i + 1)
                    src = kT[0:64, i * 512:(i + 1) * 512].rearrange("d (g c j) -> d j g c", g=2, j=16)
                    dst = (acc if i == 0 else qT)[0:64, (KB if i == 0 else 0):(KB if i == 0 else 0) + 960]
                    dst = dst.rearrange("d (b j g c) -> d b j g c", b=2, j=16, g=2)
                    for b in range(2):
                        pos = nsm[:, 32 * i + 16 * b:32 * i + 16 * b + 16]
                        ins = tt(dst[:, b], src[:, :, :, b:b + NCMP],
                                 pos.unsqueeze(2).unsqueeze(3).broadcast_to([64, 16, 2, NCMP]), ALU.add)
                    ins.then_inc(kb_done, 1)

            def gelu_start():
                dve.wait_ge(c_z, 1)
                link(tt(gel[:, 1, :], gel[:, 0, :], gel[:, 0, :], ALU.mult))
                link(ts(gel[:, 1, :], gel[:, 1, :], 0.044715, 1.0, ALU.mult, ALU.add))
                tt(gel[:, 2, :], gel[:, 1, :], gel[:, 0, :], ALU.mult).then_inc(c_e, 1)

            def gelu_end():
                dve.wait_ge(c_gel, 1)
                link(ts(gel[:, 3, :], gel[:, 3, :], 1.0, None, ALU.add))
                link(nc.vector.reciprocal(gel[:, 4, :], gel[:, 3, :]))
                link(tt(gel[:, 5, :], gel[:, 4, :], gel[:, 0, :], ALU.mult))
                nc.vector.tensor_copy(proj[0:64, 1, GVR:GVR + HC].rearrange("e (g a c) -> e g a c", g=2, a=4),
                                      gel[:, 5, 30:60].rearrange("e (g c) -> e g c", g=2).unsqueeze(2).broadcast_to(
                                          [64, 2, 4, NCMP])).then_inc(c_gel, 1)

            def compressed_out():
                dve.wait_ge(c2_mm, 1)
                nc.vector.tensor_copy(gel[:, 0, 0:30], AT[0:64, 0, 64:94]).then_inc(c2_done, 1)
                tt(proj[0:HC, 0, VCB:VCB + 512].rearrange("r (h d) -> r h d", h=8),
                   AT[0:HC, 0, 96:160].unsqueeze(1).broadcast_to([HC, 8, 64]),
                   cst[0:HC, C_HM:C_HM + 8].unsqueeze(2).broadcast_to([HC, 8, 64]), ALU.mult).then_inc(c2_done, 1)

            gate_of = proj[:, :, N_GT:N_GT + 24].rearrange("p t (h b) -> p t h b", b=3)

            def gates_out():
                dve.wait_ge(gate_exp, 1)
                gt = proj[:, :, N_GT:N_GT + 24]
                link(ts(gt, gt, 1.0, None, ALU.add))
                link(nc.vector.reciprocal(gt, gt))

            csf = proj[:, 0, CSB:CSB + 240]
            cs = csf.rearrange("p (t h c) -> p t h c", t=NT, h=8)
            csr = csf.rearrange("p (r c) -> p r c", c=NCMP)
            m01 = cst[:, C_M01:C_M01 + 30].rearrange("p (t c) -> p t c", t=NT).unsqueeze(2).broadcast_to([P, NT, 8, NCMP])
            mng = cst[:, C_MNG:C_MNG + 30].rearrange("p (t c) -> p t c", t=NT).unsqueeze(2).broadcast_to([P, NT, 8, NCMP])

            def cmp_max():
                dve.wait_ge(cs_mm, 1)
                link(tt(cs, AT[:, 0, 256:496].rearrange("p (t h c) -> p t h c", t=NT, h=8), m01, ALU.mult))
                link(tt(cs, cs, mng, ALU.add))
                link(nc.vector.tensor_reduce(cred[:, 0, :], csr, AX, ALU.max))
                tt(csr, csr, wide(cred[:, 0, :], NCMP), ALU.subtract).then_inc(cs_sub, 1)

            def cmp_probs():
                dve.wait_ge(cs_exp, 1)
                link(tt(cs, cs, m01, ALU.mult))
                link(nc.vector.tensor_reduce(cred[:, 1, :], csr, AX, ALU.add))
                link(ts(cred[:, 1, :], cred[:, 1, :], 1e-30, None, ALU.max))
                link(nc.vector.reciprocal(cred[:, 2, :], cred[:, 1, :]))
                by_head = cred[:, 2, :].rearrange("p (t h) -> p t h", t=NT)
                link(tt(by_head, by_head, gate_of[:, :, :, 0], ALU.mult))
                tt(csr, csr, wide(cred[:, 2, :], NCMP), ALU.mult).then_inc(cs_p, 1)

            def weigh(n):
                br, t, heads = GROUPS[n]
                dve.wait_ge(at_exp, n + 1)
                h = slice(8 * br + heads[0], 8 * br + heads[-1] + 1)
                v = rinv[:, t, h]
                link(ts(v, rsum[:, t, h], 1e-30, None, ALU.max))
                link(nc.vector.reciprocal(v, v))
                link(tt(v, v, gate_of[:, t, heads[0]:heads[-1] + 1, 1 + br], ALU.mult))
                p_ = pr[:, n % 2, :].rearrange("p (u k) -> p u k", u=len(heads))
                tt(p_, p_, wide(v, 512 // len(heads)), ALU.mult).then_inc(at_w, 1)

            def nsa_lo(t):
                dve.wait_ge(on_hi, t + 1)
                tt(hT_lo[:, 0:4, rows_of(t)], AT[:, NSA_O[t], :].rearrange("p (c s) -> p c s", c=4),
                   hT_hi[:, 0:4, rows_of(t)].bitcast(F32), ALU.subtract).then_inc(on_lo, 1)

            def pooled_lo():
                for g in range(4):
                    dve.wait_ge(pl_hi, 2 * (g // 2) + 2)
                    stt(u4(ulo)[:, g, :], PJ[:, 2 + g // 2, (g % 2) * S:(g % 2 + 1) * S], pscale[:, g:g + 1],
                        u4(uhi)[:, g, :].bitcast(F32), ALU.mult, ALU.subtract).then_inc(pl_lo, 1)

            tiles(T_AIN, T_AOUT, {
                5: [block_keys], 7: [gelu_start], 8: [gelu_end], 9: [compressed_out],
                10: [lambda: maxima(6), cmp_max],
                11: [gates_out, lambda: weigh(6), lambda: maxima(7), cmp_probs],
                12: [lambda: maxima(8), lambda: probs_out(6), lambda: weigh(7)],
                13: [lambda: maxima(9), lambda: probs_out(7), lambda: weigh(8)],
                14: [lambda: maxima(10), lambda: probs_out(8), lambda: weigh(9)],
                15: [lambda: maxima(11), lambda: probs_out(9), lambda: weigh(10), lambda: maxima(12), lambda: probs_out(10),
                     lambda: weigh(11), pooled_lo, lambda: maxima(13), lambda: probs_out(11), lambda: weigh(12)],
            }, range(12, 15))
            tiles(T_AOUT, T_AOUT + 4, {
                0: [lambda: maxima(14), lambda: probs_out(12), lambda: weigh(13)],
                1: [lambda: maxima(15), lambda: probs_out(13), lambda: weigh(14)],
                2: [lambda: maxima(16), lambda: probs_out(14), lambda: weigh(15)],
                3: [lambda: nsa_lo(0), lambda: maxima(17), lambda: probs_out(15), lambda: weigh(16)],
            }, range(4))
            lo_to(T_AOUT + 7)
            probs_out(16)
            weigh(17)
            lo_to(T_MLP1)
            probs_out(17)
            lo_to(T_MLP1 + 1)
            nsa_lo(1)
            out_norm(0, B_AOUT, (T_AOUT + 6, T_AOUT + 8), 5)
            mlp(1, T_MLP1)
            dve.wait_ge(wsm_hi_done, 2)
            tt(wsm_lo[:, :, :], wsm[:, :, :], wsm_hi[:, :, :].bitcast(F32), ALU.subtract).then_inc(wsm_done, 1)
            lo_to(T_CIN + 1)
            for t in range(NT):
                ln_half(1, B_MLP1, t, 0, (T_CIN, T_CIN))
                ln_half(1, B_MLP1, t, 1, (T_CIN, T_CIN))
                lo_to(T_CIN + 3) if t else None
                ln_end(1, t)
                quarter_lo(6, 2 * t)
                quarter_lo(6, 2 * t + 1)
                lo_to(T_CIN + 2)

            la = lambda t: acc[:, LOGA + 512 * t:LOGA + 512 * (t + 1)]

            def rank_in():
                dve.wait_ge(a_mm, 1)
                nc.vector.tensor_copy(lf[:, 0:2, :], AT[:, 0, 0:32].rearrange("p (t a) -> p t a", t=NT)).then_inc(a_ev, 1)

            def gla_abs():
                for t in range(NT):
                    dve.wait_ge(z_mm, t + 1)
                    link(tt(la(t), AT[:, 2 + t, :], acc[:, GB:GB + 512], ALU.add))
                    stt(prT[:, t, :], la(t), -1.0, la(t), ALU.mult, ALU.max).then_inc(z_abs, 1)

            def gla_log():
                for t in range(NT):
                    dve.wait_ge(z_ln, t + 1)
                    stt(la(t), la(t), 0.0, prT[:, t, :], ALU.min, ALU.subtract).then_inc(loga_done, 1)

            def gla_qk():
                for t in range(NT):
                    q, k = proj[:, t, 0:512], proj[:, t, 512:1024]
                    a, b, c = GLA_E[t]
                    dve.wait_ge(eb_done, 3 * t + 3)
                    tt(q, q, a, ALU.mult)
                    link(tt(kT[:, D + 512 * t:D + 512 * (t + 1)], k, c, ALU.mult))
                    tt(k, k, b, ALU.mult).then_inc(kz_done, 1)

            def gla_causal():
                for t in range(NT):
                    dve.wait_ge(ga_mm, t + 1)
                    tt(prT[:, t, :].rearrange("p (h s) -> p h s", h=4),
                       AT[:, 2 + t, :].rearrange("p (h s) -> p h s", h=4),
                       cst[:, C_CAU:C_CAU + P].unsqueeze(1).broadcast_to([P, 4, P]), ALU.mult).then_inc(ga_done, 1)

            st = lambda n, h: acc[:, ST + D * n + 256 * h:ST + D * n + 256 * (h + 1)]

            def state(n):
                dve.wait_ge(eb_done, 7)
                for j in range(2):
                    dve.wait_ge(up_st, 2 * n + j + 1)
                    for h in (2 * j, 2 * j + 1):
                        ups = AT[:, j, 256 * (h % 2):256 * (h % 2 + 1)]
                        if n == 0:
                            ins = nc.vector.tensor_copy(st(0, h), ups)
                        else:
                            ins = stt(st(n, h), st(n - 1, h), dec[:, h, n:n + 1], ups, ALU.mult, ALU.add)
                    ins.then_inc(st_done, 1)
                    dve.wait_ge(st_done, 2 * n + j + 1)

            def gla_var(t):
                dve.wait_ge(sq_done, 14 + t + 1)
                variance(S_GO + 4 * t, 4, 256, LN_EPS)

            r_at = lambda j, t: proj[:, t, 2048 + 512 * j:2048 + 512 * (j + 1)]

            logit = lambda j, t: bank(B_CIN + 4 + j, t)
            out_at = lambda j, t: proj[:, t, half(j)]

            def r_gain(j):
                for t in range(NT):
                    dve.wait_ge(gt_abs, 4 + 2 * j + t + 1)
                    ins = tt(out_at(j, t).rearrange("p (h d) -> p h d", h=2),
                             logit(j, t).rearrange("p (h d) -> p h d", h=2),
                             acc[:, NG:NG + 256].unsqueeze(1).broadcast_to([P, 2, 256]), ALU.mult)
                link(ins)

            def r_min(j):
                for t in range(NT):
                    k = 4 + 2 * j + t
                    gate_min(k, logit(j, t), r_at(j, t))
                    dve.wait_ge(gt_min, k + 1)
                    dve.nop().then_inc(bank_free[j], 1)

            def gla_norm(j, t):
                rstd_wait() if j == 0 else None
                for h in (2 * j, 2 * j + 1):
                    c = slice(256 * (h % 2), 256 * (h % 2 + 1))
                    k = S_GO + 4 * t + h
                    o = out_at(j, t)[:, c]
                    ins = stt(o, AT[:, 2 * t + j, c], rstd[:, k:k + 1], o, ALU.mult, ALU.mult)
                return ins

            def gated(j, t):
                dve.wait_ge(gt_sig, 4 + 2 * j + t + 1)
                tt(out_at(j, t), out_at(j, t), r_at(j, t), ALU.mult).then_inc(src_ready, 1)

            def gated_first():
                for t in range(NT):
                    link(gla_norm(0, t))
                    gated(0, t)

            def norm_second():
                for t in range(NT):
                    ins = gla_norm(1, t)
                link(ins)

            tiles(T_CIN, T_COUT, {
                3: [rank_in], 5: [gla_abs, gla_log], 8: [gla_qk], 13: [gla_causal],
                16: [lambda: state(0)], 17: [lambda: state(1)], 18: [lambda: state(2)],
                19: [lambda: r_gain(0), lambda: r_min(0), lambda: gla_var(0)], 20: [lambda: gla_var(1), gated_first],
                22: [lambda: quarter_lo(7, 0), lambda: quarter_lo(7, 1)],
                23: [lambda: r_gain(1), norm_second, lambda: r_min(1), lambda: gated(1, 0), lambda: gated(1, 1)],
            })
            tiles(T_COUT, T_COUT + 4, {
                1: [lambda: quarter_lo(7, 2), lambda: quarter_lo(7, 3)],
            })
            out_norm(2, B_COUT, (T_COUT + 6, T_COUT + 8), 8)
            mlp(2, T_MLP2)
            for t in range(NT):
                for h in range(2):
                    ln_half(3, B_MLP2, t, h, (T_END, T_END))
                ln_end(3, t)

        @block.tensor
        def _(pe):
            mm = nc.tensor.matmul

            def transposes(n, q, src, waits=()):
                t, j = QUARTERS[n][q]
                pe.wait_ge(src_ready, units(n) + q + 1)
                for s, v in waits:
                    pe.wait_ge(s, v)
                for c in range(4):
                    ins = nc.tensor.transpose(tr_bank(n, t, j)[:, c * P:(c + 1) * P], src(t, 4 * j + c), ident)
                ins.then_inc(tr_done, 1)

            from_x = lambda t, c: x[:, t, c * P:(c + 1) * P]
            from_q = lambda t, c: qT[:, t * D + c * P:t * D + (c + 1) * P]
            from_proj = lambda t, c: proj[:, t, c * P:(c + 1) * P]

            def three(o, a, b, hi, lo, start, stop):
                mm(o, a, hi, start=start, stop=False)
                mm(o, a, lo, start=False, stop=False)
                return mm(o, b, hi, start=False, stop=stop)

            def tile_part(o, s, t, hi, lo, k0, n=512, start=False, stop=False):
                for kk in range(KPT):
                    w = slice(512 * kk, 512 * kk + n)
                    ins = three(o[:, 0:n], hi[:, k0 + kk, rows_of(t)], lo[:, k0 + kk, rows_of(t)], whi[:, s % SPL, w],
                                wlo[:, s % SPL, w], start and kk == 0, stop and kk == KPT - 1)
                return ins

            def bank_wait(pb, t):
                if pb >= 2:
                    pe.wait_ge(bank_free[pb % 2], 2 * (pb // 2) - 1 + t)

            def tile_of(pb, s0, i, n=512):
                s = s0 + i
                pe.wait_ge(raw_done, raw_of(s) + 1)
                for t in range(NT):
                    if i == 0:
                        bank_wait(pb, t)
                    ins = tile_part(bank(pb, t), s, t, hT_hi, hT_lo, KPT * i, n, i == 0, i == BLK - 1)
                ins.then_inc(w_used, 1)

            def first_block(pb, s0, stage, turn1):
                for t in range(NT):
                    if t == 1:
                        turn1()
                    bank_wait(pb, t)
                    for i in range(BLK):
                        if i % 2 == 0:
                            pe.wait_ge(hTlo_done, units(stage) + 2 * t + i // 2 + 1)
                        if t == 0:
                            pe.wait_ge(raw_done, raw_of(s0 + i) + 1)
                        ins = tile_part(bank(pb, t), s0 + i, t, hT_hi, hT_lo, KPT * i, 512, i == 0, i == BLK - 1)
                        if t == NT - 1:
                            ins.then_inc(w_used, 1)

            def out_first(pb, s0, q):
                h, i = q // 2, q % 2
                pe.wait_ge(raw_done, raw_of(s0 + q) + 1)
                for t in range(NT):
                    if i == 0:
                        bank_wait(pb + h, t)
                    ins = tile_part(bank(pb + h, t), s0 + q, t, u4(uhi), u4(ulo), KPT * i, start=i == 0)
                ins.then_inc(w_used, 1)

            def out_tile(pb, s0, k0, t, q):
                h, i = q // 2, q % 2
                s = s0 + 4 + q
                if t == 0:
                    pe.wait_ge(raw_done, raw_of(s) + 1)
                ins = tile_part(bank(pb + h, t), s, t, hT_hi, hT_lo, k0 + KPT * i, stop=i == 1)
                if t == NT - 1:
                    ins.then_inc(w_used, 1)
                elif i == 1:
                    ins.then_inc(prod_done, 1)

            def out_second(pb, s0, k0, done, ready, early, t0=0):
                for t in range(t0, NT):
                    pe.wait_ge(done, ready + t + 1)
                    for q in range(4):
                        if t == NT - 1 and q == 3:
                            early()
                        out_tile(pb, s0, k0, t, q)

            def small(n, o, done):
                for t in range(NT):
                    for k in range(KC):
                        ins = three(AT[:, 0, n * t:n * (t + 1)], hT_hi[:, k, rows_of(t)], hT_lo[:, k, rows_of(t)],
                                    wsm_hi[:, k, 0:n], wsm_lo[:, k, 0:n], k == 0, k == KC - 1)
                ins.then_inc(done, 1)

            def mod_bcast(n, bank0):
                pe.wait_ge(raw_done, ADA_AT[KC * n + KC - 1] + 1)
                i = ADA_ORDER[n]
                for j in range(2):
                    ins = mm(AT[:, bank0 + j, :], cst[:, C_TRI + P:C_TRI + 2 * P],
                             acc[:, i * D + 512 * j:i * D + 512 * (j + 1)], start=True, stop=True)
                    ins.then_inc(mod_mm, 1)

            def mlp(m, s0, pb, stage, src, early=None, spare=None):
                j0 = m * MLP_STEPS

                def up_first(t, half):
                    pe.wait_ge(hTlo_done, units(stage) + 2 * t + half + 1)
                    s = s0 + half
                    if t == 0:
                        pe.wait_ge(raw_done, raw_of(s) + 1)
                    for kk in range(4):
                        k = 4 * half + kk
                        w = slice(kk * FFB, (kk + 1) * FFB)
                        ins = three(AT[:, 2 * t, 0:FFB], hT_hi[:, k, rows_of(t)], hT_lo[:, k, rows_of(t)],
                                    whi[:, s % SPL, w], wlo[:, s % SPL, w], k == 0, k == KC - 1)
                    if t == NT - 1:
                        ins.then_inc(w_used, 1)
                    elif half == 1:
                        ins.then_inc(up_mm, 1)

                def turn_first():
                    pe.wait_ge(usq, j0 + 1)
                    for f in range(2):
                        for t in range(NT):
                            c = f * S + t * P
                            ins = nc.tensor.transpose(AT[:, 3, c:c + P],
                                                      pr[:, 1, t * FFB + f * P:t * FFB + (f + 1) * P], ident)
                    ins.then_inc(up_tr, 1)

                def up(j, k0, i=None, middle=None):
                    at = lambda v, d: v if i is None else i * d + v
                    if j0 + j >= 2:
                        pe.wait_ge(relu_done, at(j0 + j - 1, TURN))
                    for half in range(2):
                        s = s0 + k0 + half
                        pe.wait_ge(raw_done, at(raw_of(s) + 1, 4 * TURN))
                        if middle and half:
                            middle()
                        for kk in range(4):
                            k = 4 * half + kk
                            for f in range(2):
                                o = AT[:, j % 2, f * S:(f + 1) * S]
                                c = slice(kk * FFB + f * P, kk * FFB + (f + 1) * P)
                                first = k == 0 and f == 0
                                last = k == KC - 1
                                mm(o, whi[:, s % SPL, c], hT_hi[:, k, :], start=first, stop=False, skip_group_check=True)
                                mm(o, whi[:, s % SPL, c], hT_lo[:, k, :], start=False, stop=False, skip_group_check=True)
                                ins = mm(o, wlo[:, s % SPL, c], hT_hi[:, k, :], start=False, stop=last,
                                         skip_group_check=True)
                        ins.then_inc(w_used, 1)

                def down_part(j, s, f, t, h, first=False, last=False):
                    c = slice(f * S + t * P, f * S + (t + 1) * P)
                    w = slice(512 * h, 512 * (h + 1))
                    return three(bank(pb + h, t), uhi[:, j % 2, c], ulo[:, j % 2, c], whi[:, s % SPL, w],
                                 wlo[:, s % SPL, w], first, last)

                def down(j, k0, i=None, first=False):
                    at = lambda v, d: v if i is None else i * d + v
                    pe.wait_ge(ulo_done, at(j0 + j + 1, TURN))
                    for f in range(2):
                        s = s0 + k0 + f
                        pe.wait_ge(raw_done, at(raw_of(s) + 1, 4 * TURN))
                        for t in range(NT):
                            for h in range(2):
                                if first and f == 0:
                                    bank_wait(pb + h, t)
                                ins = down_part(j, s, f, t, h, first and f == 0)
                        ins.then_inc(w_used, 1)

                transposes(stage, 1, src)
                up_first(0, 0)
                transposes(stage, 2, src)
                up_first(0, 1)
                transposes(stage, 3, src)
                up_first(1, 0)
                up_first(1, 1)
                up(1, 2, middle=turn_first)
                down(0, 4, first=True)
                with pe.Fori(0, TURNS) as i:
                    for q in range(TURN):
                        up(2 + q, 6 + 4 * q, i)
                        down(1 + q, 8 + 4 * q, i)
                up(14, 54)
                down(13, 56)
                up(15, 58)
                if spare:
                    spare()
                for t in range(NT):
                    if t == 0:
                        parts = [(j, f, h) for j in (14, 15) for h in range(2) for f in range(2)]
                    else:
                        parts = [(j, f, h) for h in range(2) for j in (14, 15) for f in range(2)]
                    for j, f, h in parts:
                        s = s0 + (60 if j == 14 else 62) + f
                        last = j == MLP_STEPS - 1 and f == 1
                        if t == 0 and h == 0:
                            if f == 0:
                                pe.wait_ge(ulo_done, j0 + j + 1)
                            pe.wait_ge(raw_done, raw_of(s) + 1)
                        elif t == NT - 1 and h == 1 and j == 14 and f == 1 and early:
                            early()
                        ins = down_part(j, s, f, t, h, last=last)
                        if t == 0 and last:
                            ins.then_inc(prod_done, 1)
                        elif t == NT - 1 and h == 1:
                            ins.then_inc(w_used, 1)
                        elif t == NT - 1 and last:
                            ins.then_inc(half_done, 1)

            def softmax_scores(n):
                br, t, heads = GROUPS[n]
                fox = n < NF
                before = [g for g in range(0 if fox else NF, n) if S_BANK[g] == S_BANK[n]]
                if before:
                    pe.wait_ge(at_exp, before[-1] + 1)
                kw = P * (t + 1)
                for u, h in enumerate(heads):
                    rows = slice(0, 104) if fox else slice(0, 64)
                    q = qT[rows, h * S + t * P:h * S + (t + 1) * P]
                    k0 = h * S if fox else (1024, 1536)[br] + S * (h // 4)
                    o = AT[:, S_BANK[n], u * kw:(u + 1) * kw]
                    mm(o, q, kT[rows, k0:k0 + kw], start=True, stop=False)
                    ins = mm(o[:, kw - P:kw], identb[:, :], negb[:, :], start=False, stop=True)
                ins.then_inc(at_mm, 1)

            def prob_transposes(n):
                pe.wait_ge(at_exp, n + 1)
                if n >= NF:
                    pe.wait_ge(at_w, n - NF + 1)
                if n >= 1:
                    pe.wait_ge(at_trd, n)
                for c in range(4):
                    ins = nc.tensor.transpose(AT[:, 2, c * P:(c + 1) * P], pr[:, n % 2, c * P:(c + 1) * P], ident)
                ins.then_inc(at_tr, 1)


            def mixer(pb, s0, stage, turn1, cols, between):
                first_block(pb, s0, stage, turn1)
                for b, n in enumerate(cols):
                    for i in range(BLK):
                        if b:
                            tile_of(pb + b, s0 + BLK * b, i, n)
                        if b or i == BLK - 1:
                            for step in between.get(BLK * b + i, ()):
                                step()

            def quarters(n, src, qs, waits=()):
                def run():
                    for q in qs:
                        transposes(n, q, src, waits)
                return run

            mod_at = lambda i: AT[:, 2 * i, :]

            def mod_bias(j):
                pe.wait_ge(ld_bada, 16)
                for i in range(2):
                    c = ADA_ORDER[i] * D + 512 * j
                    mm(mod_at(i), cst[0:1, C_TRI + P:C_TRI + 2 * P], bada[:, c:c + 512], start=True, stop=False)

            def mod_tile(n, i):
                r = ADA_AT[n]
                pe.wait_ge(raw_full[r % RAW], 16 * (r // RAW + 1))
                c = 512 * ADA_ORDER[i]
                return mm(mod_at(i), cspread[:, n % KC, :], raw_slot(r)[:, c:c + 512], start=False, stop=False)

            def mod_sums(n, i):
                pe.wait_ge(raw_done, ADA_AT[n] + 1)
                c = ADA_ORDER[i] * D + 512 * (n // KC)
                mm(mod_at(i), cst[:, C_TRI + P:C_TRI + 2 * P], acc[:, c:c + 512], start=False, stop=True)\
                    .then_inc(mod_mm, 1)

            def first_half(t):
                pe.wait_ge(hTlo_done, units(0) + t + 1)
                for q in range(4):
                    b, i = FIRST[q]
                    if t == 0 and q == 1:
                        transposes(0, 1, from_q)
                    if t == 0:
                        pe.wait_ge(raw_done, raw_of(T_IN + q) + 1)
                    ins = tile_part(bank(B_IN + b, t), T_IN + q, t, hT_hi, hT_lo, KPT * i, start=i == 0)
                    if t == NT - 1:
                        ins.then_inc(w_used, 1)

            def second_half(b, t):
                pe.wait_ge(hTlo_done, units(0) + NT + t + 1)
                for q in (4 + 2 * b, 5 + 2 * b):
                    i = FIRST[q][1]
                    if t == 0 and q == 5:
                        transposes(0, 3, from_q)
                    if t == 0:
                        pe.wait_ge(raw_done, raw_of(T_IN + q) + 1)
                    ins = tile_part(bank(B_IN + b, t), T_IN + q, t, hT_hi, hT_lo, KPT * i, stop=i == BLK - 1)
                    if t == NT - 1:
                        ins.then_inc(w_used, 1)

            def mod_row_half(j):
                own = [n for n in ADA_PE if n // KC == j]
                for n in own:
                    for i in range(2):
                        ins = mod_tile(n, i)
                    ins.then_inc(ada_mm, 1)
                for i in range(2):
                    mod_sums(max(n for n in range(KC * j, KC * (j + 1)) if n not in own), i)

            pe.wait_ge(ld_cst, 16)
            pe.wait_ge(cb_done, 1)
            mod_bias(0)
            mod_row_half(0)
            transposes(0, 0, from_q)
            first_half(0)
            mod_bias(1)
            first_half(1)
            mod_row_half(1)
            transposes(0, 2, from_q)
            second_half(0, 0)
            second_half(0, 1)
            def forget_logits():
                pe.wait_ge(wsm_done, 1)
                small(8, AT, ff_mm)

            def cumulate():
                pe.wait_ge(ff_done, 1)
                for p0, c0 in ((64, 0), (96, S)):
                    mm(AT[p0:p0 + 8, 1, c0:c0 + S], lf[:, 4, 0:8], cst[:, C_TRI:C_TRI + S], start=True, stop=False)
                    ins = mm(AT[p0:p0 + 8, 1, c0 + P:c0 + S], lf[:, 4, 8:16], cst[:, C_TRI:C_TRI + P],
                             start=False, stop=True)
                ins.then_inc(cum_mm, 1)

            def head_transposes(f):
                t, j = (f // 2) % 2, f % 2
                pe.wait_ge(qk_norm, 2 * (f // 4) + t + 1)
                if f >= 2:
                    pe.wait_ge(hd_done, f - 1)
                c0 = FQ if f < 4 else FK
                for a in range(4):
                    h = 4 * j + a
                    ins = nc.tensor.transpose(AT[0:64, 2 + f % 2, a * P:(a + 1) * P],
                                              proj[:, t, c0 + 64 * h:c0 + 64 * (h + 1)], ident)
                ins.then_inc(hd_tr, 1)

            def fox_scores(n):
                if n == 0:
                    pe.wait_ge(hd_done, 8)
                    pe.wait_ge(cum_done, 2)
                    pe.wait_ge(ld_sel, 32)
                    pe.wait_ge(cast_done, 3)
                softmax_scores(n)

            def fox_values(n):
                if n == 0:
                    pe.wait_ge(bank_free[0], 4)
                if n == 2:
                    pe.wait_ge(at_out, 1)
                _, t, heads = GROUPS[n]
                pe.wait_ge(at_trd, n + 1)
                b = 0
                for h in heads:
                    for kt in range(t + 1):
                        ins = mm(AT[:, 3, 64 * h:64 * h + 64], prT[:, n % 2, b * P:(b + 1) * P],
                                 proj[:, kt, FV + 64 * h:FV + 64 * (h + 1)], start=kt == 0, stop=kt == t)
                        b += 1
                ins.then_inc(at_pv, 1)

            def turn(f):
                t = f % 2
                pe.wait_ge(at_exp, NF)
                if f >= 2:
                    pe.wait_ge(mod_row, 2)
                pe.wait_ge(rope_done, f + 1)
                c0 = RQ if f < 2 else RK
                for h in range(4):
                    ins = nc.tensor.transpose(AT[:, f % 2, h * P:(h + 1) * P], proj[:, t, c0 + h * P:c0 + (h + 1) * P],
                                              ident)
                ins.then_inc(rt_tr, 1)

            def fox_quarters():
                transposes(1, 0, from_proj, [(at_trd, NF)])
                transposes(1, 1, from_proj, [(at_out, 2)])

            def gate_row():
                pe.wait_ge(rt_done, 2)
                mod_bcast(2, 0)

            def ret_scores(h):
                pe.wait_ge(rt_done, 4)
                if h >= 2:
                    pe.wait_ge(rp_done, h - 1)
                q, k = rows[:, 0, h * S:(h + 1) * S], rows[:, 1, h * S:(h + 1) * S]
                mm(AT[:, h % 2, 0:S], k[:, 0:P], q, start=True, stop=True)
                mm(AT[:, h % 2, S:S + P], k[:, P:S], q[:, P:S], start=True, stop=True).then_inc(rs_mm, 1)

            def ret_values(h):
                pe.wait_ge(rp_done, h + 1)
                if h == 0:
                    pe.wait_ge(bank_free[0], 8)
                    pe.wait_ge(hTlo_done, units(1) + 2)
                v = lambda t: proj[:, t, RV + h * P:RV + (h + 1) * P]
                o = slice(h * P, (h + 1) * P)
                mm(AT[:, 2, o], pr[:, h % 2, 0:P], v(0), start=True, stop=True)
                mm(AT[:, 3, o], pr[:, h % 2, P:S], v(0), start=True, stop=False)
                mm(AT[:, 3, o], pr[:, h % 2, S:S + P], v(1), start=False, stop=True).then_inc(rv_mm, 1)

            def scale_row():
                pe.wait_ge(rp_done, 4)
                mod_bcast(3, 0)

            def shift_row():
                pe.wait_ge(mod_row, 4)
                mod_bcast(4, 0)

            S_, T_, V_ = fox_scores, prob_transposes, fox_values
            between = {
                8: [lambda f=f: head_transposes(f) for f in range(4)],
                10: [lambda f=f: head_transposes(f) for f in range(4, 8)],
                11: [lambda: S_(0)], 12: [lambda: T_(0), lambda: S_(1)],
                13: [lambda: V_(0), lambda: T_(1), lambda: S_(2)], 14: [lambda: V_(1), lambda: T_(2), lambda: S_(3)],
                15: [lambda: V_(2), lambda: T_(3), lambda: S_(4)], 16: [lambda: V_(3), lambda: T_(4), lambda: S_(5)],
                17: [lambda: V_(4), lambda: T_(5)], 18: [lambda: V_(5)],
                22: [lambda: turn(0), lambda: turn(1)], 23: [gate_row],
                26: [lambda: turn(2), lambda: turn(3), fox_quarters],
                27: [lambda: ret_scores(0), lambda: ret_scores(1)],
                28: [lambda: ret_values(0), lambda: ret_scores(2), lambda: ret_values(1), lambda: ret_scores(3)],
                29: [lambda: ret_values(2), lambda: ret_values(3)],
                30: [scale_row],
            }

            forget_logits()
            for t in range(NT):
                second_half(1, t)
            cumulate()
            for b in range(2, len(W_IN)):
                for i in range(BLK):
                    tile_of(B_IN + b, T_IN + BLK * b, i)
                    for step in between.get(BLK * b + i, ()):
                        step()
            for q in range(4):
                if q == 0:
                    pe.wait_ge(hTlo_done, units(1) + 2)
                out_first(B_OUT, T_OUT, q)
                if q == 3:
                    shift_row()
                if q == 2:
                    for k in (2, 3):
                        transposes(1, k, from_proj)
            out_second(B_OUT, T_OUT, 4, hTlo_done, units(1) + 2, quarters(2, from_q, (0,), [(mod_row, 6)]))

            def gate_f_row():
                mod_bcast(5, 2)

            mlp(0, T_MLP0, B_MLP0, 2, from_q, quarters(3, from_x, (0, 1)), gate_f_row)

            def nsa_transposes(f):
                if f < 3:
                    pe.wait_ge(bank_free[0], 2 * (B_AIN // 2) + 2)
                    srcs = [proj[:, t, 512 + P * f + 64 * g:512 + P * f + 64 * (g + 1)] for g in range(2) for t in range(NT)]
                elif f < 7:
                    t, j = (f - 3) // 2, (f - 3) % 2
                    pe.wait_ge(bank_free[1], 2 * ((B_AIN + 1) // 2) + 2)
                    if f == 3:
                        pe.wait_ge(c_mm, 1)
                    srcs = [proj[:, t, 64 * (4 * j + a):64 * (4 * j + a + 1)] for a in range(4)]
                else:
                    pe.wait_ge(bank_free[0], 2 * ((B_AIN + 2) // 2) + 2)
                    pe.wait_ge(at_trd, NF + 1)
                    srcs = [proj[:, t, 1024 + 64 * g:1024 + 64 * (g + 1)] for g in range(2) for t in range(NT)]
                if 2 <= f < 7:
                    pe.wait_ge(nt_done, f - 1)
                for c, a in enumerate(srcs):
                    ins = nc.tensor.transpose(AT[0:64, 2 if f == 7 else 2 + f % 2, c * P:(c + 1) * P], a, ident)
                ins.then_inc(nt_tr, 1)

            def compress():
                for i in range(2):
                    pe.wait_ge(kb_done, i + 1)
                    kb = (acc if i == 0 else qT)[0:64, (KB if i == 0 else 0):(KB if i == 0 else 0) + 960]
                    for j in range(32):
                        ins = mm(AT[0:64, 0, 32 * i:32 * i + 30], acc[0:64, 2048 * i + 64 * j:2048 * i + 64 * (j + 1)],
                                 kb[:, 30 * j:30 * (j + 1)], start=j == 0, stop=j == 31)
                ins.then_inc(c_mm, 1)

            def compress2():
                pe.wait_ge(c_gel, 2)
                mm(AT[0:64, 0, 64:94], nsm[:, 66:130], gel[:, 5, 0:30], start=True, stop=True)
                mm(AT[0:HC, 0, 96:160], proj[0:64, 1, GVR:GVR + HC], nsm[:, 130:194], start=True, stop=True)\
                    .then_inc(c2_mm, 1)

            def cmp_scores():
                pe.wait_ge(c2_done, 2)
                pe.wait_ge(nt_done, 7)
                for t in range(NT):
                    for h in range(8):
                        ins = mm(AT[:, 0, 256 + HC * t + NCMP * h:256 + HC * t + NCMP * (h + 1)],
                                 qT[0:64, h * S + t * P:h * S + (t + 1) * P],
                                 gel[:, 0, NCMP * (h // 4):NCMP * (h // 4 + 1)], start=True, stop=True)
                ins.then_inc(cs_mm, 1)

            def cmp_transposes():
                pe.wait_ge(cs_p, 1)
                for t in range(NT):
                    ins = nc.tensor.transpose(AT[0:HC, 0, t * P:(t + 1) * P], proj[:, 0, CSB + HC * t:CSB + HC * (t + 1)],
                                              ident)
                ins.then_inc(ct_tr, 1)

            def started(t, parts, seen=set()):
                new = not parts & {p for u, p in seen if u == t}
                seen.update((t, p) for p in parts)
                return new

            def cmp_values():
                pe.wait_ge(ct_done, 1)
                for t in range(NT):
                    for c in range(4):
                        ins = mm(AT[:, NSA_O[t], c * P:(c + 1) * P], proj[0:HC, 0, VCB + c * P:VCB + (c + 1) * P],
                                 proj[0:HC, 0, PCT + t * P:PCT + (t + 1) * P], start=started(t, {0, 1}), stop=False,
                                 skip_group_check=True)
                ins.then_inc(cv_mm, 1)

            def nsa_scores(n):
                if n == NF:
                    pe.wait_ge(nt_done, 7)
                softmax_scores(n)

            def nsa_probs(n):
                if n == NF + 1:
                    pe.wait_ge(nt_done, 8)
                prob_transposes(n)

            def nsa_values(n):
                br, t, heads = GROUPS[n]
                pe.wait_ge(at_trd, n + 1)
                if t == 1:
                    pe.wait_ge(ct_done, 1)
                c0 = heads[0] // 2 * P
                v0 = (896, 1152)[br] + 64 * (heads[0] // 4)
                by_parity = prT[:, n % 2, :].rearrange("p (a b s) -> p b a s", b=2, s=P)
                for e in range(2):
                    o = AT[64 * e:64 * e + 64, NSA_O[t], :]
                    if t == 0:
                        ins = mm(o[:, c0:c0 + 2 * P].rearrange("d (a s) -> d a s", a=2), proj[:, 0, v0:v0 + 64],
                                 by_parity[:, e], start=started(t, {e}), stop=br == 1, skip_group_check=True)
                    else:
                        for kt in range(NT):
                            ins = mm(o[:, c0:c0 + P], proj[:, kt, v0:v0 + 64],
                                     prT[:, n % 2, (2 * e + kt) * P:(2 * e + kt + 1) * P], start=started(t, {e}),
                                     stop=br == 1 and kt == 1, skip_group_check=True)
                ins.then_inc(at_pv, 1)

            def pool_bands():
                pe.wait_ge(bank_free[0], 2 * ((B_AIN + 2) // 2) + 2)
                pe.wait_ge(bank_free[1], 2 * ((B_AIN + 3) // 2) + 2)
                pe.wait_ge(ld_tab, 16)
                for g in range(4):
                    o = PJ[:, g // 2, (g % 2) * S:(g % 2 + 1) * S]
                    u = lambda t: proj[:, t, N_U + P * g:N_U + P * (g + 1)]
                    mm(o, u(0), tab[:, 384 * g:384 * g + S], start=True, stop=False)
                    ins = mm(o[:, P:S], u(1), tab[:, 384 * g + S:384 * (g + 1)], start=False, stop=True)
                    if g % 2:
                        ins.then_inc(pm_mm, 1)

            def pool_mix():
                pe.wait_ge(pm_done, 2)
                for g in range(4):
                    ins = mm(PJ[:, 2 + g // 2, (g % 2) * S:(g % 2 + 1) * S], acc[:, POOLW + P * g:POOLW + P * (g + 1)],
                             proj[:, 1, RT_ + S * g:RT_ + S * (g + 1)], start=True, stop=True)
                    if g % 2:
                        ins.then_inc(py_mm, 1)

            S_, T_, V_ = nsa_scores, nsa_probs, nsa_values
            between = {
                4: [lambda: nsa_transposes(0), lambda: nsa_transposes(1)], 5: [lambda: nsa_transposes(2)],
                7: [compress], 8: [lambda: nsa_transposes(3), lambda: nsa_transposes(4)],
                9: [lambda: nsa_transposes(5), lambda: nsa_transposes(6), compress2],
                10: [lambda: S_(6), cmp_scores],
                11: [lambda: S_(7)],
                12: [lambda: T_(6), lambda: S_(8)],
                13: [lambda: V_(6), lambda: nsa_transposes(7), lambda: T_(7), cmp_transposes, lambda: S_(9)],
                14: [cmp_values, lambda: V_(7), lambda: T_(8), lambda: S_(10)],
                15: [lambda: V_(8), lambda: T_(9), lambda: S_(11), pool_bands, lambda: V_(9), lambda: T_(10), lambda: S_(12),
                     pool_mix, lambda: V_(10), lambda: T_(11), lambda: S_(13)],
            }
            mixer(B_AIN, T_AIN, 3, quarters(3, from_x, (2, 3), [(mod_row, 8)]), [n for _, n in A_IN], between)
            between = {0: [lambda: V_(11), lambda: T_(12), lambda: S_(14)],
                       1: [lambda: V_(12), lambda: T_(13), lambda: S_(15)],
                       2: [lambda: V_(13), lambda: T_(14), lambda: S_(16)],
                       3: [lambda: V_(14), lambda: T_(15), lambda: S_(17)]}
            for q in range(4):
                if q == 0:
                    pe.wait_ge(pl_lo, 4)
                out_first(B_AOUT, T_AOUT, q)
                for step in between[q]:
                    step()
            pe.wait_ge(on_lo, 1)
            out_tile(B_AOUT, T_AOUT, 0, 0, 0)
            V_(15)
            T_(16)
            out_tile(B_AOUT, T_AOUT, 0, 0, 1)
            out_tile(B_AOUT, T_AOUT, 0, 0, 2)
            V_(16)
            T_(17)
            out_tile(B_AOUT, T_AOUT, 0, 0, 3)
            V_(17)
            out_second(B_AOUT, T_AOUT, 0, on_lo, 0, quarters(5, from_x, (0,), [(on_lo, 2)]), 1)
            mlp(1, T_MLP1, B_MLP1, 5, from_x, quarters(6, from_x, (0, 1)))


            def gate_inputs():
                pe.wait_ge(wsm_done, 2)
                small(16, AT, a_mm)

            def gate_rank():
                pe.wait_ge(a_ev, 1)
                for t in range(NT):
                    ins = nc.tensor.transpose(AT[0:16, 1, t * P:(t + 1) * P], lf[:, t, :], ident)
                ins.then_inc(aT_tr, 1)

            def gate_logits():
                pe.wait_ge(aT_done, 1)
                pe.wait_ge(ld_gla, 80)
                for t in range(NT):
                    mm(AT[:, 2 + t, :], aT[:, rows_of(t)], acc[0:16, GW2:GW2 + 512], start=True, stop=True)\
                        .then_inc(z_mm, 1)

            def cumulated():
                for t in range(NT):
                    pe.wait_ge(loga_done, 2)
                    la = acc[:, LOGA + 512 * t:LOGA + 512 * (t + 1)]
                    mm(AT[:, 2 * t, :], cst[:, C_TRC:C_TRC + P], la, start=True, stop=True)
                    mm(AT[:, 2 * t + 1, :], cst[:, C_SUF:C_SUF + P], la, start=True, stop=True).then_inc(b_mm, 1)

            def chunk_decay():
                pe.wait_ge(eb_done, 2)
                for t in range(NT):
                    for h in range(4):
                        ins = mm(AT[:, 0, 4 * h + 2 * t:4 * h + 2 * t + 2],
                                 acc[:, LOGA + 512 * t + P * h:LOGA + 512 * t + P * (h + 1)],
                                 cst[:, C_IND:C_IND + 2], start=True, stop=True)
                ins.then_inc(b_mm, 1)

            def gla_transposes(f):
                t = f // 2
                pe.wait_ge(kz_done, t + 1)
                if f == 0:
                    pe.wait_ge(eb_done, 7)
                if f == 3:
                    pe.wait_ge(g_trd, 1)
                for h in range(4):
                    c0 = 512 * (f % 2) + P * h
                    ins = nc.tensor.transpose(AT[:, (1, 2, 3, 1)[f], h * P:(h + 1) * P], proj[:, t, c0:c0 + P], ident)
                ins.then_inc(g_tr, 1)

            def gla_scores(t):
                pe.wait_ge(g_trd, 4)
                for h in range(4):
                    c = slice(h * S + t * P, h * S + (t + 1) * P)
                    ins = mm(AT[:, (2, 3)[t], h * P:(h + 1) * P], kT[:, c], qT[:, c], start=True, stop=True)
                ins.then_inc(ga_mm, 1)

            def gla_update(n):
                if n == 0:
                    pe.wait_ge(bank_free[0], 2 * ((B_CIN + 2) // 2) + 2)
                    pe.wait_ge(bank_free[1], 2 * ((B_CIN + 3) // 2) + 2)
                t, p0 = n // 2, 64 * (n % 2)
                for j in range(2):
                    if n:
                        pe.wait_ge(st_done, 2 * (n - 1) + j + 1)
                    for h in (2 * j, 2 * j + 1):
                        ins = mm(AT[:, j, 256 * (h % 2):256 * (h % 2 + 1)],
                                 kT[p0:p0 + 64, D + 512 * t + P * h:D + 512 * t + P * (h + 1)],
                                 proj[p0:p0 + 64, t, 1024 + 256 * h:1024 + 256 * (h + 1)], start=True, stop=True)
                    ins.then_inc(up_st, 1)

            def gla_out(t):
                pe.wait_ge(st_done, 6)
                pe.wait_ge(ga_done, 2)
                for h in range(4):
                    o = AT[:, 2 * t + h // 2, 256 * (h % 2):256 * (h % 2 + 1)]
                    ins = mm(o, prT[:, t, h * P:(h + 1) * P], proj[:, t, 1024 + 256 * h:1024 + 256 * (h + 1)],
                             start=True, stop=False, skip_group_check=True)
                    for half in range(2):
                        n = 2 * t + half
                        if n:
                            c0 = h * S + 64 * n
                            ins = mm(o[64 * half:64 * half + 64, :], qT[:, c0:c0 + 64],
                                     acc[:, ST + D * (n - 1) + 256 * h:ST + D * (n - 1) + 256 * (h + 1)],
                                     start=False, stop=True, skip_group_check=True)
                ins.then_inc(go_mm, 1)

            between = {
                3: [gate_inputs], 4: [gate_rank], 5: [gate_logits], 8: [cumulated], 9: [chunk_decay],
                11: [lambda f=f: gla_transposes(f) for f in range(3)], 12: [lambda: gla_transposes(3), lambda: gla_scores(0)],
                13: [lambda: gla_scores(1)],
                16: [lambda: gla_update(0)], 17: [lambda: gla_update(1)], 18: [lambda: gla_update(2)],
                19: [lambda: gla_out(0)], 20: [lambda: gla_out(1)],
                22: [lambda: transposes(7, 0, from_proj), lambda: transposes(7, 1, from_proj)],
            }
            mixer(B_CIN, T_CIN, 6, quarters(6, from_x, (2, 3)), [512] * len(C_IN), between)
            for q in range(4):
                if q == 0:
                    pe.wait_ge(hTlo_done, units(7) + 2)
                out_first(B_COUT, T_COUT, q)
                if q == 2:
                    for k in (2, 3):
                        transposes(7, k, from_proj)
            out_second(B_COUT, T_COUT, 4, hTlo_done, units(7) + 2, quarters(8, from_x, (0,), [(hTlo_done, units(8))]))
            mlp(2, T_MLP2, B_MLP2, 8, from_x)


_INS = ['x', 'c', 'w_ada', 'b_ada', 'w_in', 'b_forget', 'q_norm_gain', 'k_norm_gain', 'fox_out_gain', 'ret_out_gain',
        'w_out', 'w_mlp_in', 'w_mlp_out', 'a_w_in_2', 'a_cmp_pos_2', 'a_cmp_w1_2', 'a_cmp_b1_2', 'a_cmp_w2_2',
        'a_pool_w_2', 'a_pool_scale_2', 'a_w_out_2', 'c_w_in_2', 'c_gate_w2_2', 'c_gate_b_2', 'c_norm_g_2',
        'c_w_out_2', 'ln1_g_2', 'ln1_b_2', 'ln2_g_2', 'ln2_b_2', 'mlp_w1_2', 'mlp_w2_2']


def kernel(**inputs):
    import numpy as _np
    import concourse.bacc as _bacc
    from concourse import mybir as _mybir
    from concourse.bass_utils import run_bass_kernel_spmd as _run

    nc = _bacc.Bacc("TRN2", target_bir_lowering=False, num_devices=1)
    arrays, dram = {}, {}
    for name, a in list(((n, inputs[n]) for n in _INS)) + list(constants().items()):
        a = _np.ascontiguousarray(a)
        arrays[f"in_{name}_dram"] = a
        dram[name] = nc.dram_tensor(f"in_{name}_dram", a.shape, _mybir.dt.from_np(a.dtype), kind="ExternalInput").ap()
    out = nc.dram_tensor("out_0_dram", (1, S, D), F32, kind="ExternalOutput").ap()
    block_program(nc, dram, out)
    r = _run(nc, [arrays], core_ids=[0])
    return r.results[0]["out_0_dram"]
```
